# Optimizing a Trainium2 kernel written in Bass

```python
import math
import jax, jax.numpy as jnp
from jax import lax
import numpy as np

D_MODEL = 2048
BATCH = 1
SEQ = 256
DEPTH = 2

GRID_W = 64
CTX_LEN = 256
N_MIXERS = 2
N_ATTN_LAYERS = (DEPTH + N_MIXERS - 1) // N_MIXERS
N_FOURIER_LAYERS = DEPTH // N_MIXERS
HEAD_DIM = 64
VALUE_DIM = 2 * HEAD_DIM
N_HEADS = D_MODEL // VALUE_DIM
Q_WIDTH = N_HEADS * 2 * HEAD_DIM
ATTN_WIDTH = N_HEADS * VALUE_DIM
ATTN_SCALE = HEAD_DIM ** -0.5
Q_BLOCK = 128
ROPE_THETA = 10000.0
ROPE_FREQS = HEAD_DIM // 4
FOURIER_GROUPS = 8
FOURIER_WIDTH = D_MODEL
FOURIER_GROUP_DIM = FOURIER_WIDTH // FOURIER_GROUPS
FFN_HIDDEN = ((8 * D_MODEL // 3 + 255) // 256) * 256
RMS_EPS = 1e-6

kernel_name = 'hybrid_diffattn_fnet_dit_trunk'

def rms_norm(x, g):
    xf = x.astype(jnp.float32)
    y = xf * lax.rsqrt(jnp.mean(xf * xf, axis=-1, keepdims=True) + RMS_EPS)
    return (y * g.astype(jnp.float32)).astype(x.dtype)

def ada_params(cond, w_mod, b_mod):
    m = jax.nn.silu(cond) @ w_mod + b_mod
    return jnp.split(m[..., None, :], 6, axis=-1)

def modulate(h, shift, scale):
    return h * (1.0 + scale) + shift

def axial_rope_tables(n_tokens):
    rows_count = n_tokens // GRID_W
    row = jnp.repeat(jnp.arange(rows_count), GRID_W)
    col = jnp.tile(jnp.arange(GRID_W), rows_count)
    inv_freq = ROPE_THETA ** (-jnp.arange(ROPE_FREQS, dtype=jnp.float32) / ROPE_FREQS)
    ang = jnp.stack([row[:, None] * inv_freq, col[:, None] * inv_freq], axis=1)
    return jnp.cos(ang), jnp.sin(ang)

def apply_axial_rope(x, cos, sin):
    xs = x.reshape(x.shape[:-1] + (2, 2, ROPE_FREQS))
    xa, xb = xs[..., 0, :], xs[..., 1, :]
    c = cos[None, :, None, None].astype(x.dtype)
    s = sin[None, :, None, None].astype(x.dtype)
    out = jnp.stack([xa * c - xb * s, xb * c + xa * s], axis=-2)
    return out.reshape(x.shape)

def diff_attention(h_lat, h_ctx, w_qkv, w_o, lam, subln_g, lambda_init, cos, sin, with_ctx_queries):
    B, N, _ = h_lat.shape
    Lc = h_ctx.shape[1]
    lf = lam.astype(jnp.float32)
    lam_full = jnp.exp(jnp.sum(lf[0] * lf[1])) - jnp.exp(jnp.sum(lf[2] * lf[3])) + lambda_init

    q_l, k_l, v_l = jnp.split(h_lat @ w_qkv, [Q_WIDTH, 2 * Q_WIDTH], axis=-1)
    q_l = apply_axial_rope(q_l.reshape(B, N, N_HEADS, 2, HEAD_DIM), cos, sin)
    k_l = apply_axial_rope(k_l.reshape(B, N, N_HEADS, 2, HEAD_DIM), cos, sin)
    v_l = v_l.reshape(B, N, N_HEADS, VALUE_DIM)
    k_c, v_c = jnp.split(h_ctx @ w_qkv[:, Q_WIDTH:], 2, axis=-1)
    k_c = k_c.reshape(B, Lc, N_HEADS, 2, HEAD_DIM)
    v_c = v_c.reshape(B, Lc, N_HEADS, VALUE_DIM)
    k_all = jnp.concatenate([k_l, k_c], axis=1)
    v_all = jnp.concatenate([v_l, v_c], axis=1)

    def attend(q, k, v):
        s = jnp.einsum('bqhcd,bkhcd->bhcqk', q, k).astype(jnp.float32) * ATTN_SCALE
        p = jax.nn.softmax(s, axis=-1)
        a = (p[:, :, 0] - lam_full * p[:, :, 1]).astype(v.dtype)
        o = jnp.einsum('bhqk,bkhe->bqhe', a, v)
        o = rms_norm(o, subln_g) * (1.0 - lambda_init)
        return o.reshape(o.shape[0], o.shape[1], ATTN_WIDTH)

    n_blocks = N // Q_BLOCK
    q_blocks = q_l.reshape(B, n_blocks, Q_BLOCK, N_HEADS, 2, HEAD_DIM).swapaxes(0, 1)
    o_l = lax.map(lambda qb: attend(qb, k_all, v_all), q_blocks)
    y_l = o_l.swapaxes(0, 1).reshape(B, N, ATTN_WIDTH) @ w_o
    y_c = None
    if with_ctx_queries:
        q_c = (h_ctx @ w_qkv[:, :Q_WIDTH]).reshape(B, Lc, N_HEADS, 2, HEAD_DIM)
        y_c = attend(q_c, k_c, v_c) @ w_o
    return y_l, y_c

def fourier_mix(h, w_in, w_out):
    B, N, _ = h.shape
    u = (h @ w_in).reshape(B, N, FOURIER_GROUPS, FOURIER_GROUP_DIM).astype(jnp.float32)
    f = jnp.fft.fft2(u, axes=(1, 3), norm='ortho').real
    return f.astype(h.dtype).reshape(B, N, FOURIER_WIDTH) @ w_out

def swiglu(h, w_gu, w_down):
    g, u = jnp.split(h @ w_gu, 2, axis=-1)
    return (jax.nn.silu(g) * u) @ w_down

def setup_inputs(seed: int = 0) -> dict:
    key = jax.random.key(seed)
    ks = jax.random.split(key, 16)
    nrm = jax.random.normal
    D = D_MODEL
    return {
        'x': nrm(ks[0], (BATCH, SEQ, D), jnp.float32),
        'c': nrm(ks[1], (BATCH, D), jnp.float32),
        'ctx': nrm(ks[2], (BATCH, CTX_LEN, D), jnp.float32),
        'c_ctx': nrm(ks[3], (D,), jnp.float32),
        'mod_w': nrm(ks[4], (DEPTH, D, 6 * D), jnp.float32) * (0.5 * D ** -0.5),
        'mod_b': 0.01 * nrm(ks[5], (DEPTH, 6 * D), jnp.float32),
        'norm_g': 1.0 + 0.05 * nrm(ks[6], (DEPTH, 4, D), jnp.float32),
        'ffn_w_gu': nrm(ks[7], (DEPTH, D, 2 * FFN_HIDDEN), jnp.float32) * D ** -0.5,
        'ffn_w_down': nrm(ks[8], (DEPTH, FFN_HIDDEN, D), jnp.float32) * FFN_HIDDEN ** -0.5,
        'attn_w_qkv': nrm(ks[9], (N_ATTN_LAYERS, D, 2 * Q_WIDTH + ATTN_WIDTH), jnp.float32) * D ** -0.5,
        'attn_w_o': nrm(ks[10], (N_ATTN_LAYERS, ATTN_WIDTH, D), jnp.float32) * ATTN_WIDTH ** -0.5,
        'attn_lambda': 0.1 * nrm(ks[11], (N_ATTN_LAYERS, 4, HEAD_DIM), jnp.float32),
        'attn_subln_g': 1.0 + 0.05 * nrm(ks[12], (N_ATTN_LAYERS, VALUE_DIM), jnp.float32),
        'four_w_in': nrm(ks[13], (N_FOURIER_LAYERS, D, FOURIER_WIDTH), jnp.float32) * D ** -0.5,
        'four_w_out': nrm(ks[14], (N_FOURIER_LAYERS, FOURIER_WIDTH, D), jnp.float32) * FOURIER_WIDTH ** -0.5,
    }

def reference(x, c, ctx, c_ctx, mod_w, mod_b, norm_g, ffn_w_gu, ffn_w_down, attn_w_qkv, attn_w_o,
              attn_lambda, attn_subln_g, four_w_in, four_w_out):
    n_tokens = x.shape[1]
    cos, sin = axial_rope_tables(n_tokens)
    x_c = ctx
    last_ctx_reader = max(i for i in range(DEPTH) if i % N_MIXERS == 0)
    for i in range(DEPTH):
        j = i // N_MIXERS
        is_attn = (i % N_MIXERS) == 0
        ctx_update = i < last_ctx_reader
        need_h_c = ctx_update or (is_attn and i <= last_ctx_reader)
        g = norm_g[i]
        sh1, sc1, gt1, sh2, sc2, gt2 = ada_params(c, mod_w[i], mod_b[i])
        h_l = modulate(rms_norm(x, g[0]), sh1, sc1)
        if need_h_c:
            csh1, csc1, cgt1, csh2, csc2, cgt2 = ada_params(c_ctx, mod_w[i], mod_b[i])
            h_c = modulate(rms_norm(x_c, g[0]), csh1, csc1)
        if is_attn:
            lambda_init = 0.8 - 0.6 * math.exp(-0.3 * i)
            y_l, y_c = diff_attention(h_l, h_c, attn_w_qkv[j], attn_w_o[j], attn_lambda[j], attn_subln_g[j],
                                      lambda_init, cos, sin, ctx_update)
        else:
            y_l = fourier_mix(h_l, four_w_in[j], four_w_out[j])
            y_c = fourier_mix(h_c, four_w_in[j], four_w_out[j]) if ctx_update else None
        x = x + gt1 * rms_norm(y_l, g[1])
        x = x + gt2 * rms_norm(swiglu(modulate(rms_norm(x, g[2]), sh2, sc2), ffn_w_gu[i], ffn_w_down[i]), g[3])
        if ctx_update:
            x_c = x_c + cgt1 * rms_norm(y_c, g[1])
            x_c = x_c + cgt2 * rms_norm(swiglu(modulate(rms_norm(x_c, g[2]), csh2, csc2), ffn_w_gu[i], ffn_w_down[i]), g[3])
    return x


_drawn_inputs = setup_inputs


def setup_inputs(seed=0):
    import zlib

    import numpy as np

    out = dict(_drawn_inputs(seed))
    spreads = {}
    factors = {}
    for name, (base, spread) in spreads.items():
        noise = np.random.default_rng([zlib.crc32(name.encode()), seed]).standard_normal(out[name].shape)
        drawn = base * np.exp(spread * noise) if base else spread * noise
        out[name] = __import__('jax').numpy.asarray(drawn.astype(out[name].dtype))
    for name, factor in factors.items():
        out[name] = (out[name] * factor).astype(out[name].dtype)
    return out
```

```python
from contextlib import ExitStack

import numpy as np

import concourse.bass as bass
from concourse import mybir

ALU = mybir.AluOpType
ACT = mybir.ActivationFunctionType
AX_X = mybir.AxisListType.X
F32 = mybir.dt.float32
F32R = mybir.dt.float32r
BF16 = mybir.dt.bfloat16

P = 128
D = 2048
SEQ = 256
CTX = 256
KT = D // P
TT = SEQ // P
HEADS = 16
HEAD_DIM = 64
GROUPS = 4
HPG = HEADS // GROUPS
FFN = 5632
FGROUPS = 8
PART = 4 * P
PARTS = FFN // PART
EPS = 1e-6
SCALE = HEAD_DIM ** -0.5
LAMBDA_INIT = 0.8 - 0.6
GRID_W = 64
THETA = 10000.0

RING = 4
START_CHUNKS = 2 * KT
PRE = RING

C_IDENT, C_COS, C_SIN = 0, P, P + SEQ
C_END = P + 2 * SEQ
DFT_COLS = 2048

ROW_BANKS = ((2, 3), (4, 5))
COL_BANK, SUM_BANK = 6, 7


class Stage:

    def __init__(self, before, n_w, hosts=None, turns=1):
        self.raw0, self.w0, self.m0 = before
        self.n_w, self.turns = n_w, turns
        self.hosts = hosts or [0] * n_w
        assert self.hosts[:2] == [0, 0]
        self.n_m = sum(self.hosts)
        self.n_raw = n_w + self.n_m
        assert self.n_raw % RING == 0 and n_w % 2 == 0
        self.after = (self.raw0 + turns * self.n_raw, self.w0 + turns * n_w, self.m0 + turns * self.n_m)

    def raw(self, j):
        if j >= self.n_w:
            return self.raw0 + self.n_raw + j - self.n_w
        return self.raw0 + j + sum(self.hosts[:j])

    def order(self):
        kt = 0
        for j in range(self.n_w):
            yield "w", j
            for _ in range(self.hosts[j]):
                yield "m", kt
                kt += 1


def spread(n_w, n_m):
    k = n_w - 2
    return [0, 0] + [(j + 1) * n_m // k - j * n_m // k for j in range(k)]


QKV = Stage((0, 0, 0), 3 * HPG, [0] * 4 + [2] * 8, GROUPS)
WO = Stage(QKV.after, 16, spread(16, KT))
UP0 = Stage(WO.after, 8)
LOOP0 = Stage(UP0.after, 24, spread(24, KT), 5)
DOWN0 = Stage(LOOP0.after, 4)
FIN = Stage(DOWN0.after, 4, turns=4)
FOUT = Stage(FIN.after, 16)
UP1 = Stage(FOUT.after, 8)
LOOP1 = Stage(UP1.after, 24, turns=5)
DOWN1 = Stage(LOOP1.after, 4)
LAST = DOWN1.after
FFN_STAGES = ((UP0, LOOP0, DOWN0), (UP1, LOOP1, DOWN1))

PREP_LAT, PREP_CTX, PREP_O, PREP_F0, PREP_FOUR, PREP_F1 = range(6)


def at(base, per_turn, i):
    return base if i is None else base + per_turn * i


class Link:

    def __init__(self, eng, sem):
        self.eng, self.sem, self.n, self.more = eng, sem, 0, 0

    def __call__(self, ins):
        ins.then_inc(self.sem, 1)
        self.n += 1
        self.eng.wait_ge(self.sem, self.n + self.more)

    def turn(self, i, per_turn):
        self.start, self.per_turn, self.more = self.n, per_turn, per_turn * i

    def end(self, turns):
        assert self.n - self.start == self.per_turn, (self.n - self.start, self.per_turn)
        self.n, self.more = self.start + turns * self.per_turn, 0


def trunk(nc, x, c, ctx, c_ctx, mod_w, mod_b, norm_g, w_gu, w_down, w_qkv, w_o, lam, subln_g,
          w_in, w_out, consts, dft, out):
    x_d = x.rearrange("b (t p) d -> p (b t) d", p=P)
    ctx_d = ctx.rearrange("b (t p) d -> p (b t) d", p=P)
    out_d = out.rearrange("b (t p) d -> p (b t) d", p=P)
    mod_d = mod_w.rearrange("l d n -> (l d) n")
    gu_d = w_gu.rearrange("l d n -> (l d) n")
    down_d = w_down.rearrange("l d n -> (l d) n")
    qkv_d = w_qkv.rearrange("l d n -> (l d) n")
    wo_d = w_o.rearrange("l d n -> (l d) n")
    in_d = w_in.rearrange("l d n -> (l d) n")
    out_w_d = w_out.rearrange("l d n -> (l d) n")
    gate_scratch = nc.dram_tensor("gate_scratch", (4, D), F32, kind="Internal").ap()

    es = ExitStack()
    with es:
        def sb(name, shape, dt=F32):
            return es.enter_context(nc.sbuf_tensor(name, shape, dt))

        def sem(name):
            return es.enter_context(nc.semaphore(name))

        raw = sb("raw", [P, RING, 2048])
        w_hi = sb("w_hi", [P, 2, 2048], F32R)
        w_lo = sb("w_lo", [P, 2, 2048], F32R)
        LAT_HI, CTX_HI, LAT_LO, CTX_LO = range(4)
        hT = sb("hT", [P, KT, 4, SEQ], F32R)
        act_hi = hT[:, 0:8, CTX_HI, :]
        act_lo = hT[:, 0:8, CTX_LO, :]
        y = sb("y", [P, TT, D])
        acc = sb("acc", [P, 2048])
        htmp = acc[:, :].rearrange("p (b k t) -> p b k t", b=4, k=2)
        region = sb("region", [P, 8192])
        qT = region[:, 0:1024].rearrange("p (h t) -> p h t", h=HPG)
        kT = region[:, 1024:3072].rearrange("p (h t) -> p h t", h=HPG)
        v_sb = region[:, 3072:5120].rearrange("p (t e) -> p t e", t=4)
        probs = region[:, 5120:7168].rearrange("p (b c k) -> p b c k", b=2, c=2)
        aT = region[:, 7168:8192].rearrange("p (b k) -> p b k", b=2)
        xn0 = region[:, 0:4096].rearrange("p (t d) -> p t d", t=TT)
        small_rows = region[:, 4096:4608].rearrange("p (n k) -> p n k", n=4)
        lam_rows = region[:, 4608:4864].rearrange("p (n k) -> p n k", n=4)
        start_rows = region[:, 5120:6144].rearrange("p (n k) -> p n k", n=2)
        xs = region[:, 0:4096].rearrange("p (t d) -> p t d", t=TT)
        gate_row = region[:, 4096:6144]
        silu_g = region[:, 6144:6656].rearrange("p (b t) -> p b t", b=2)
        act_f = region[:, 6656:7168].rearrange("p (b t) -> p b t", b=2)
        uT = region[:, 4096:8192].rearrange("p (k t) -> p k t", k=KT)
        dft_sb = y[:, 0, :]
        dft_group = dft_sb[:, 0:1024].rearrange("p (k f) -> p k f", k=2)
        dft_cos = dft_sb[:, 1024:1536].rearrange("p (k t) -> p k t", k=2)
        dft_sin = dft_sb[:, 1536:2048].rearrange("p (k t) -> p k t", k=2)
        ab = y[:, 1, :].rearrange("p (b t f) -> p b t f", b=2, t=2)

        cst = sb("cst", [P, C_END])
        ident = cst[:, C_IDENT:C_IDENT + P]
        rope_cos = cst[:, C_COS:C_COS + SEQ]
        rope_sin = cst[:, C_SIN:C_SIN + SEQ]
        rope_c = sb("rope_c", [P, SEQ])
        rope_s = sb("rope_s", [P, SEQ])
        row_sb = sb("row_sb", [P, 512])
        gate16 = sb("gate16", [16, P])
        c_cols = sb("c_cols", [P, 2 * KT])
        g_cols = sb("g_cols", [P, 8 * KT])
        b_cols = sb("b_cols", [P, 12 * KT])
        p_cols = sb("p_cols", [P, 12 * KT])
        silu_c = sb("silu_c", [P, 2 * KT])
        start_w = sb("start_w", [P, KT, 32])
        start_cols = sb("start_cols", [P, 2, 2, KT])
        ab_cols = sb("ab_cols", [P, 2, KT])
        gate_cols = sb("gate_cols", [P, KT])
        ones = sb("ones", [P, 32])
        subln = sb("subln", [P, 1])
        lam_prod = sb("lam_prod", [P, 2, HEAD_DIM])
        lam_s = sb("lam_s", [P, 4])
        stat = sb("stat", [P, 8, 16])
        s_max, s_neg, s_sum, s_rec, s_sq, s_ms, s_rstd, s_half = (stat[:, n, :] for n in range(8))
        junk = sb("junk", [P, 512], BF16)
        spare = sb("spare", [P, 2])

        ps = es.enter_context(nc.psum_tensor("ps", [P, 8, 512], F32))

        raw_landed = [sem(f"raw_landed{s}") for s in range(RING)]
        start_used = sem("start_used")
        raw_done = sem("raw_done")
        hi_ready = sem("hi_ready")
        chunk_used = sem("chunk_used")
        acc_free = sem("acc_free")
        row_copied = sem("row_copied")
        cols_made = sem("cols_made")
        cols_copied = sem("cols_copied")
        in_x = sem("in_x")
        in_ctx = sem("in_ctx")
        in_small = sem("in_small")
        in_xs = sem("in_xs")
        in_dft = sem("in_dft")
        half_set = sem("half_set")
        zeros_set = sem("zeros_set")
        dve_step = sem("dve_step")
        act_step = sem("act_step")
        rope_step = sem("rope_step")
        small_T = sem("small_T")
        small_cols = sem("small_cols")
        silu_c_made = sem("silu_c_made")
        start_w_made = sem("start_w_made")
        start_row = sem("start_row")
        start_T = sem("start_T")
        lam_summed = sem("lam_summed")
        lam_exp = sem("lam_exp")
        sq_made = sem("sq_made")
        ms_made = sem("ms_made")
        rstd_made = sem("rstd_made")
        xn_made = sem("xn_made")
        ab_made = sem("ab_made")
        pair_T = sem("pair_T")
        pair_dve = sem("pair_dve")
        pair_act = sem("pair_act")
        pair_hi = sem("pair_hi")
        pair_lo = sem("pair_lo")
        q_copied = sem("q_copied")
        k_copied = sem("k_copied")
        qk_ready = sem("qk_ready")
        v_act = sem("v_act")
        v_dve = sem("v_dve")
        scores_done = sem("scores_done")
        neg_made = sem("neg_made")
        exp_done = sem("exp_done")
        mix_done = sem("mix_done")
        mix_T = sem("mix_T")
        aT_ready = sem("aT_ready")
        pv_done = sem("pv_done")
        o_copied = sem("o_copied")
        head_ms = sem("head_ms")
        head_rstd = sem("head_rstd")
        wo_copied = sem("wo_copied")
        gate_T = sem("gate_T")
        gate_col = sem("gate_col")
        gate_16 = sem("gate_16")
        gate_dma = sem("gate_dma")
        res_done = sem("res_done")
        y_zero = [sem(f"y_zero{l}") for l in range(2)]
        y_added = [sem(f"y_added{l}") for l in range(2)]
        silu_done = [sem(f"silu_done{l}") for l in range(2)]
        act_done = [sem(f"act_done{l}") for l in range(2)]
        act_hi_done = [sem(f"act_hi_done{l}") for l in range(2)]
        act_lo_done = [sem(f"act_lo_done{l}") for l in range(2)]
        u_copied = sem("u_copied")
        ab_done = sem("ab_done")
        ab_copied = sem("ab_copied")
        f_done = sem("f_done")
        f_hi = sem("f_hi")
        f_lo = sem("f_lo")
        fo_copied = sem("fo_copied")
        out_done = sem("out_done")

        block = es.enter_context(nc.Block())

        N_LAT, N_CTX, N_ATT, N_X0, N_FFN0, N_X1, N_FOUR, N_X2, N_FFN1 = range(9)

        @block.sync
        def _(sp):
            def load(src, n0, per_turn, i):
                sp.wait_ge(raw_done, at(n0 + 1, per_turn, i))
                s = n0 % RING
                k = src.shape[1] if len(src.shape) == 3 else 1
                dst = raw[:, s, :] if k == 1 else raw[:, s, :].rearrange("p (k c) -> p k c", k=k)
                sp.dma_start(dst, src).then_inc(raw_landed[s], 16)

            def cols(w, col):
                return w[0:D, bass.ds(col, P)].rearrange("(k p) c -> p k c", p=P)

            def rows(w, row, col):
                return w[bass.ds(row, 4 * P), bass.ds(col, 512)].rearrange("(k p) c -> p k c", p=P)

            def stage(st, source, param, i=None):
                n0 = st.raw0
                for kind, j in st.order():
                    if kind == "w":
                        src = source(j)
                    else:
                        layer = 0 if param[0] == 0 else 1
                        src = mod_d[layer * D + j * P:layer * D + (j + 1) * P, bass.ds(param[1] * D, D)]
                    load(src, n0, st.n_raw, i)
                    n0 += 1

            for n in range(START_CHUNKS):
                if n >= RING:
                    sp.wait_ge(start_used, n - RING + 1)
                par, kt = divmod(n, KT)
                sp.dma_start(raw[:, n % RING, :], mod_d[kt * P:(kt + 1) * P, par * D:(par + 1) * D])\
                    .then_inc(raw_landed[n % RING], 16)
            sp.wait_ge(start_used, START_CHUNKS)

            with sp.Fori(0, GROUPS) as i:
                def qkv(j):
                    kind, t = divmod(j, HPG)
                    if kind < 2:
                        return cols(qkv_d, i * 512 + (kind * D + t * P))
                    return rows(qkv_d, t * 512, i * 512 + 2 * D)
                stage(QKV, qkv, (0, i + 2), i)

            stage(WO, lambda j: rows(wo_d, (j % 4) * 512, (j // 4) * 512), (1, 0))

            for layer in range(2):
                gu = gu_d[layer * D:(layer + 1) * D, :]
                dn = down_d[layer * FFN:(layer + 1) * FFN, :]
                up, loop, down = FFN_STAGES[layer]

                def up_src(part, j):
                    return cols(gu, part * PART + ((j // 2) * P + (j % 2) * FFN))

                def down_src(part, j):
                    return rows(dn, part * PART, j * 512)

                stage(up, lambda j: up_src(0, j), None)
                with sp.Fori(0, 5) as i:
                    def body(j):
                        half, k = divmod(j, 12)
                        if k < 8:
                            return up_src(2 * i + (1 + half), k)
                        return down_src(2 * i + half, k - 8)
                    stage(loop, body, (1, i + 1), i)
                stage(down, lambda j: down_src(PARTS - 1, j), None)
                if layer == 0:
                    with sp.Fori(0, 4) as i:
                        stage(FIN, lambda j: cols(in_d, i * 512 + j * P), None, i)
                    stage(FOUT, lambda j: rows(out_w_d, (j % 4) * 512, (j // 4) * 512), None)

            for t in range(TT):
                sp.wait_ge(res_done, 12 + 2 * t + 2)
                sp.dma_start(out_d[:, t, :], xs[:, t, :]).then_inc(out_done, 16)
            sp.wait_ge(out_done, 16 * TT)
            sp.wait_ge(gate_dma, 16 * 8)

        @block.gpsimd
        def _(pool):
            nc.gpsimd.memset(ones[:, :], 1.0).then_inc(zeros_set, 1)
            nc.gpsimd.memset(start_w[:, :, :], 0.0).then_inc(zeros_set, 1)
            nc.gpsimd.memset(s_half, -0.5).then_inc(half_set, 1)
            pool.wait_ge(half_set, 1)

            def power(n, src_ready, count, done, width):
                pool.wait_ge(src_ready, count)
                nc.gpsimd.tensor_tensor(s_rstd[:, n:n + width], s_ms[:, n:n + width],
                                        s_half[:, 0:width], ALU.pow).then_inc(done, 1)

            def gate(n):
                pool.wait_ge(gate_16, n + 1)
                pool.dma_start(gate_scratch[n, :].rearrange("(k c) -> k c", c=P), gate16[:, :])\
                    .then_inc(gate_dma, 16)
                pool.wait_ge(gate_dma, 32 * n + 16)
                pool.dma_start(gate_row, gate_scratch[n, :].partition_broadcast(P)).then_inc(gate_dma, 16)

            power(0, ms_made, 1, rstd_made, 2)
            power(2, ms_made, 2, rstd_made, 2)
            with pool.Fori(0, GROUPS) as i:
                pool.wait_ge(head_ms, i + 1)
                nc.gpsimd.tensor_tensor(s_rstd[:, 8:16], s_ms[:, 8:16], s_half[:, 0:8], ALU.pow)\
                    .then_inc(head_rstd, 1)
            pool.wait_ge(pair_T, 8 * PREP_O + 8)
            pool.dma_start(xs, x_d).then_inc(in_xs, 16)
            gate(0)
            power(0, ms_made, 3, rstd_made, 2)
            power(2, ms_made, 4, rstd_made, 2)
            for layer in range(2):
                pool.wait_ge(pair_T, 8 * (PREP_F0, PREP_F1)[layer] + 8)
                for n in range(4):
                    nc.gpsimd.memset(y[:, n // 2, (n % 2) * 1024:(n % 2 + 1) * 1024], 0.0)\
                        .then_inc(y_zero[layer], 1)
                gate(1 + 2 * layer)
                power(0, ms_made, 5 + 4 * layer, rstd_made, 2)
                if layer == 0:
                    power(2, ms_made, 6, rstd_made, 2)
                    pool.wait_ge(pair_T, 8 * PREP_FOUR + 8)
                    pool.dma_start(dft_sb, dft).then_inc(in_dft, 16)
                    pool.wait_ge(ab_done, 16)
                    gate(2)
                    power(0, ms_made, 7, rstd_made, 2)
                    power(2, ms_made, 8, rstd_made, 2)

        @block.scalar
        def _(act):
            link = Link(act, act_step)

            def high(st, j, i=None):
                n, m = st.raw(j), st.w0 + j
                act.wait_ge(raw_landed[n % RING],
                            at(16 * ((START_CHUNKS + n) // RING + 1), 16 * st.n_raw // RING, i))
                if m >= 2:
                    act.wait_ge(chunk_used, at(m - 1, st.n_w, i))
                nc.scalar.activation(w_hi[:, m % 2, :], raw[:, n % RING, :], ACT.Copy).then_inc(hi_ready, 1)

            def used(st, j, i=None):
                act.wait_ge(chunk_used, at(st.w0 + j + 1, st.n_w, i))

            def prep(n, hi):
                def odd(pr):
                    act.wait_ge(pair_T, 8 * n + pr + 1)
                    act.wait_ge(ab_made, n + 1)
                    if pr >= 4 or n:
                        act.wait_ge(pair_lo, 8 * n + max(pr - 3, 0))
                    for k in range(2):
                        kt = 2 * pr + k
                        ins = nc.scalar.activation(htmp[:, pr % 4, k, :], ps[:, pr, k * 256:(k + 1) * 256],
                                                   ACT.Identity, bias=ab_cols[:, 1, kt:kt + 1],
                                                   scale=ab_cols[:, 0, kt:kt + 1])
                        ins.then_inc(pair_act, 1)

                def high_pair(pr):
                    if pr % 2:
                        act.wait_ge(pair_act, 8 * n + pr + 1)
                    else:
                        act.wait_ge(pair_dve, 8 * n + pr + 2)
                    nc.scalar.activation(hT[:, 2 * pr:2 * pr + 2, hi, :], htmp[:, pr % 4, :, :], ACT.Copy)\
                        .then_inc(pair_hi, 1)

                for pr in range(0, 8, 2):
                    odd(pr + 1)
                    high_pair(pr)
                    high_pair(pr + 1)

            def squares(n, parts, ready):
                for p, (sem_, val) in enumerate(ready):
                    t, b = divmod(p, 4)
                    act.wait_ge(sem_, val)
                    ins = nc.scalar.activation(junk[:, :], parts[:, t, b * 512:(b + 1) * 512], ACT.Square,
                                               accum_out=s_sq[:, p:p + 1])
                    if p < 7:
                        link(ins)
                ins.then_inc(sq_made, 1)
                act.wait_ge(sq_made, n + 1)

            def row_copy(p, i=None):
                act.wait_ge(acc_free, at(p + 2, 1, i))
                nc.scalar.activation(row_sb[:, :], ps[:, SUM_BANK, :], ACT.Copy).then_inc(row_copied, 1)

            def gate(n):
                act.wait_ge(gate_T, n + 1)
                if n:
                    act.wait_ge(gate_dma, 32 * n)
                nc.scalar.activation(gate16[:, :], ps[0:16, SUM_BANK, 0:P], ACT.Copy).then_inc(gate_16, 1)

            act.dma_start(small_rows[0:16, 0, :], c.rearrange("b (k c) -> (b k) c", c=P)).then_inc(in_small, 16)
            act.dma_start(small_rows[16:32, 0, :], c_ctx.rearrange("(k c) -> k c", c=P)).then_inc(in_small, 16)
            act.dma_start(small_rows[:, 1, :], norm_g.rearrange("l n (k c) -> (l n k) c", c=P))\
                .then_inc(in_small, 16)
            for layer in range(2):
                act.dma_start(small_rows[0:96, 2 + layer, :], mod_b[layer, :].rearrange("(k c) -> k c", c=P))\
                    .then_inc(in_small, 16)
            act.dma_start(cst[:, :], consts).then_inc(in_small, 16)
            act.dma_start(subln[:, :], subln_g.rearrange("l e -> e l")).then_inc(in_small, 16)
            act.dma_start(lam_rows[:, :, :], lam.rearrange("l n d -> (l n) d").partition_broadcast(P))\
                .then_inc(in_small, 16)
            act.dma_start(xn0, x_d).then_inc(in_x, 16)
            act.dma_start(y[:, :, :], ctx_d).then_inc(in_ctx, 16)

            act.wait_ge(small_cols, 3)
            nc.scalar.activation(silu_c[:, :], c_cols[:, :], ACT.Silu).then_inc(silu_c_made, 1)
            squares(N_LAT, xn0, [(in_x, 16)] * 8)
            act.wait_ge(ms_made, 1)
            squares(N_CTX, y, [(in_ctx, 16)] * 8)
            act.wait_ge(lam_summed, 1)
            nc.scalar.activation(lam_s[:, 2:4], lam_s[:, 0:2], ACT.Exp).then_inc(lam_exp, 1)
            for par in range(2):
                act.wait_ge(start_used, KT * (par + 1))
                nc.scalar.activation(start_rows[:, par, :], ps[:, par, :], ACT.Copy).then_inc(start_row, 1)
            high(QKV, 0)
            high(QKV, 1)
            prep(PREP_LAT, LAT_HI)
            prep(PREP_CTX, CTX_HI)

            with act.Fori(0, GROUPS) as i:
                for s in range(QKV.n_w):
                    high(QKV, s + 2, i)
                    used(QKV, s, i)
                    if 4 <= s < 8:
                        nc.scalar.activation(kT[:, s - 4, :], ps[:, s % 2, :], ACT.Copy).then_inc(k_copied, 1)
                    if s == 10:
                        row_copy(0, i)
                for t in range(2):
                    nc.scalar.activation(v_sb[:, t, :], ps[:, 2 + t, :], ACT.Copy).then_inc(v_act, 1)

                def exps(u):
                    act.wait_ge(neg_made, at(u + 1, 8, i))
                    if u >= 2:
                        act.wait_ge(mix_T, at(u - 1, 8, i))
                    for h in range(2):
                        bank = 2 * (u % 3) + h
                        nc.scalar.activation(probs[:, u % 2, h, :], ps[:, bank, :], ACT.Exp,
                                             bias=s_neg[:, 2 * u + h:2 * u + h + 1], scale=SCALE,
                                             accum_out=s_sum[:, 2 * u + h:2 * u + h + 1]).then_inc(exp_done, 1)

                def mixT(u):
                    act.wait_ge(mix_T, at(u + 1, 8, i))
                    if u >= 2:
                        act.wait_ge(pv_done, at(u - 1, 8, i))
                    nc.scalar.activation(aT[:, u % 2, :], ps[:, COL_BANK, :], ACT.Copy).then_inc(aT_ready, 1)

                exps(0)
                for u in range(8):
                    if u + 1 < 8:
                        exps(u + 1)
                    mixT(u)

            prep(PREP_O, LAT_HI)

            for s in range(WO.n_w):
                high(WO, s + 2)
                if s % 4 == 3:
                    used(WO, s)
                    for t in range(2):
                        nc.scalar.activation(y[:, t, (s // 4) * 512:(s // 4 + 1) * 512],
                                             ps[:, ROW_BANKS[(s // 4) % 2][t], :], ACT.Copy)\
                            .then_inc(wo_copied, 1)
                if s == 14:
                    row_copy(4)
            gate(0)
            squares(N_ATT, y, [(wo_copied, 2 * b + t + 1) for t in range(2) for b in range(4)])

            def ffn(layer):
                up, loop, down = FFN_STAGES[layer]

                def up_step(st, s, hidden, per, slot, i=None):
                    if s % 2 == 0:
                        used(st, s, i)
                        nc.scalar.activation(silu_g[:, hidden % 2, :], ps[:, 0, 0:256], ACT.Silu)\
                            .then_inc(silu_done[layer], 1)
                    else:
                        act.wait_ge(act_done[layer], at(hidden + 1, per, i))
                        nc.scalar.activation(act_hi[:, slot, :], act_f[:, hidden % 2, :], ACT.Copy)\
                            .then_inc(act_hi_done[layer], 1)

                for s in range(8):
                    high(up, s + 2)
                    up_step(up, s, s // 2, 0, s // 2)
                with act.Fori(0, 5) as i:
                    for s in range(24):
                        high(loop, s + 2, i)
                        half, k = divmod(s, 12)
                        if k < 8:
                            up_step(loop, s, 4 + 4 * half + k // 2, 8, 4 * (1 - half) + k // 2, i)
                        if layer == 0 and s == 22:
                            row_copy(5, i)
                for s in range(4):
                    if layer == 0 or s < 2:
                        if not (layer == 1 and s + 2 >= 4):
                            high(down, s + 2)
                gate(1 + 2 * layer)
                base = 8 * (PARTS - 1)
                squares(N_FFN0 if layer == 0 else N_FFN1, y,
                        [(y_added[layer], base + 2 * b + t + 1) for t in range(2) for b in range(4)])

            def squares_x(n, r):
                act.wait_ge(ms_made, n)
                squares(n, xs, [(res_done, 4 * r + 2 * (p // 4) + 2) for p in range(8)])

            squares_x(N_X0, 0)
            prep(PREP_F0, LAT_HI)
            ffn(0)
            squares_x(N_X1, 1)
            prep(PREP_FOUR, LAT_HI)

            for n in range(2):
                nc.scalar.activation(spare[:, n:n + 1], ones[:, n:n + 1], ACT.Copy).then_inc(u_copied, 1)
            with act.Fori(0, 4) as i:
                for s in range(4):
                    high(FIN, s + 2, i)
                    used(FIN, s, i)
                    nc.scalar.activation(uT[:, bass.ds(i * 4 + s, 1), :], ps[:, s % 2, 0:256]
                                         .unsqueeze(1), ACT.Copy).then_inc(u_copied, 1)
            for f in range(KT):
                act.wait_ge(f_done, f + 1)
                nc.scalar.activation(hT[:, f, CTX_HI, :], ps[:, 4 + f % 2, 0:256], ACT.Copy).then_inc(f_hi, 1)
            for s in range(FOUT.n_w):
                high(FOUT, s + 2)
                if s % 4 == 3:
                    used(FOUT, s)
                    for t in range(2):
                        nc.scalar.activation(y[:, t, (s // 4) * 512:(s // 4 + 1) * 512],
                                             ps[:, ROW_BANKS[(s // 4) % 2][t], :], ACT.Copy)\
                            .then_inc(fo_copied, 1)
            gate(2)
            squares(N_FOUR, y, [(fo_copied, 2 * b + t + 1) for t in range(2) for b in range(4)])
            squares_x(N_X2, 2)
            prep(PREP_F1, LAT_HI)
            ffn(1)

        @block.vector
        def _(dve):
            link = Link(dve, dve_step)

            def low(st, j, i=None):
                n, m = st.raw(j), st.w0 + j
                dve.wait_ge(hi_ready, at(m + 1, st.n_w, i))
                nc.vector.tensor_tensor(w_lo[:, m % 2, :], raw[:, n % RING, :],
                                        w_hi[:, m % 2, :].bitcast(F32), ALU.subtract).then_inc(raw_done, 1)
                if j >= st.n_w:
                    return
                for q in range(st.hosts[j]):
                    n += 1
                    kt = sum(st.hosts[:j]) + q
                    dve.wait_ge(raw_landed[n % RING],
                                at(16 * ((START_CHUNKS + n) // RING + 1), 16 * st.n_raw // RING, i))
                    if kt == 0:
                        dve.wait_ge(acc_free, at(st.m0 // KT + 1, 1, i))
                        nc.vector.tensor_scalar(acc[:, :], raw[:, n % RING, :], silu_c[:, 0:1], None,
                                                ALU.mult).then_inc(raw_done, 1)
                    else:
                        dve.wait_ge(raw_done, at(n + PRE, st.n_raw, i))
                        nc.vector.scalar_tensor_tensor(out=acc[:, :], in0=raw[:, n % RING, :],
                                                       scalar=silu_c[:, kt:kt + 1], in1=acc[:, :],
                                                       op0=ALU.mult, op1=ALU.add).then_inc(raw_done, 1)

            def used(st, j, i=None):
                dve.wait_ge(chunk_used, at(st.w0 + j + 1, st.n_w, i))

            def prep(n, lo, hi):
                def even(pr):
                    dve.wait_ge(pair_T, 8 * n + pr + 1)
                    if pr >= 4:
                        dve.wait_ge(pair_lo, 8 * n + pr - 3)
                    for k in range(2):
                        kt = 2 * pr + k
                        nc.vector.tensor_scalar(htmp[:, pr % 4, k, :], ps[:, pr, k * 256:(k + 1) * 256],
                                                ab_cols[:, 0, kt:kt + 1], ab_cols[:, 1, kt:kt + 1],
                                                ALU.mult, ALU.add).then_inc(pair_dve, 1)

                def low_pair(pr):
                    dve.wait_ge(pair_hi, 8 * n + pr + 1)
                    nc.vector.tensor_tensor(hT[:, 2 * pr:2 * pr + 2, lo, :], htmp[:, pr % 4, :, :],
                                            hT[:, 2 * pr:2 * pr + 2, hi, :].bitcast(F32), ALU.subtract)\
                        .then_inc(pair_lo, 1)

                even(0)
                for pr in range(0, 8, 2):
                    if pr + 2 < 8:
                        even(pr + 2)
                    low_pair(pr)
                    low_pair(pr + 1)

            def mean_square(n):
                dve.wait_ge(sq_made, n + 1)
                link(nc.vector.tensor_reduce(s_max[:, 0:2], s_sq[:, 0:8].rearrange("p (t b) -> p t b", t=2),
                                             AX_X, ALU.add))
                o = 2 * (n % 2 if n < 2 else (n - 2) % 2)
                nc.vector.tensor_scalar(s_ms[:, o:o + 2], s_max[:, 0:2], 1.0 / D, EPS, ALU.mult, ALU.add)\
                    .then_inc(ms_made, 1)
                dve.wait_ge(rstd_made, n + 1)
                return s_rstd[:, o:o + 2]

            def normalise(dst, src, rstd):
                for t in range(TT):
                    nc.vector.tensor_scalar(dst[:, t, :], src[:, t, :], rstd[:, t:t + 1], None, ALU.mult)\
                        .then_inc(xn_made, 1)

            def cols_of(layer, par):
                return slice((6 * layer + par) * KT, (6 * layer + par + 1) * KT)

            def modulation(layer, shift, scale, norm):
                link(nc.vector.scalar_tensor_tensor(
                    out=ab_cols[:, 0, :], in0=p_cols[:, cols_of(layer, scale)], scalar=1.0,
                    in1=b_cols[:, cols_of(layer, scale)], op0=ALU.add, op1=ALU.add))
                g = g_cols[:, (4 * layer + norm) * KT:(4 * layer + norm + 1) * KT]
                link(nc.vector.tensor_tensor(ab_cols[:, 0, :], ab_cols[:, 0, :], g, ALU.mult))
                nc.vector.tensor_tensor(ab_cols[:, 1, :], p_cols[:, cols_of(layer, shift)],
                                        b_cols[:, cols_of(layer, shift)], ALU.add).then_inc(ab_made, 1)

            def gate(n, layer, par, norm):
                if n:
                    dve.wait_ge(gate_T, n)
                link(nc.vector.tensor_tensor(gate_cols[:, :], p_cols[:, cols_of(layer, par)],
                                             b_cols[:, cols_of(layer, par)], ALU.add))
                g = g_cols[:, (4 * layer + norm) * KT:(4 * layer + norm + 1) * KT]
                nc.vector.tensor_tensor(gate_cols[:, :], gate_cols[:, :], g, ALU.mult).then_inc(gate_col, 1)

            def residual(n, r, norm):
                rstd = mean_square(norm)
                dve.wait_ge(gate_dma, 32 * n + 32)
                if n == 0:
                    dve.wait_ge(in_xs, 16)
                for t in range(TT):
                    nc.vector.scalar_tensor_tensor(out=y[:, t, :], in0=y[:, t, :], scalar=rstd[:, t:t + 1],
                                                   in1=gate_row, op0=ALU.mult, op1=ALU.mult)\
                        .then_inc(res_done, 1)
                    dve.wait_ge(res_done, 4 * r + 2 * t + 1)
                    nc.vector.tensor_tensor(xs[:, t, :], xs[:, t, :], y[:, t, :], ALU.add)\
                        .then_inc(res_done, 1)

            def param_cols(idx, count, i=None):
                dve.wait_ge(cols_made, at(count, 1, i))
                dst = p_cols[:, bass.ds(idx * KT, KT)] if i is not None else p_cols[:, idx * KT:(idx + 1) * KT]
                nc.vector.tensor_copy(dst.rearrange("p (b r) -> p r b", b=4),
                                      ps[:, COL_BANK, :].rearrange("p (r b z) -> p r b z", r=4, b=4)[:, :, :, 0])\
                    .then_inc(cols_copied, 1)

            for n in range(PRE):
                nc.vector.memset(gate_cols[:, n:n + 1], 0.0).then_inc(raw_done, 1)
            dve.wait_ge(small_T, 4)
            nc.vector.tensor_copy(c_cols[:, :], ps[:, 2, 0:32]).then_inc(small_cols, 1)
            nc.vector.tensor_copy(g_cols[:, :], ps[:, 3, 0:128]).then_inc(small_cols, 1)
            nc.vector.tensor_copy(b_cols[:, :].rearrange("p (l k) -> p l k", l=2),
                                  ps[:, 4:6, 0:96]).then_inc(small_cols, 1)
            dve.wait_ge(silu_c_made, 1)
            dve.wait_ge(zeros_set, 2)
            nc.vector.tensor_copy(start_w[:, :, 0:2], silu_c[:, :].rearrange("p (v k) -> p k v", v=2))\
                .then_inc(start_w_made, 1)
            link(nc.vector.tensor_tensor(lam_prod[:, :, :], lam_rows[:, 0::2, :], lam_rows[:, 1::2, :], ALU.mult))
            nc.vector.tensor_reduce(lam_s[:, 0:2], lam_prod[:, :, :], AX_X, ALU.add).then_inc(lam_summed, 1)
            link(nc.vector.tensor_scalar(subln[:, :], subln[:, :], 1.0 - LAMBDA_INIT, None, ALU.mult))
            normalise(xn0, xn0, mean_square(N_LAT))
            normalise(y, y, mean_square(N_CTX))
            dve.wait_ge(lam_exp, 1)
            link(nc.vector.tensor_scalar(lam_s[:, 0:1], lam_s[:, 3:4], -LAMBDA_INIT, None, ALU.add))
            link(nc.vector.tensor_tensor(lam_s[:, 0:1], lam_s[:, 0:1], lam_s[:, 2:3], ALU.subtract))
            neg_lam = lam_s[:, 0:1]
            dve.wait_ge(start_T, 1)
            for par in range(2):
                for v in range(2):
                    link(nc.vector.tensor_copy(
                        start_cols[:, par, v, :].rearrange("p (b r) -> p r b", b=4),
                        ps[:, 6 + par, :].rearrange("p (r b z) -> p r b z", r=4, b=4)[:, :, :, v]))

            def start_modulation(v):
                link(nc.vector.scalar_tensor_tensor(
                    out=ab_cols[:, 0, :], in0=start_cols[:, 1, v, :], scalar=1.0,
                    in1=b_cols[:, cols_of(0, 1)], op0=ALU.add, op1=ALU.add))
                link(nc.vector.tensor_tensor(ab_cols[:, 0, :], ab_cols[:, 0, :], g_cols[:, 0:KT], ALU.mult))
                nc.vector.tensor_tensor(ab_cols[:, 1, :], start_cols[:, 0, v, :], b_cols[:, cols_of(0, 0)],
                                        ALU.add).then_inc(ab_made, 1)
                dve.wait_ge(ab_made, v + 1)

            start_modulation(0)
            prep(PREP_LAT, LAT_LO, LAT_HI)
            dve.wait_ge(pair_act, 8)
            dve.wait_ge(pair_dve, 8)
            start_modulation(1)
            prep(PREP_CTX, CTX_LO, CTX_HI)
            low(QKV, 0)
            low(QKV, 1)

            SWAP = [(r + 16) % 32 for r in range(32)]

            def rope(t, tile, i):
                nc.vector.tensor_tensor(rope_c[:, :], t, rope_cos, ALU.mult).then_inc(rope_step, 1)
                link(nc.vector.stream_shuffle(rope_s[:, :], t, SWAP))
                nc.vector.tensor_tensor(rope_s[:, :], rope_s[:, :], rope_sin, ALU.mult).then_inc(rope_step, 1)
                dve.wait_ge(rope_step, at(2 * tile + 2, 16, i))
                nc.vector.tensor_tensor(t, rope_c[:, :], rope_s[:, :], ALU.add).then_inc(qk_ready, 1)

            with dve.Fori(0, GROUPS) as i:
                link.turn(i, 8 * 1 + 8 * 3 + 2)
                for s in range(QKV.n_w):
                    if s < 4:
                        used(QKV, s, i)
                        nc.vector.tensor_copy(qT[:, s, :], ps[:, s % 2, 0:256]).then_inc(q_copied, 1)
                        dve.wait_ge(q_copied, at(s + 1, 4, i))
                        if s:
                            dve.wait_ge(qk_ready, at(s, 8, i))
                        rope(qT[:, s, :], s, i)
                    elif s < 8:
                        dve.wait_ge(k_copied, at(s - 3, 4, i))
                        dve.wait_ge(qk_ready, at(s, 8, i))
                        rope(kT[:, s - 4, 0:256], s, i)
                    low(QKV, s + 2, i)
                used(QKV, 11, i)
                for t in range(2, 4):
                    nc.vector.tensor_copy(v_sb[:, t, :], ps[:, 2 + t, :]).then_inc(v_dve, 1)
                param_cols(i + 2, 1, i)

                def maxima(u):
                    dve.wait_ge(scores_done, at(u + 1, 8, i))
                    bank = 2 * (u % 3)
                    link(nc.vector.tensor_reduce(s_max[:, 2 * u:2 * u + 2], ps[:, bank:bank + 2, :], AX_X, ALU.max))
                    nc.vector.tensor_scalar(s_neg[:, 2 * u:2 * u + 2], s_max[:, 2 * u:2 * u + 2], -SCALE, None,
                                            ALU.mult).then_inc(neg_made, 1)

                def mix(u):
                    dve.wait_ge(exp_done, at(2 * u + 2, 16, i))
                    link(nc.vector.reciprocal(s_rec[:, 2 * u:2 * u + 2], s_sum[:, 2 * u:2 * u + 2]))
                    e0, e1 = probs[:, u % 2, 0, :], probs[:, u % 2, 1, :]
                    nc.vector.tensor_scalar(e1, e1, s_rec[:, 2 * u + 1:2 * u + 2], neg_lam, ALU.mult, ALU.mult)\
                        .then_inc(dve_step, 1)
                    link.n += 1
                    dve.wait_ge(dve_step, link.n + link.more)
                    nc.vector.scalar_tensor_tensor(out=e0, in0=e0, scalar=s_rec[:, 2 * u:2 * u + 1], in1=e1,
                                                   op0=ALU.mult, op1=ALU.add).then_inc(mix_done, 1)

                def o_copy(u):
                    h, t = divmod(u, 2)
                    dve.wait_ge(pv_done, at(u + 1, 8, i))
                    nc.vector.tensor_copy(y[:, t, bass.ds(i * 512 + h * P, P)],
                                          ps[:, SUM_BANK, (u % 4) * P:(u % 4 + 1) * P]).then_inc(o_copied, 1)

                maxima(0)
                maxima(1)
                for u in range(8):
                    mix(u)
                    if u + 2 < 8:
                        maxima(u + 2)
                    if u:
                        o_copy(u - 1)
                o_copy(7)
                dve.wait_ge(o_copied, at(8, 8, i))
                sq = probs[:, 0, :, :]
                o = y[:, :, bass.ds(i * 512, 512)]
                link(nc.vector.tensor_tensor(sq, o, o, ALU.mult))
                link(nc.vector.tensor_reduce(s_sq[:, 8:16], sq.rearrange("p t (h e) -> p t h e", h=4), AX_X, ALU.add))
                nc.vector.tensor_scalar(s_ms[:, 8:16], s_sq[:, 8:16], 1.0 / P, EPS, ALU.mult, ALU.add)\
                    .then_inc(head_ms, 1)
                dve.wait_ge(head_rstd, i + 1)
                for t in range(TT):
                    o = y[:, t, bass.ds(i * 512, 512)].rearrange("p (h e) -> p h e", h=4)
                    r = s_rstd[:, 8 + 4 * t:12 + 4 * t].unsqueeze(2).to_broadcast([P, 4, P])
                    nc.vector.tensor_tensor(o, o, r, ALU.mult).then_inc(xn_made, 1)
            link.end(GROUPS)

            dve.wait_ge(pair_act, 16)
            link(nc.vector.tensor_copy(ab_cols[:, 0, :], subln[:, 0:1].to_broadcast([P, KT])))
            nc.vector.memset(ab_cols[:, 1, :], 0.0).then_inc(ab_made, 1)
            dve.wait_ge(ab_made, 3)
            prep(PREP_O, LAT_LO, LAT_HI)

            gate(0, 0, 2, 1)
            for s in range(WO.n_w):
                low(WO, s + 2)
            param_cols(6, 5)
            residual(0, 0, N_ATT)

            def next_input(n, prep_n, layer, shift, scale, norm):
                modulation(layer, shift, scale, norm)
                normalise(y, xs, mean_square(n))
                dve.wait_ge(ab_made, prep_n + 1)
                prep(prep_n, LAT_LO, LAT_HI)

            next_input(N_X0, PREP_F0, 0, 3, 4, 2)

            def ffn(layer):
                up, loop, down = FFN_STAGES[layer]
                gate(1 + 2 * layer, layer, 5, 3)

                def act_mul(st, s, hidden, per, i=None):
                    used(st, s, i)
                    dve.wait_ge(silu_done[layer], at(hidden + 1, per, i))
                    if hidden >= 2:
                        dve.wait_ge(act_lo_done[layer], at(hidden - 1, per, i))
                    nc.vector.tensor_tensor(act_f[:, hidden % 2, :], ps[:, 1, 0:256], silu_g[:, hidden % 2, :],
                                            ALU.mult).then_inc(act_done[layer], 1)

                def act_low(hidden, per, slot, i=None):
                    dve.wait_ge(act_hi_done[layer], at(hidden + 1, per, i))
                    nc.vector.tensor_tensor(act_lo[:, slot, :], act_f[:, hidden % 2, :],
                                            act_hi[:, slot, :].bitcast(F32), ALU.subtract)\
                        .then_inc(act_lo_done[layer], 1)

                def add(st, s, b, part8, i=None):
                    used(st, s, i)
                    for t in range(TT):
                        done = part8 + 2 * b + t
                        if i is not None or done:
                            if part8 or i is None:
                                dve.wait_ge(y_added[layer], at(done, 16, i))
                        blk = y[:, t, b * 512:(b + 1) * 512]
                        nc.vector.tensor_tensor(blk, blk, ps[:, ROW_BANKS[b % 2][t], :], ALU.add)\
                            .then_inc(y_added[layer], 1)

                for s in range(8):
                    if s % 2:
                        act_mul(up, s, s // 2, 0)
                    low(up, s + 2)
                    if s % 2:
                        act_low(s // 2, 0, s // 2)
                dve.wait_ge(y_zero[layer], 4)
                with dve.Fori(0, 5) as i:
                    for s in range(24):
                        half, k = divmod(s, 12)
                        hidden = 4 + 4 * half + k // 2
                        if k < 8 and k % 2:
                            act_mul(loop, s, hidden, 8, i)
                        if k >= 8:
                            add(loop, s, k - 8, 8 * half, i)
                        low(loop, s + 2, i)
                        if k < 8 and k % 2:
                            act_low(hidden, 8, 4 * (1 - half) + k // 2, i)
                    if layer == 0:
                        param_cols(i + 7, 6, i)
                for s in range(4):
                    add(down, s, s, 8 * (PARTS - 1))
                    if not (layer == 1 and s + 2 >= 4):
                        low(down, s + 2)

            ffn(0)
            residual(1, 1, N_FFN0)
            next_input(N_X1, PREP_FOUR, 1, 0, 1, 0)

            with dve.Fori(0, 4) as i:
                for s in range(4):
                    low(FIN, s + 2, i)
            gate(2, 1, 2, 1)

            def f_low(f):
                dve.wait_ge(f_hi, f + 1)
                nc.vector.tensor_tensor(hT[:, f, CTX_LO, :], ps[:, 4 + f % 2, 0:256],
                                        hT[:, f, CTX_HI, :].bitcast(F32), ALU.subtract).then_inc(f_lo, 1)

            for g in range(FGROUPS):
                for t in range(TT):
                    dve.wait_ge(ab_done, 2 * g + t + 1)
                    nc.vector.tensor_copy(ab[:, g % 2, t, :], ps[:, 2 + t, :]).then_inc(ab_copied, 1)
                if g:
                    f_low(2 * g - 2)
                    f_low(2 * g - 1)
            f_low(KT - 2)
            f_low(KT - 1)
            for s in range(FOUT.n_w):
                low(FOUT, s + 2)
            residual(2, 2, N_FOUR)
            next_input(N_X2, PREP_F1, 1, 3, 4, 2)
            ffn(1)
            residual(3, 3, N_FFN1)

        @block.tensor
        def _(pe):
            def chunk(st, j, i=None):
                n = st.raw(j)
                pe.wait_ge(raw_done, at(n + PRE + 1, st.n_raw, i))
                return (st.w0 + j) % 2

            def column_tile(st, j, bank, i=None, both=False, ready=None):
                slot = chunk(st, j, i)
                n = 512 if both else 256
                for kt in range(KT):
                    if ready is not None and kt % 2 == 0:
                        pe.wait_ge(pair_lo, ready + kt // 2 + 1)
                    for q, (w, part) in enumerate(((w_hi, LAT_HI), (w_hi, LAT_LO), (w_lo, LAT_HI))):
                        rhs = hT[:, kt, part:part + (2 if both else 1), :]
                        last = nc.tensor.matmul(ps[:, bank, 0:n], w[:, slot, kt * P:(kt + 1) * P], rhs,
                                                start=(kt == 0 and q == 0), stop=(kt == KT - 1 and q == 2))
                last.then_inc(chunk_used, 1)

            def row_chunk(st, j, tiles, first, final, i=None):
                slot = chunk(st, j, i)
                for k in range(4):
                    cols = slice(k * 512, (k + 1) * 512)
                    for bank, hi, lo in tiles:
                        for q, (a, w) in enumerate(((hi, w_hi), (lo, w_hi), (hi, w_lo))):
                            last = nc.tensor.matmul(ps[:, bank, :], a(k), w[:, slot, cols],
                                                    start=(first and k == 0 and q == 0),
                                                    stop=(final and k == 3 and q == 2))
                last.then_inc(chunk_used, 1)

            def latent_rows(b, kt0, hi=LAT_HI, lo=LAT_LO):
                return [(ROW_BANKS[b % 2][t],
                         lambda k, t=t: hT[:, kt0 + k, hi, t * P:(t + 1) * P],
                         lambda k, t=t: hT[:, kt0 + k, lo, t * P:(t + 1) * P]) for t in range(TT)]

            def prep(n, src, ready):
                for pr in range(8):
                    if n == PREP_CTX:
                        pe.wait_ge(pair_lo, pr + 1)
                        if pr % 2:
                            pe.wait_ge(pair_act, pr + 1)
                    for t in range(TT):
                        if pr == 0:
                            ready(t)
                        for k in range(2):
                            kt = 2 * pr + k
                            last = nc.tensor.transpose(ps[:, pr, k * 256 + t * P:k * 256 + (t + 1) * P],
                                                       src[:, t, kt * P:(kt + 1) * P], ident)
                    last.then_inc(pair_T, 1)

            def sum_rows(fma_raw, i=None, per_turn=0):
                pe.wait_ge(raw_done, at(fma_raw + PRE + 1, per_turn, i))
                for b in range(4):
                    last = nc.tensor.matmul(ps[32 * b:32 * b + 32, SUM_BANK, :], ones[:, :],
                                            acc[:, b * 512:(b + 1) * 512], start=True, stop=True)
                last.then_inc(acc_free, 1)

            def rows_to_cols(count, i=None):
                pe.wait_ge(row_copied, at(count, 1, i))
                for r in range(4):
                    last = nc.tensor.transpose(ps[:, COL_BANK, r * P:(r + 1) * P],
                                               row_sb[:, r * P:(r + 1) * P], ident)
                last.then_inc(cols_made, 1)

            def gate(n):
                pe.wait_ge(gate_col, n + 1)
                nc.tensor.transpose(ps[0:16, SUM_BANK, 0:P], gate_cols[:, :], ident).then_inc(gate_T, 1)

            pe.wait_ge(in_small, 16 * 8)
            pe.wait_ge(zeros_set, 1)
            for n, (rows, width) in enumerate(((32, 32), (128, 128), (96, 96), (96, 96))):
                nc.tensor.transpose(ps[:, 2 + n, 0:width], small_rows[0:rows, n, :], ident[0:rows, 0:rows])\
                    .then_inc(small_T, 1)
            pe.wait_ge(start_w_made, 1)
            for n in range(START_CHUNKS):
                par, kt = divmod(n, KT)
                pe.wait_ge(raw_landed[n % RING], 16 * (n // RING + 1))
                for b in range(4):
                    last = nc.tensor.matmul(ps[32 * b:32 * b + 32, par, :], start_w[:, kt, :],
                                            raw[:, n % RING, b * 512:(b + 1) * 512],
                                            start=(kt == 0), stop=(kt == KT - 1))
                last.then_inc(start_used, 1)
            pe.wait_ge(start_row, 2)
            for par in range(2):
                for r in range(4):
                    last = nc.tensor.transpose(ps[:, 6 + par, r * P:(r + 1) * P],
                                               start_rows[:, par, r * P:(r + 1) * P], ident)
                last.then_inc(acc_free if par == 0 else start_T, 1)
            pe.wait_ge(ab_made, 1)
            pe.wait_ge(small_cols, 3)
            prep(PREP_LAT, xn0, lambda t: pe.wait_ge(xn_made, t + 1))
            prep(PREP_CTX, y, lambda t: pe.wait_ge(xn_made, t + 3))
            pe.wait_ge(pair_lo, 16)

            with pe.Fori(0, GROUPS) as i:
                for s in range(QKV.n_w):
                    if s < 8:
                        if 2 <= s < 6:
                            pe.wait_ge(q_copied, at(s - 1, 4, i))
                        elif s >= 6:
                            pe.wait_ge(k_copied, at(s - 5, 4, i))
                        column_tile(QKV, s, s % 2, i, both=s >= 4)
                    else:
                        kt0 = 4 * (s - 8)
                        tiles = [(2 + t,
                                  lambda k, t=t: hT[:, kt0 + k, LAT_HI + t // 2, (t % 2) * P:(t % 2 + 1) * P],
                                  lambda k, t=t: hT[:, kt0 + k, LAT_LO + t // 2, (t % 2) * P:(t % 2 + 1) * P])
                                 for t in range(4)]
                        row_chunk(QKV, s, tiles, s == 8, s == 11, i)
                    if s == 10:
                        sum_rows(QKV.raw0 + QKV.n_raw - 1, i, QKV.n_raw)
                    if s == 11:
                        rows_to_cols(1, i)

                def scores(u):
                    h, t = divmod(u, 2)
                    if u == 0:
                        pe.wait_ge(qk_ready, at(8, 8, i))
                        pe.wait_ge(k_copied, at(4, 4, i))
                    if u == 1:
                        pe.wait_ge(v_act, at(2, 2, i))
                    if u == 2:
                        pe.wait_ge(v_dve, at(2, 2, i))
                    if u >= 3:
                        pe.wait_ge(exp_done, at(2 * u - 4, 16, i))
                    for cmp in range(2):
                        rows = slice(64 * cmp, 64 * cmp + 64)
                        last = nc.tensor.matmul(ps[:, 2 * (u % 3) + cmp, :], qT[rows, h, t * P:(t + 1) * P],
                                                kT[rows, h, :], start=True, stop=True)
                    last.then_inc(scores_done, 1)

                def transpose_mix(u):
                    pe.wait_ge(mix_done, at(u + 1, 8, i))
                    if u == 0:
                        pe.wait_ge(cols_copied, at(1, 1, i))
                    else:
                        pe.wait_ge(aT_ready, at(u, 8, i))
                    for k in range(4):
                        last = nc.tensor.transpose(ps[:, COL_BANK, k * P:(k + 1) * P],
                                                   probs[:, u % 2, 0, k * P:(k + 1) * P], ident)
                    last.then_inc(mix_T, 1)

                def values(u):
                    h = u // 2
                    pe.wait_ge(aT_ready, at(u + 1, 8, i))
                    if u:
                        pe.wait_ge(o_copied, at(u, 8, i))
                    for k in range(4):
                        last = nc.tensor.matmul(ps[:, SUM_BANK, (u % 4) * P:(u % 4 + 1) * P],
                                                aT[:, u % 2, k * P:(k + 1) * P], v_sb[:, k, h * P:(h + 1) * P],
                                                start=(k == 0), stop=(k == 3))
                    last.then_inc(pv_done, 1)

                scores(0)
                scores(1)
                for u in range(8):
                    if u + 2 < 8:
                        scores(u + 2)
                    transpose_mix(u)
                    if u:
                        values(u - 1)
                values(7)

            pe.wait_ge(ab_made, 3)
            prep(PREP_O, y, lambda t: pe.wait_ge(xn_made, 12))

            pe.wait_ge(pair_lo, 24)
            for s in range(WO.n_w):
                b = s // 4
                if b >= 2 and s % 4 == 0:
                    pe.wait_ge(wo_copied, 2 * (b - 1))
                row_chunk(WO, s, latent_rows(b, 4 * (s % 4)), s % 4 == 0, s % 4 == 3)
                if s == 14:
                    sum_rows(WO.raw0 + WO.n_raw - 1)
                if s == 15:
                    rows_to_cols(5)
            gate(0)

            def next_prep(n, first_xn):
                pe.wait_ge(gate_16, n - 2)
                prep(n, y, lambda t: pe.wait_ge(xn_made, first_xn + t))

            next_prep(PREP_F0, 13)

            def ffn(layer):
                up, loop, down = FFN_STAGES[layer]
                first = 8 * (PREP_F0, PREP_F1)[layer]

                def up_tile(st, s, hidden, per, i=None):
                    if s % 2 == 0:
                        if hidden:
                            pe.wait_ge(silu_done[layer], at(hidden, per, i))
                    elif hidden:
                        pe.wait_ge(act_done[layer], at(hidden, per, i))
                    column_tile(st, s, s % 2, i, ready=first if (hidden == 0 and s == 0) else None)

                def down_chunk(st, s, b, part8, slot, i=None):
                    if b == 0:
                        pe.wait_ge(act_lo_done[layer], at(part8 // 2 + 4, 8, i))
                    if part8 or b >= 2:
                        pe.wait_ge(y_added[layer], at(part8 + 2 * b - 2, 16, i))
                    tiles = [(ROW_BANKS[b % 2][t],
                              lambda k, t=t: act_hi[:, slot + k, t * P:(t + 1) * P],
                              lambda k, t=t: act_lo[:, slot + k, t * P:(t + 1) * P]) for t in range(TT)]
                    row_chunk(st, s, tiles, True, True, i)

                for s in range(8):
                    if s == 1:
                        pe.wait_ge(pair_lo, first + 8)
                    up_tile(up, s, s // 2, 0)
                with pe.Fori(0, 5) as i:
                    for s in range(24):
                        half, k = divmod(s, 12)
                        if k < 8:
                            up_tile(loop, s, 4 + 4 * half + k // 2, 8, i)
                        else:
                            down_chunk(loop, s, k - 8, 8 * half, 4 * half, i)
                        if layer == 0 and s == 22:
                            sum_rows(LOOP0.raw0 + LOOP0.n_raw - 1, i, LOOP0.n_raw)
                        if layer == 0 and s == 23:
                            rows_to_cols(6, i)
                for s in range(4):
                    down_chunk(down, s, s, 8 * (PARTS - 1), 0)
                gate(1 + 2 * layer)

            ffn(0)
            next_prep(PREP_FOUR, 15)

            pe.wait_ge(pair_lo, 8 * PREP_FOUR + 8)
            with pe.Fori(0, 4) as i:
                for s in range(4):
                    pe.wait_ge(u_copied, at(s + 1, 4, i))
                    column_tile(FIN, s, s % 2, i)

            def group_dft(g):
                pe.wait_ge(u_copied, 16 + 2)
                pe.wait_ge(in_dft, 16)
                if g:
                    pe.wait_ge(ab_copied, 2 * g)
                for t in range(TT):
                    for k in range(2):
                        last = nc.tensor.matmul(ps[:, 2 + t, :], uT[:, 2 * g + k, t * P:(t + 1) * P],
                                                dft_group[:, k, :], start=(k == 0), stop=(k == 1))
                    last.then_inc(ab_done, 1)

            def token_dft(f):
                g, half = divmod(f, 2)
                pe.wait_ge(ab_copied, 2 * g + 2)
                if f >= 2:
                    pe.wait_ge(f_lo, f - 1)
                for q, table in enumerate((dft_cos, dft_sin)):
                    for k in range(2):
                        col = q * 256 + half * P
                        last = nc.tensor.matmul(ps[:, 4 + f % 2, 0:256], ab[:, g % 2, k, col:col + P],
                                                table[:, k, :], start=(q == 0 and k == 0),
                                                stop=(q == 1 and k == 1))
                last.then_inc(f_done, 1)

            for g in range(FGROUPS):
                group_dft(g)
                if g:
                    token_dft(2 * g - 2)
                    token_dft(2 * g - 1)
            token_dft(KT - 2)
            token_dft(KT - 1)
            pe.wait_ge(f_lo, KT)
            for s in range(FOUT.n_w):
                b = s // 4
                if b >= 2 and s % 4 == 0:
                    pe.wait_ge(fo_copied, 2 * (b - 1))
                row_chunk(FOUT, s, latent_rows(b, 4 * (s % 4), CTX_HI, CTX_LO), s % 4 == 0, s % 4 == 3)
            gate(2)
            next_prep(PREP_F1, 17)
            ffn(1)


def shape_constants():
    inv = (np.float32(THETA) ** (-np.arange(16, dtype=np.float32) / np.float32(16))).astype(np.float32)
    tok = np.arange(SEQ)
    pos = np.stack([tok // GRID_W, tok % GRID_W]).astype(np.float32)
    row = np.arange(P)
    axis, second, freq = (row % 64) // 32, (row % 32) // 16, row % 16
    ang = (pos[axis] * inv[freq][:, None]).astype(np.float32)
    cos, sin = np.cos(ang), np.sin(ang) * np.where(second == 1, 1.0, -1.0)[:, None]
    consts = np.concatenate([np.eye(P), cos, sin], axis=1).astype(np.float32)
    n = np.arange(256)
    a = 2.0 * np.pi * ((n[:, None] * n[None, :]) % 256) / 256.0
    c, s = np.cos(a) / 16.0, np.sin(a) / 16.0
    tiles = lambda m: m.reshape(2, P, -1).transpose(1, 0, 2).reshape(P, -1)
    dft = np.concatenate([tiles(np.concatenate([c, s], axis=1)), tiles(c), tiles(-s)], axis=1)
    return consts, np.ascontiguousarray(dft.astype(np.float32))


_INS = ["x", "c", "ctx", "c_ctx", "mod_w", "mod_b", "norm_g", "ffn_w_gu", "ffn_w_down", "attn_w_qkv",
        "attn_w_o", "attn_lambda", "attn_subln_g", "four_w_in", "four_w_out"]


def kernel(**inputs):
    import concourse.bacc as _bacc
    from concourse.bass_utils import run_bass_kernel_spmd as _run

    nc = _bacc.Bacc("TRN2", target_bir_lowering=False, num_devices=1)
    arrays, args = {}, []
    named = [(name, np.ascontiguousarray(inputs[name])) for name in _INS]
    consts, dft = shape_constants()
    for name, a in named + [("consts", consts), ("dft", dft)]:
        arrays[f"in_{name}"] = a
        args.append(nc.dram_tensor(f"in_{name}", a.shape, mybir.dt.from_np(a.dtype), kind="ExternalInput").ap())
    out = nc.dram_tensor("out_0", (1, SEQ, D), F32, kind="ExternalOutput").ap()
    trunk(nc, *args, out)
    r = _run(nc, [arrays], core_ids=[0])
    return r.results[0]["out_0"]
```

```python
from contextlib import ExitStack

import numpy as np

import concourse.bass as bass
from concourse import mybir

ALU = mybir.AluOpType
ACT = mybir.ActivationFunctionType
AX_X = mybir.AxisListType.X
F32 = mybir.dt.float32
F32R = mybir.dt.float32r
BF16 = mybir.dt.bfloat16

P = 128
D = 2048
SEQ = 256
CTX = 256
KT = D // P
TT = SEQ // P
HEADS = 16
HEAD_DIM = 64
GROUPS = 4
HPG = HEADS // GROUPS
FFN = 5632
FGROUPS = 8
PART = 4 * P
PARTS = FFN // PART
EPS = 1e-6
SCALE = HEAD_DIM ** -0.5
LAMBDA_INIT = 0.8 - 0.6
GRID_W = 64
THETA = 10000.0

RING = 4
START_CHUNKS = 2 * KT
PRE = RING

C_IDENT, C_COS, C_SIN = 0, P, P + SEQ
C_END = P + 2 * SEQ
DFT_COLS = 2048

ROW_BANKS = ((2, 3), (4, 5))
COL_BANK, SUM_BANK = 6, 7


class Stage:

    def __init__(self, before, n_w, hosts=None, turns=1):
        self.raw0, self.w0, self.m0 = before
        self.n_w, self.turns = n_w, turns
        self.hosts = hosts or [0] * n_w
        assert self.hosts[0] == 0
        self.n_m = sum(self.hosts)
        self.n_raw = n_w + self.n_m
        assert self.n_raw % RING == 0 and n_w % 2 == 0
        self.after = (self.raw0 + turns * self.n_raw, self.w0 + turns * n_w, self.m0 + turns * self.n_m)

    def raw(self, j):
        if j >= self.n_w:
            return self.raw0 + self.n_raw + j - self.n_w
        return self.raw0 + j + sum(self.hosts[:j])

    def order(self):
        kt = 0
        for j in range(self.n_w):
            yield "w", j
            for _ in range(self.hosts[j]):
                yield "m", kt
                kt += 1


def spread(n_w, n_m):
    k = n_w - 2
    return [0, 0] + [(j + 1) * n_m // k - j * n_m // k for j in range(k)]


QKV_HOSTS = [0, 0, 1, 0, 1, 0, 1, 1, 1, 3, 4, 4]
QKV0 = Stage((0, 0, 0), 3 * HPG, [0, 0, 0, 0, 1, 1, 1, 1, 2, 2, 4, 4])
QKV = Stage(QKV0.after, 3 * HPG, QKV_HOSTS, GROUPS - 1)
WO = Stage(QKV.after, 16)

ATTEND = [[], ["S0"], ["T0"], ["S1", "V0"], ["S2", "S3", "T1"], ["S4", "S5", "T2", "V1", "T3"],
          ["S6", "S7", "T4", "V2", "T5", "V3"], ["V4", "T6", "V5", "T7"], ["V6", "V7"], [], [], []]
EARLY_PAIRS = 2 * (GROUPS - 1)
ATTEND_LAST = ["S0", "S1"] + [op for u in range(8) for op in
                                    ([f"S{u + 2}"] if u < 6 else []) + [f"T{u}"] +
                                    ([f"V{u - 1}"] if u else []) + ([f"O{u + 1}"] if 0 < u < 5 else [])]
ATTEND_LAST += ["V7"]
UP0 = Stage(WO.after, 8)
LOOP0 = Stage(UP0.after, 24, spread(20, KT) + [0] * 4, 5)
DOWN0 = Stage(LOOP0.after, 4)
FIN0 = Stage(DOWN0.after, 4)
FIN = Stage(FIN0.after, 4, turns=3)
FOUT_EARLY = 12
FOUT = Stage(FIN.after, 16, [0, FOUT_EARLY, 0, 0, 1, 1, 1, 1] + [0] * 8)
UP1 = Stage(FOUT.after, 8)
LOOP1 = Stage(UP1.after, 24, turns=5)
DOWN1 = Stage(LOOP1.after, 4)
LAST = DOWN1.after
FFN_STAGES = ((UP0, LOOP0, DOWN0), (UP1, LOOP1, DOWN1))

LOOP0_SUM, FOUT_SUM = 21, 8

PREP_LAT, PREP_CTX, PREP_O, PREP_F0, PREP_FOUR, PREP_F1 = range(6)


def at(base, per_turn, i):
    return base if i is None else base + per_turn * i


class Link:

    def __init__(self, eng, sem):
        self.eng, self.sem, self.n, self.more = eng, sem, 0, 0

    def __call__(self, ins):
        ins.then_inc(self.sem, 1)
        self.n += 1
        self.eng.wait_ge(self.sem, self.n + self.more)

    def turn(self, i, per_turn):
        self.start, self.per_turn, self.more = self.n, per_turn, per_turn * i

    def end(self, turns):
        assert self.n - self.start == self.per_turn, (self.n - self.start, self.per_turn)
        self.n, self.more = self.start + turns * self.per_turn, 0


def trunk(nc, x, c, ctx, c_ctx, mod_w, mod_b, norm_g, w_gu, w_down, w_qkv, w_o, lam, subln_g,
          w_in, w_out, consts, dft, out):
    x_d = x.rearrange("b (t p) d -> p (b t) d", p=P)
    ctx_d = ctx.rearrange("b (t p) d -> p (b t) d", p=P)
    out_d = out.rearrange("b (t p) d -> p (b t) d", p=P)
    mod_d = mod_w.rearrange("l d n -> (l d) n")
    gu_d = w_gu.rearrange("l d n -> (l d) n")
    down_d = w_down.rearrange("l d n -> (l d) n")
    qkv_d = w_qkv.rearrange("l d n -> (l d) n")
    wo_d = w_o.rearrange("l d n -> (l d) n")
    in_d = w_in.rearrange("l d n -> (l d) n")
    out_w_d = w_out.rearrange("l d n -> (l d) n")
    gate_scratch = nc.dram_tensor("gate_scratch", (4, D), F32, kind="Internal").ap()

    es = ExitStack()
    with es:
        def sb(name, shape, dt=F32):
            return es.enter_context(nc.sbuf_tensor(name, shape, dt))

        def sem(name):
            return es.enter_context(nc.semaphore(name))

        raw = sb("raw", [P, RING, 2048])
        w_hi = sb("w_hi", [P, 2, 2048], F32R)
        w_lo = sb("w_lo", [P, 2, 2048], F32R)
        LAT_HI, CTX_HI, LAT_LO, CTX_LO = range(4)
        hT = sb("hT", [P, KT, 4, SEQ], F32R)
        act_hi = hT[:, 0:8, CTX_HI, :]
        act_lo = hT[:, 0:8, CTX_LO, :]
        y = sb("y", [P, TT, D])
        acc = sb("acc", [P, 2048])
        htmp = acc[:, :].rearrange("p (b k t) -> p b k t", b=4, k=2)
        region = sb("region", [P, 8192])
        qT = region[:, 0:1024].rearrange("p (h t) -> p h t", h=HPG)
        kT = region[:, 1024:3072].rearrange("p (h t) -> p h t", h=HPG)
        v_sb = region[:, 3072:5120].rearrange("p (t e) -> p t e", t=4)
        probs = region[:, 5120:7168].rearrange("p (b c k) -> p b c k", b=2, c=2)
        aT = region[:, 7168:8192].rearrange("p (b k) -> p b k", b=2)
        xn0 = region[:, 0:4096].rearrange("p (t d) -> p t d", t=TT)
        small_rows = region[:, 4096:4608].rearrange("p (n k) -> p n k", n=4)
        lam_rows = region[:, 4608:4864].rearrange("p (n k) -> p n k", n=4)
        start_rows = region[:, 5120:6144].rearrange("p (n k) -> p n k", n=2)
        xs = region[:, 0:4096].rearrange("p (t d) -> p t d", t=TT)
        gate_row = region[:, 4096:6144]
        silu_g = region[:, 6144:6656].rearrange("p (b t) -> p b t", b=2)
        act_f = region[:, 6656:7168].rearrange("p (b t) -> p b t", b=2)
        uT = region[:, 4096:8192].rearrange("p (k t) -> p k t", k=KT)
        dft_sb = y[:, 0, :]
        dft_group = dft_sb[:, 0:1024].rearrange("p (k f) -> p k f", k=2)
        dft_cos = dft_sb[:, 1024:1536].rearrange("p (k t) -> p k t", k=2)
        dft_sin = dft_sb[:, 1536:2048].rearrange("p (k t) -> p k t", k=2)
        ab = y[:, 1, :].rearrange("p (b t f) -> p b t f", b=2, t=2)

        cst = sb("cst", [P, C_END])
        ident = cst[:, C_IDENT:C_IDENT + P]
        rope_cos = cst[:, C_COS:C_COS + SEQ]
        rope_sin = cst[:, C_SIN:C_SIN + SEQ]
        rope_c = sb("rope_c", [P, SEQ])
        rope_s = sb("rope_s", [P, SEQ])
        row_sb = sb("row_sb", [P, 512])
        gate16 = sb("gate16", [16, P])
        c_cols = sb("c_cols", [P, 2 * KT])
        g_cols = sb("g_cols", [P, 8 * KT])
        b_cols = sb("b_cols", [P, 12 * KT])
        p_cols = sb("p_cols", [P, 12 * KT])
        silu_c = sb("silu_c", [P, 2 * KT])
        start_w = sb("start_w", [P, KT, 32])
        start_cols = sb("start_cols", [P, 2, 2, KT])
        ab_cols = sb("ab_cols", [P, 2, KT])
        ab_ctx = sb("ab_ctx", [P, 2, KT])
        q_next = sb("q_next", [P, HPG, SEQ])
        gate_cols = sb("gate_cols", [P, KT])
        ones = sb("ones", [P, 32])
        subln = sb("subln", [P, 1])
        lam_prod = sb("lam_prod", [P, 2, HEAD_DIM])
        lam_s = sb("lam_s", [P, 4])
        stat = sb("stat", [P, 10, 16])
        s_max, s_neg, s_sum, s_rec, s_sq, s_ms, s_rstd, s_half, s_hsq, s_tot = (
            stat[:, n, :] for n in range(10))
        junk = sb("junk", [P, 512], BF16)

        ps = es.enter_context(nc.psum_tensor("ps", [P, 8, 512], F32))

        raw_landed = [sem(f"raw_landed{s}") for s in range(RING)]
        start_used = sem("start_used")
        raw_done = sem("raw_done")
        hi_ready = sem("hi_ready")
        hi_used = sem("hi_used")
        chunk_used = sem("chunk_used")
        acc_free = sem("acc_free")
        row_copied = sem("row_copied")
        cols_made = sem("cols_made")
        cols_copied = sem("cols_copied")
        in_x = sem("in_x")
        in_ctx = sem("in_ctx")
        in_small = sem("in_small")
        in_xs = sem("in_xs")
        in_dft = sem("in_dft")
        half_set = sem("half_set")
        zeros_set = sem("zeros_set")
        dve_step = sem("dve_step")
        act_step = sem("act_step")
        rope_step = sem("rope_step")
        small_T = sem("small_T")
        small_cols = sem("small_cols")
        silu_c_made = sem("silu_c_made")
        start_w_made = sem("start_w_made")
        start_hi = sem("start_hi")
        start_row = sem("start_row")
        start_T = sem("start_T")
        lam_summed = sem("lam_summed")
        lam_exp = sem("lam_exp")
        squared = sem("squared")
        ms_made = sem("ms_made")
        rstd_made = sem("rstd_made")
        xn_made = sem("xn_made")
        ab_made = sem("ab_made")
        early_T = sem("early_T")
        early_back = sem("early_back")
        pair_T = sem("pair_T")
        pair_dve = sem("pair_dve")
        pair_act = sem("pair_act")
        pair_hi = sem("pair_hi")
        pair_lo = sem("pair_lo")
        q_copied = sem("q_copied")
        k_copied = sem("k_copied")
        qk_ready = sem("qk_ready")
        v_act = sem("v_act")
        v_dve = sem("v_dve")
        scores_done = sem("scores_done")
        neg_made = sem("neg_made")
        exp_done = sem("exp_done")
        mix_done = sem("mix_done")
        mix_T = sem("mix_T")
        aT_ready = sem("aT_ready")
        pv_done = sem("pv_done")
        o_copied = sem("o_copied")
        head_ms = sem("head_ms")
        head_rstd = sem("head_rstd")
        gated = sem("gated")
        gate_T = sem("gate_T")
        gate_col = sem("gate_col")
        gate_16 = sem("gate_16")
        gate_dma = sem("gate_dma")
        res_done = sem("res_done")
        y_zero = [sem(f"y_zero{l}") for l in range(2)]
        y_added = [sem(f"y_added{l}") for l in range(2)]
        silu_done = [sem(f"silu_done{l}") for l in range(2)]
        act_done = [sem(f"act_done{l}") for l in range(2)]
        act_hi_done = [sem(f"act_hi_done{l}") for l in range(2)]
        act_lo_done = [sem(f"act_lo_done{l}") for l in range(2)]
        u_copied = sem("u_copied")
        ab_done = sem("ab_done")
        ab_copied = sem("ab_copied")
        f_done = sem("f_done")
        f_hi = sem("f_hi")
        f_lo = sem("f_lo")
        out_done = sem("out_done")

        block = es.enter_context(nc.Block())

        N_LAT, N_CTX, N_ATT, N_X0, N_FFN0, N_X1, N_FOUR, N_X2, N_FFN1 = range(9)

        @block.sync
        def _(sp):
            def load(src, n0, per_turn, i):
                sp.wait_ge(raw_done, at(n0 + 1, per_turn, i))
                s = n0 % RING
                k = src.shape[1] if len(src.shape) == 3 else 1
                dst = raw[:, s, :] if k == 1 else raw[:, s, :].rearrange("p (k c) -> p k c", k=k)
                sp.dma_start(dst, src).then_inc(raw_landed[s], 16)

            def cols(w, col):
                return w[0:D, bass.ds(col, P)].rearrange("(k p) c -> p k c", p=P)

            def rows(w, row, col):
                return w[bass.ds(row, 4 * P), bass.ds(col, 512)].rearrange("(k p) c -> p k c", p=P)

            def stage(st, source, param, i=None):
                n0 = st.raw0
                for kind, j in st.order():
                    if kind == "w":
                        src = source(j)
                    else:
                        layer = 0 if param[0] == 0 else 1
                        src = mod_d[layer * D + j * P:layer * D + (j + 1) * P, bass.ds(param[1] * D, D)]
                    load(src, n0, st.n_raw, i)
                    n0 += 1

            for n in range(START_CHUNKS):
                if n >= RING:
                    sp.wait_ge(start_used, n - RING + 1)
                par, kt = divmod(n, KT)
                sp.dma_start(raw[:, n % RING, :], mod_d[kt * P:(kt + 1) * P, par * D:(par + 1) * D])\
                    .then_inc(raw_landed[n % RING], 16)
            sp.wait_ge(start_used, START_CHUNKS)

            def qkv(g, j):
                kind, t = divmod(j, HPG)
                if kind < 2:
                    return cols(qkv_d, g * 512 + (kind * D + t * P))
                return rows(qkv_d, t * 512, g * 512 + 2 * D)

            stage(QKV0, lambda j: qkv(0, j), (0, 2))
            with sp.Fori(0, GROUPS - 1) as i:
                stage(QKV, lambda j: qkv(i + 1, j), (0, i + 3), i)

            stage(WO, lambda j: rows(wo_d, (j % 4) * 512, (j // 4) * 512), None)

            for layer in range(2):
                gu = gu_d[layer * D:(layer + 1) * D, :]
                dn = down_d[layer * FFN:(layer + 1) * FFN, :]
                up, loop, down = FFN_STAGES[layer]

                def up_src(part, j):
                    return cols(gu, part * PART + ((j // 2) * P + (j % 2) * FFN))

                def down_src(part, j):
                    return rows(dn, part * PART, j * 512)

                stage(up, lambda j: up_src(0, j), None)
                with sp.Fori(0, 5) as i:
                    def body(j):
                        half, k = divmod(j, 12)
                        if k < 8:
                            return up_src(2 * i + (1 + half), k)
                        return down_src(2 * i + half, k - 8)
                    stage(loop, body, (1, i), i)
                stage(down, lambda j: down_src(PARTS - 1, j), None)
                if layer == 0:
                    stage(FIN0, lambda j: cols(in_d, j * P), None)
                    with sp.Fori(0, 3) as i:
                        stage(FIN, lambda j: cols(in_d, i * 512 + (512 + j * P)), None, i)
                    stage(FOUT, lambda j: rows(out_w_d, (j % 4) * 512, (j // 4) * 512), (1, 5))

            for t in range(TT):
                for b in range(4):
                    sp.wait_ge(res_done, 24 + 4 * t + b + 1)
                    sp.dma_start(out_d[:, t, b * 512:(b + 1) * 512], xs[:, t, b * 512:(b + 1) * 512])\
                        .then_inc(out_done, 16)
            sp.wait_ge(out_done, 16 * TT * 4)
            sp.wait_ge(gate_dma, 16 * 8)

        @block.gpsimd
        def _(pool):
            nc.gpsimd.memset(ones[:, :], 1.0).then_inc(zeros_set, 1)
            nc.gpsimd.memset(start_w[:, :, :], 0.0).then_inc(zeros_set, 1)
            nc.gpsimd.memset(s_half, -0.5).then_inc(half_set, 1)
            pool.wait_ge(half_set, 1)

            def power(n):
                for t in range(TT):
                    o = 2 * (n % 2) + t
                    pool.wait_ge(ms_made, 2 * n + t + 1)
                    nc.gpsimd.tensor_tensor(s_rstd[:, o:o + 1], s_ms[:, o:o + 1], s_half[:, 0:1], ALU.pow)\
                        .then_inc(rstd_made, 1)

            def gate(n):
                pool.wait_ge(gate_16, n + 1)
                pool.dma_start(gate_scratch[n, :].rearrange("(k c) -> k c", c=P), gate16[:, :])\
                    .then_inc(gate_dma, 16)
                pool.wait_ge(gate_dma, 32 * n + 16)
                pool.dma_start(gate_row, gate_scratch[n, :].partition_broadcast(P)).then_inc(gate_dma, 16)

            power(N_LAT)
            power(N_CTX)

            def head_power(i):
                pool.wait_ge(head_ms, at(1, 1, i))
                nc.gpsimd.tensor_tensor(s_rstd[:, 8:16], s_ms[:, 8:16], s_half[:, 0:8], ALU.pow)\
                    .then_inc(head_rstd, 1)

            with pool.Fori(0, GROUPS - 1) as i:
                head_power(i)
            head_power(GROUPS - 1)
            pool.wait_ge(pv_done, 8 * GROUPS)
            pool.dma_start(xs, x_d).then_inc(in_xs, 16)
            gate(0)
            power(N_ATT)
            power(N_X0)
            for layer in range(2):
                pool.wait_ge(pair_T, 8 * ((PREP_F0, PREP_F1)[layer] - 2) + 8)
                for n in range(4):
                    nc.gpsimd.memset(y[:, n // 2, (n % 2) * 1024:(n % 2 + 1) * 1024], 0.0)\
                        .then_inc(y_zero[layer], 1)
                gate(1 + 2 * layer)
                power((N_FFN0, N_FFN1)[layer])
                if layer == 0:
                    power(N_X1)
                    pool.wait_ge(pair_T, 8 * (PREP_FOUR - 2) + 8)
                    pool.dma_start(dft_sb, dft).then_inc(in_dft, 16)
                    pool.wait_ge(ab_done, 16)
                    gate(2)
                    power(N_FOUR)
                    power(N_X2)

        @block.scalar
        def _(act):
            link = Link(act, act_step)

            def high(st, j, i=None):
                n, m = st.raw(j), st.w0 + j
                act.wait_ge(raw_landed[n % RING],
                            at(16 * ((START_CHUNKS + n) // RING + 1), 16 * st.n_raw // RING, i))
                if m >= 2:
                    act.wait_ge(raw_done, at(st.raw(j - 2) + PRE + 1, st.n_raw, i))
                    act.wait_ge(hi_used, at(m - 1, st.n_w, i))
                nc.scalar.activation(w_hi[:, m % 2, :], raw[:, n % RING, :], ACT.Copy).then_inc(hi_ready, 1)

            def used(st, j, i=None):
                act.wait_ge(chunk_used, at(st.w0 + j + 1, st.n_w, i))

            def prep(n, hi):
                def odd(pr):
                    act.wait_ge(pair_T, 8 * (n - 2) + pr + 1)
                    act.wait_ge(ab_made, n)
                    act.wait_ge(pair_lo, 8 * n + max(pr - 3, 0))
                    for k in range(2):
                        kt = 2 * pr + k
                        nc.scalar.activation(htmp[:, pr % 4, k, :], ps[:, pr, k * 256:(k + 1) * 256],
                                             ACT.Identity, bias=ab_cols[:, 1, kt:kt + 1],
                                             scale=ab_cols[:, 0, kt:kt + 1]).then_inc(pair_act, 1)

                def high_pair(pr):
                    if pr % 2:
                        act.wait_ge(pair_act, 8 * (n - 3) + pr + 1)
                    else:
                        act.wait_ge(pair_dve, 8 * (n - 3) + pr + 2)
                    nc.scalar.activation(hT[:, 2 * pr:2 * pr + 2, hi, :], htmp[:, pr % 4, :, :], ACT.Copy)\
                        .then_inc(pair_hi, 1)

                for pr in range(0, 8, 2):
                    odd(pr + 1)
                    high_pair(pr)
                    high_pair(pr + 1)

            def square(n, t, b, src):
                col = 8 * (n % 2) + 4 * t + b
                if b or t or n:
                    self_count = squares_done[0]
                    act.wait_ge(squared, self_count)
                squares_done[0] += 1
                nc.scalar.activation(junk[:, :], src, ACT.Square, accum_out=s_sq[:, col:col + 1])\
                    .then_inc(squared, 1)

            squares_done = [0]

            def blocks(x_):
                return [(t, b, x_[:, t, b * 512:(b + 1) * 512]) for t in range(TT) for b in range(4)]

            def row_copy(p, i=None):
                act.wait_ge(acc_free, at(p + 2, 1, i))
                nc.scalar.activation(row_sb[:, :], ps[:, SUM_BANK, :], ACT.Copy).then_inc(row_copied, 1)

            def gate(n):
                act.wait_ge(gate_T, n + 1)
                if n:
                    act.wait_ge(gate_dma, 32 * n)
                nc.scalar.activation(gate16[:, :], ps[0:16, SUM_BANK, 0:P], ACT.Copy).then_inc(gate_16, 1)

            act.dma_start(small_rows[0:16, 0, :], c.rearrange("b (k c) -> (b k) c", c=P)).then_inc(in_small, 16)
            act.dma_start(small_rows[16:32, 0, :], c_ctx.rearrange("(k c) -> k c", c=P)).then_inc(in_small, 16)
            act.dma_start(small_rows[:, 1, :], norm_g.rearrange("l n (k c) -> (l n k) c", c=P))\
                .then_inc(in_small, 16)
            for layer in range(2):
                act.dma_start(small_rows[0:96, 2 + layer, :], mod_b[layer, :].rearrange("(k c) -> k c", c=P))\
                    .then_inc(in_small, 16)
            act.dma_start(cst[:, :], consts).then_inc(in_small, 16)
            act.dma_start(subln[:, :], subln_g.rearrange("l e -> e l")).then_inc(in_small, 16)
            act.dma_start(lam_rows[:, :, :], lam.rearrange("l n d -> (l n) d").partition_broadcast(P))\
                .then_inc(in_small, 16)
            act.dma_start(xn0, x_d).then_inc(in_x, 16)
            act.dma_start(y[:, :, :], ctx_d).then_inc(in_ctx, 16)

            act.wait_ge(small_cols, 3)
            nc.scalar.activation(silu_c[:, :], c_cols[:, :], ACT.Silu).then_inc(silu_c_made, 1)
            act.wait_ge(in_x, 16)
            for t, b, src in blocks(xn0):
                square(N_LAT, t, b, src)
            act.wait_ge(in_ctx, 16)
            for t, b, src in blocks(y):
                square(N_CTX, t, b, src)
            act.wait_ge(lam_summed, 1)
            nc.scalar.activation(lam_s[:, 2:4], lam_s[:, 0:2], ACT.Exp).then_inc(lam_exp, 1)
            for par in range(2):
                act.wait_ge(start_used, KT * (par + 1))
                nc.scalar.activation(start_rows[:, par, :], ps[:, par, :], ACT.Copy).then_inc(start_row, 1)

            def start_high(v, pr, src, ab_):
                act.wait_ge(ab_made, v + 1)
                act.wait_ge(early_back, 8 * v + pr + 1)
                for k in range(2):
                    kt = 2 * pr + k
                    nc.scalar.activation(hT[:, kt, LAT_HI + v, :], src[:, k, pr * 256:(pr + 1) * 256],
                                         ACT.Identity, bias=ab_[:, 1, kt:kt + 1], scale=ab_[:, 0, kt:kt + 1])\
                        .then_inc(start_hi, 1)

            high(QKV0, 0)
            for pr in range(8):
                start_high(0, pr, xn0, ab_cols)
            high(QKV0, 1)

            def attend(ops, i):
                for op in [o for o in ops if o[0] != "S"] + [o for o in ops if o[0] == "S"]:
                    u = int(op[1:])
                    if op[0] == "T":
                        act.wait_ge(mix_T, at(u + 1, 8, i))
                        if u >= 2:
                            act.wait_ge(pv_done, at(u - 1, 8, i))
                        nc.scalar.activation(aT[:, u % 2, :], ps[:, COL_BANK, :], ACT.Copy).then_inc(aT_ready, 1)
                    elif op[0] == "V":
                        h, t = divmod(u, 2)
                        act.wait_ge(pv_done, at(u + 1, 8, i))
                        nc.scalar.activation(y[:, t, bass.ds(i * 512 + h * P, P)],
                                             ps[:, SUM_BANK, (u % 4) * P:(u % 4 + 1) * P], ACT.Copy)\
                            .then_inc(o_copied, 1)
                    else:
                        act.wait_ge(neg_made, at(u + 1, 8, i))
                        if u >= 2:
                            act.wait_ge(mix_T, at(u - 1, 8, i))
                        for h in range(2):
                            bank = 2 + 2 * (u % 2) + h
                            nc.scalar.activation(probs[:, u % 2, h, :], ps[:, bank, :], ACT.Exp,
                                                 bias=s_neg[:, 2 * u + h:2 * u + h + 1], scale=SCALE,
                                                 accum_out=s_sum[:, 2 * u + h:2 * u + h + 1])\
                                .then_inc(exp_done, 1)

            def qkv_step(st, s, g, i=None):
                high(st, s + 2, i)
                used(st, s, i)
                if s < 4:
                    nc.scalar.activation(q_next[:, s, :], ps[:, s % 2, 0:256], ACT.Copy).then_inc(q_copied, 1)
                elif s < 8:
                    nc.scalar.activation(kT[:, s - 4, :], ps[:, s % 2, :], ACT.Copy).then_inc(k_copied, 1)
                if s == 11:
                    for t in range(2):
                        nc.scalar.activation(v_sb[:, t, :], ps[:, 2 + t, :], ACT.Copy).then_inc(v_act, 1)
                    row_copy(0, g)

            for s in range(QKV0.n_w):
                qkv_step(QKV0, s, 0)
                if s < 2:
                    for pr in range(4 * s, 4 * s + 4):
                        start_high(1, pr, y, ab_ctx)
            with act.Fori(0, GROUPS - 1) as i:
                for s in range(QKV.n_w):
                    attend(ATTEND[s], i)
                    qkv_step(QKV, s, i + 1, i)
            def o_high(pr):
                act.wait_ge(pair_T, pr + 1)
                nc.scalar.activation(hT[:, 2 * pr:2 * pr + 2, LAT_HI, :],
                                     ps[:, pr % 2, :].rearrange("p (k t) -> p k t", k=2),
                                     ACT.Copy, scale=subln[:, 0:1]).then_inc(pair_hi, 1)

            order = ["S0"] + [op for u in range(8) for op in
                              ([f"S{u + 1}"] if u < 7 else []) + ([f"O{u}"] if u < EARLY_PAIRS else []) +
                              [f"T{u}"] + ([f"V{u - 1}"] if u else [])]
            for op in order + ["V7"]:
                if op[0] == "O":
                    o_high(int(op[1:]))
                else:
                    attend([op], GROUPS - 1)

            for s in range(WO.n_w):
                high(WO, s + 2)
                if s == 1:
                    for pr in range(EARLY_PAIRS, 8):
                        o_high(pr)
                if s % 4 == 3:
                    used(WO, s)
                    for t in range(2):
                        square(N_ATT, t, s // 4, ps[:, ROW_BANKS[(s // 4) % 2][t], :])
                if s == 0:
                    gate(0)

            def ffn(layer):
                up, loop, down = FFN_STAGES[layer]

                def up_step(st, s, hidden, per, slot, i=None):
                    if s % 2 == 0:
                        used(st, s, i)
                        nc.scalar.activation(silu_g[:, hidden % 2, :], ps[:, 0, 0:256], ACT.Silu)\
                            .then_inc(silu_done[layer], 1)
                    else:
                        act.wait_ge(act_done[layer], at(hidden + 1, per, i))
                        nc.scalar.activation(act_hi[:, slot, :], act_f[:, hidden % 2, :], ACT.Copy)\
                            .then_inc(act_hi_done[layer], 1)

                for s in range(8):
                    high(up, s + 2)
                    up_step(up, s, s // 2, 0, s // 2)
                    if s == 0:
                        gate(1 + 2 * layer)
                with act.Fori(0, 5) as i:
                    for s in range(24):
                        high(loop, s + 2, i)
                        half, k = divmod(s, 12)
                        if k < 8:
                            up_step(loop, s, 4 + 4 * half + k // 2, 8, 4 * (1 - half) + k // 2, i)
                        if layer == 0 and s == LOOP0_SUM:
                            row_copy(4, i)
                for s in range(4):
                    if layer == 0 or s < 2:
                        high(down, s + 2)
                    for t in range(TT):
                        act.wait_ge(y_added[layer], 8 * (PARTS - 1) + 2 * s + t + 1)
                        square((N_FFN0, N_FFN1)[layer], t, s, y[:, t, s * 512:(s + 1) * 512])

            def squares_x(n, r):
                for t, b, src in blocks(xs):
                    act.wait_ge(res_done, 8 * r + 4 * t + b + 1)
                    square(n, t, b, src)

            squares_x(N_X0, 0)
            prep(PREP_F0, LAT_HI)
            ffn(0)
            squares_x(N_X1, 1)
            prep(PREP_FOUR, LAT_HI)

            def fin_step(st, s, tile, i=None):
                high(st, s + 2, i)
                used(st, s, i)
                nc.scalar.activation(uT[:, bass.ds(tile, 1), :], ps[:, s % 2, 0:256].unsqueeze(1), ACT.Copy)\
                    .then_inc(u_copied, 1)

            for s in range(4):
                fin_step(FIN0, s, s)
            with act.Fori(0, 3) as i:
                for s in range(4):
                    fin_step(FIN, s, i * 4 + (4 + s), i)
            for f in range(KT):
                act.wait_ge(f_done, f + 1)
                nc.scalar.activation(hT[:, f, CTX_HI, :], ps[:, 4 + f % 2, 0:256], ACT.Copy).then_inc(f_hi, 1)
            gate(2)
            for s in range(FOUT.n_w):
                high(FOUT, s + 2)
                if s % 4 == 3:
                    used(FOUT, s)
                    for t in range(2):
                        square(N_FOUR, t, s // 4, ps[:, ROW_BANKS[(s // 4) % 2][t], :])
                if s == FOUT_SUM:
                    row_copy(9)
            squares_x(N_X2, 2)
            prep(PREP_F1, LAT_HI)
            ffn(1)

        @block.vector
        def _(dve):
            link = Link(dve, dve_step)

            def low(st, j, i=None):
                n, m = st.raw(j), st.w0 + j
                dve.wait_ge(hi_ready, at(m + 1, st.n_w, i))
                if m >= 2:
                    dve.wait_ge(chunk_used, at(m - 1, st.n_w, i))
                nc.vector.tensor_tensor(w_lo[:, m % 2, :], raw[:, n % RING, :],
                                        w_hi[:, m % 2, :].bitcast(F32), ALU.subtract).then_inc(raw_done, 1)
                if j < st.n_w and not (st is FOUT and j == 1):
                    fold(st, j, range(st.hosts[j]), i)

            def fold(st, j, which, i=None):
                for q in which:
                    n = st.raw(j) + 1 + q
                    kt = sum(st.hosts[:j]) + q
                    dve.wait_ge(raw_landed[n % RING],
                                at(16 * ((START_CHUNKS + n) // RING + 1), 16 * st.n_raw // RING, i))
                    if kt == 0:
                        if st is QKV0:
                            dve.wait_ge(pair_lo, 16)
                        dve.wait_ge(acc_free, at(st.m0 // KT + 1, 1, i))
                        nc.vector.tensor_scalar(acc[:, :], raw[:, n % RING, :], silu_c[:, 0:1], None,
                                                ALU.mult).then_inc(raw_done, 1)
                    else:
                        dve.wait_ge(raw_done, at(n + PRE, st.n_raw, i))
                        nc.vector.scalar_tensor_tensor(out=acc[:, :], in0=raw[:, n % RING, :],
                                                       scalar=silu_c[:, kt:kt + 1], in1=acc[:, :],
                                                       op0=ALU.mult, op1=ALU.add).then_inc(raw_done, 1)

            def used(st, j, i=None):
                dve.wait_ge(chunk_used, at(st.w0 + j + 1, st.n_w, i))

            def prep(n, lo, hi):
                def even(pr):
                    dve.wait_ge(pair_T, 8 * (n - 2) + pr + 1)
                    if pr >= 4:
                        dve.wait_ge(pair_lo, 8 * n + pr - 3)
                    for k in range(2):
                        kt = 2 * pr + k
                        nc.vector.tensor_scalar(htmp[:, pr % 4, k, :], ps[:, pr, k * 256:(k + 1) * 256],
                                                ab_cols[:, 0, kt:kt + 1], ab_cols[:, 1, kt:kt + 1],
                                                ALU.mult, ALU.add).then_inc(pair_dve, 1)

                def low_pair(pr):
                    dve.wait_ge(pair_hi, 8 * (n - 2) + pr + 1)
                    nc.vector.tensor_tensor(hT[:, 2 * pr:2 * pr + 2, lo, :], htmp[:, pr % 4, :, :],
                                            hT[:, 2 * pr:2 * pr + 2, hi, :].bitcast(F32), ALU.subtract)\
                        .then_inc(pair_lo, 1)

                even(0)
                for pr in range(0, 8, 2):
                    if pr + 2 < 8:
                        even(pr + 2)
                    low_pair(pr)
                    low_pair(pr + 1)

            def mean_square(n, t, ready):
                dve.wait_ge(squared, 8 * n + ready)
                o = 2 * (n % 2) + t
                link(nc.vector.tensor_reduce(s_tot[:, o:o + 1], s_sq[:, 4 * o:4 * o + 4], AX_X, ALU.add))
                nc.vector.tensor_scalar(s_ms[:, o:o + 1], s_tot[:, o:o + 1], 1.0 / D, EPS, ALU.mult, ALU.add)\
                    .then_inc(ms_made, 1)

            def rstd(n, t):
                dve.wait_ge(rstd_made, 2 * n + t + 1)
                o = 2 * (n % 2) + t
                return s_rstd[:, o:o + 1]

            def normalise(n, t, dst, src):
                scale = rstd(n, t)
                for half in range(2):
                    cols = slice(half * D // 2, (half + 1) * D // 2)
                    nc.vector.tensor_scalar(dst[:, t, cols], src[:, t, cols], scale, None, ALU.mult)\
                        .then_inc(xn_made, 1)

            def cols_of(layer, par):
                return slice((6 * layer + par) * KT, (6 * layer + par + 1) * KT)

            def modulation(layer, shift, scale, norm):
                link(nc.vector.scalar_tensor_tensor(
                    out=ab_cols[:, 0, :], in0=p_cols[:, cols_of(layer, scale)], scalar=1.0,
                    in1=b_cols[:, cols_of(layer, scale)], op0=ALU.add, op1=ALU.add))
                g = g_cols[:, (4 * layer + norm) * KT:(4 * layer + norm + 1) * KT]
                link(nc.vector.tensor_tensor(ab_cols[:, 0, :], ab_cols[:, 0, :], g, ALU.mult))
                nc.vector.tensor_tensor(ab_cols[:, 1, :], p_cols[:, cols_of(layer, shift)],
                                        b_cols[:, cols_of(layer, shift)], ALU.add).then_inc(ab_made, 1)

            def gate(n, layer, par, norm):
                if n:
                    dve.wait_ge(gate_T, n)
                link(nc.vector.tensor_tensor(gate_cols[:, :], p_cols[:, cols_of(layer, par)],
                                             b_cols[:, cols_of(layer, par)], ALU.add))
                g = g_cols[:, (4 * layer + norm) * KT:(4 * layer + norm + 1) * KT]
                nc.vector.tensor_tensor(gate_cols[:, :], gate_cols[:, :], g, ALU.mult).then_inc(gate_col, 1)

            def gate_block(r, norm, t, b, src):
                dve.wait_ge(squared, 8 * norm + 2 * b + t + 1)
                dve.wait_ge(gate_dma, 32 * r + 32)
                nc.vector.tensor_tensor(y[:, t, b * 512:(b + 1) * 512], src,
                                        gate_row[:, b * 512:(b + 1) * 512], ALU.mult).then_inc(gated, 1)

            def residual(r, norm, next_norm):
                mean_square(norm, 0, 7)
                mean_square(norm, 1, 8)
                dve.wait_ge(gated, 8 * r + 8)
                if r == 0:
                    dve.wait_ge(in_xs, 16)
                for t in range(TT):
                    scale = rstd(norm, t)
                    for b in range(4):
                        blk = xs[:, t, b * 512:(b + 1) * 512]
                        nc.vector.scalar_tensor_tensor(out=blk, in0=y[:, t, b * 512:(b + 1) * 512],
                                                       scalar=scale, in1=blk, op0=ALU.mult, op1=ALU.add)\
                            .then_inc(res_done, 1)
                        if next_norm is not None and t == 1 and b == 1:
                            mean_square(next_norm, 0, 4)
                if next_norm is not None:
                    normalise(next_norm, 0, y, xs)
                    mean_square(next_norm, 1, 8)
                    normalise(next_norm, 1, y, xs)

            def param_cols(idx, count, i=None):
                dve.wait_ge(cols_made, at(count, 1, i))
                dst = p_cols[:, bass.ds(idx * KT, KT)] if i is not None else p_cols[:, idx * KT:(idx + 1) * KT]
                nc.vector.tensor_copy(dst.rearrange("p (b r) -> p r b", b=4),
                                      ps[:, COL_BANK, :].rearrange("p (r b z) -> p r b z", r=4, b=4)[:, :, :, 0])\
                    .then_inc(cols_copied, 1)

            for n in range(PRE):
                nc.vector.memset(gate_cols[:, n:n + 1], 0.0).then_inc(raw_done, 1)
            dve.wait_ge(small_T, 4)
            nc.vector.tensor_copy(c_cols[:, :], ps[:, 2, 0:32]).then_inc(small_cols, 1)
            nc.vector.tensor_copy(g_cols[:, :], ps[:, 3, 0:128]).then_inc(small_cols, 1)
            nc.vector.tensor_copy(b_cols[:, :].rearrange("p (l k) -> p l k", l=2),
                                  ps[:, 4:6, 0:96]).then_inc(small_cols, 1)
            dve.wait_ge(silu_c_made, 1)
            dve.wait_ge(zeros_set, 2)
            nc.vector.tensor_copy(start_w[:, :, 0:2], silu_c[:, :].rearrange("p (v k) -> p k v", v=2))\
                .then_inc(start_w_made, 1)
            link(nc.vector.tensor_tensor(lam_prod[:, :, :], lam_rows[:, 0::2, :], lam_rows[:, 1::2, :], ALU.mult))
            nc.vector.tensor_reduce(lam_s[:, 0:2], lam_prod[:, :, :], AX_X, ALU.add).then_inc(lam_summed, 1)
            link(nc.vector.tensor_scalar(subln[:, :], subln[:, :], 1.0 - LAMBDA_INIT, None, ALU.mult))
            for n, x_ in ((N_LAT, xn0), (N_CTX, y)):
                mean_square(n, 0, 4)
                mean_square(n, 1, 8)
                for t in range(TT):
                    normalise(n, t, x_, x_)
            dve.wait_ge(lam_exp, 1)
            link(nc.vector.tensor_scalar(lam_s[:, 0:1], lam_s[:, 3:4], -LAMBDA_INIT, None, ALU.add))
            link(nc.vector.tensor_tensor(lam_s[:, 0:1], lam_s[:, 0:1], lam_s[:, 2:3], ALU.subtract))
            neg_lam = lam_s[:, 0:1]
            for v, x_ in enumerate((xn0, y)):
                for pr in range(8):
                    dve.wait_ge(early_T, 8 * v + pr + 1)
                    nc.vector.tensor_copy(x_[:, :, pr * 256:(pr + 1) * 256],
                                          ps[:, 2 + pr % 4, :].rearrange("p (k t) -> p k t", k=2))\
                        .then_inc(early_back, 1)
            dve.wait_ge(start_T, 1)
            for v, ab_ in enumerate((ab_cols, ab_ctx)):
                for par in range(2):
                    link(nc.vector.tensor_copy(
                        start_cols[:, par, v, :].rearrange("p (b r) -> p r b", b=4),
                        ps[:, 6 + par, :].rearrange("p (r b z) -> p r b z", r=4, b=4)[:, :, :, v]))
                link(nc.vector.scalar_tensor_tensor(
                    out=ab_[:, 0, :], in0=start_cols[:, 1, v, :], scalar=1.0,
                    in1=b_cols[:, cols_of(0, 1)], op0=ALU.add, op1=ALU.add))
                link(nc.vector.tensor_tensor(ab_[:, 0, :], ab_[:, 0, :], g_cols[:, 0:KT], ALU.mult))
                nc.vector.tensor_tensor(ab_[:, 1, :], start_cols[:, 0, v, :], b_cols[:, cols_of(0, 0)],
                                        ALU.add).then_inc(ab_made, 1)
                dve.wait_ge(ab_made, v + 1)

            def start_low(v, pr, x_, ab_):
                if v or pr >= 4:
                    dve.wait_ge(pair_lo, 8 * v + pr - 3)
                for k in range(2):
                    kt = 2 * pr + k
                    link(nc.vector.tensor_scalar(htmp[:, pr % 4, k, :], x_[:, k, pr * 256:(pr + 1) * 256],
                                                 ab_[:, 0, kt:kt + 1], ab_[:, 1, kt:kt + 1],
                                                 ALU.mult, ALU.add))
                dve.wait_ge(start_hi, 16 * v + 2 * pr + 2)
                nc.vector.tensor_tensor(hT[:, 2 * pr:2 * pr + 2, LAT_LO + v, :], htmp[:, pr % 4, :, :],
                                        hT[:, 2 * pr:2 * pr + 2, LAT_HI + v, :].bitcast(F32), ALU.subtract)\
                    .then_inc(pair_lo, 1)

            for pr in range(8):
                start_low(0, pr, xn0, ab_cols)
                if pr == 1:
                    low(QKV0, 0)
            low(QKV0, 1)

            SWAP = [(r + 16) % 32 for r in range(32)]

            def rope(dst, src, tile, g):
                if tile:
                    dve.wait_ge(qk_ready, at(tile, 8, g))
                nc.vector.tensor_tensor(rope_c[:, :], src, rope_cos, ALU.mult).then_inc(rope_step, 1)
                link(nc.vector.stream_shuffle(rope_s[:, :], src, SWAP))
                nc.vector.tensor_tensor(rope_s[:, :], rope_s[:, :], rope_sin, ALU.mult).then_inc(rope_step, 1)
                dve.wait_ge(rope_step, at(2 * tile + 2, 16, g))
                nc.vector.tensor_tensor(dst, rope_c[:, :], rope_s[:, :], ALU.add).then_inc(qk_ready, 1)

            def maxima(u, i):
                dve.wait_ge(scores_done, at(u + 1, 8, i))
                bank = 2 + 2 * (u % 2)
                link(nc.vector.tensor_reduce(s_max[:, 2 * u:2 * u + 2], ps[:, bank:bank + 2, :], AX_X, ALU.max))
                nc.vector.tensor_scalar(s_neg[:, 2 * u:2 * u + 2], s_max[:, 2 * u:2 * u + 2], -SCALE, None,
                                        ALU.mult).then_inc(neg_made, 1)

            def mix(u, i):
                dve.wait_ge(exp_done, at(2 * u + 2, 16, i))
                link(nc.vector.reciprocal(s_rec[:, 2 * u:2 * u + 2], s_sum[:, 2 * u:2 * u + 2]))
                e0, e1 = probs[:, u % 2, 0, :], probs[:, u % 2, 1, :]
                link(nc.vector.tensor_scalar(e1, e1, s_rec[:, 2 * u + 1:2 * u + 2], neg_lam, ALU.mult, ALU.mult))
                nc.vector.scalar_tensor_tensor(out=e0, in0=e0, scalar=s_rec[:, 2 * u:2 * u + 1], in1=e1,
                                               op0=ALU.mult, op1=ALU.add).then_inc(mix_done, 1)

            def head_squares(i):
                dve.wait_ge(o_copied, at(8, 8, i))
                sq = probs[:, 0, :, :]
                o = y[:, :, bass.ds(i * 512, 512)]
                link(nc.vector.tensor_tensor(sq, o, o, ALU.mult))
                link(nc.vector.tensor_reduce(s_hsq[:, 0:8], sq.rearrange("p t (h e) -> p t h e", h=4), AX_X, ALU.add))
                nc.vector.tensor_scalar(s_ms[:, 8:16], s_hsq[:, 0:8], 1.0 / P, EPS, ALU.mult, ALU.add)\
                    .then_inc(head_ms, 1)

            def head_norm(i):
                dve.wait_ge(head_rstd, at(1, 1, i))
                for t in range(TT):
                    o = y[:, t, bass.ds(i * 512, 512)].rearrange("p (h e) -> p h e", h=4)
                    r = s_rstd[:, 8 + 4 * t:12 + 4 * t].unsqueeze(2).to_broadcast([P, 4, P])
                    nc.vector.tensor_tensor(o, o, r, ALU.mult).then_inc(xn_made, 1)

            def attend(ops, i):
                units = [int(op[1:]) for op in ops if op[0] == "S"]
                for u in units:
                    maxima(u, i)
                for u in units:
                    mix(u, i)

            def qkv_step(st, s, g, i=None):
                if 5 <= s < 9:
                    dve.wait_ge(k_copied, at(s - 4, 4, g))
                    rope(kT[:, s - 5, 0:256], kT[:, s - 5, 0:256], s - 5, g)
                if s >= 8:
                    dve.wait_ge(q_copied, at(s - 7, 4, g))
                    rope(qT[:, s - 8, :], q_next[:, s - 8, :], s - 4, g)
                if s == 11:
                    used(st, 11, i)
                    for t in range(2, 4):
                        nc.vector.tensor_copy(v_sb[:, t, :], ps[:, 2 + t, :]).then_inc(v_dve, 1)
                low(st, s + 2, i)

            for s in range(QKV0.n_w):
                qkv_step(QKV0, s, 0)
                if s < 2:
                    for pr in range(4 * s, 4 * s + 4):
                        start_low(1, pr, y, ab_ctx)
            with dve.Fori(0, GROUPS - 1) as i:
                link.turn(i, 8 * 1 + 8 * 3 + 2)
                for s in range(QKV.n_w):
                    if s == 1:
                        param_cols(i + 2, 1, i)
                    attend(ATTEND[s], i)
                    if s == 9:
                        head_squares(i)
                    if s == 11:
                        head_norm(i)
                    qkv_step(QKV, s, i + 1, i)
            link.end(GROUPS - 1)
            param_cols(5, 4)
            last = GROUPS - 1
            maxima(0, last)
            maxima(1, last)

            def o_low(pr):
                dve.wait_ge(pair_hi, pr + 1)
                nc.vector.scalar_tensor_tensor(out=hT[:, 2 * pr:2 * pr + 2, LAT_LO, :],
                                               in0=ps[:, pr % 2, :].rearrange("p (k t) -> p k t", k=2),
                                               scalar=subln[:, 0:1],
                                               in1=hT[:, 2 * pr:2 * pr + 2, LAT_HI, :].bitcast(F32),
                                               op0=ALU.mult, op1=ALU.subtract).then_inc(pair_lo, 1)

            for u in range(8):
                mix(u, last)
                if u + 2 < 8:
                    maxima(u + 2, last)
                if u < EARLY_PAIRS:
                    o_low(u)
            gate(0, 0, 2, 1)
            head_squares(last)

            for s in range(WO.n_w):
                if s < WO.n_w - 1:
                    low(WO, s + 2)
                if s == 0:
                    head_norm(last)
                if s == 1:
                    for pr in range(EARLY_PAIRS, 8):
                        o_low(pr)
                if s % 4 == 3:
                    for t in range(TT):
                        gate_block(0, N_ATT, t, s // 4, ps[:, ROW_BANKS[(s // 4) % 2][t], :])

            def next_input(r, norm, next_norm, prep_n, st, layer, shift, scale, norm_g_):
                modulation(layer, shift, scale, norm_g_)
                residual(r, norm, next_norm)
                dve.wait_ge(ab_made, prep_n)
                prep(prep_n, LAT_LO, LAT_HI)
                low(st, st.n_w + 1)

            next_input(0, N_ATT, N_X0, PREP_F0, WO, 0, 3, 4, 2)

            def ffn(layer):
                up, loop, down = FFN_STAGES[layer]
                gate(1 + 2 * layer, layer, 5, 3)

                def act_mul(st, s, hidden, per, i=None):
                    used(st, s, i)
                    dve.wait_ge(silu_done[layer], at(hidden + 1, per, i))
                    if hidden >= 2:
                        dve.wait_ge(act_lo_done[layer], at(hidden - 1, per, i))
                    nc.vector.tensor_tensor(act_f[:, hidden % 2, :], ps[:, 1, 0:256], silu_g[:, hidden % 2, :],
                                            ALU.mult).then_inc(act_done[layer], 1)

                def act_low(hidden, per, slot, i=None):
                    dve.wait_ge(act_hi_done[layer], at(hidden + 1, per, i))
                    nc.vector.tensor_tensor(act_lo[:, slot, :], act_f[:, hidden % 2, :],
                                            act_hi[:, slot, :].bitcast(F32), ALU.subtract)\
                        .then_inc(act_lo_done[layer], 1)

                def add(st, s, b, part8, i=None):
                    used(st, s, i)
                    for t in range(TT):
                        done = part8 + 2 * b + t
                        if i is not None or done:
                            if part8 or i is None:
                                dve.wait_ge(y_added[layer], at(done, 16, i))
                        blk = y[:, t, b * 512:(b + 1) * 512]
                        nc.vector.tensor_tensor(blk, blk, ps[:, ROW_BANKS[b % 2][t], :], ALU.add)\
                            .then_inc(y_added[layer], 1)

                for s in range(8):
                    if s % 2:
                        act_mul(up, s, s // 2, 0)
                    low(up, s + 2)
                    if s % 2:
                        act_low(s // 2, 0, s // 2)
                dve.wait_ge(y_zero[layer], 4)
                with dve.Fori(0, 5) as i:
                    for s in range(24):
                        half, k = divmod(s, 12)
                        hidden = 4 + 4 * half + k // 2
                        if k < 8 and k % 2:
                            act_mul(loop, s, hidden, 8, i)
                        if k >= 8:
                            add(loop, s, k - 8, 8 * half, i)
                        low(loop, s + 2, i)
                        if k < 8 and k % 2:
                            act_low(hidden, 8, 4 * (1 - half) + k // 2, i)
                    if layer == 0:
                        param_cols(i + 6, 5, i)
                def gate_y(s):
                    for t in range(TT):
                        gate_block(1 + 2 * layer, (N_FFN0, N_FFN1)[layer], t, s,
                                   y[:, t, s * 512:(s + 1) * 512])

                for s in range(4):
                    add(down, s, s, 8 * (PARTS - 1))
                    if s < (3 if layer == 0 else 2):
                        low(down, s + 2)
                    if s:
                        gate_y(s - 1)
                gate_y(3)

            ffn(0)
            next_input(1, N_FFN0, N_X1, PREP_FOUR, DOWN0, 1, 0, 1, 0)

            for s in range(4):
                low(FIN0, s + 2)
            with dve.Fori(0, 3) as i:
                for s in range(4):
                    low(FIN, s + 2, i)
            gate(2, 1, 2, 1)

            def f_low(f):
                dve.wait_ge(f_hi, f + 1)
                nc.vector.tensor_tensor(hT[:, f, CTX_LO, :], ps[:, 4 + f % 2, 0:256],
                                        hT[:, f, CTX_HI, :].bitcast(F32), ALU.subtract).then_inc(f_lo, 1)

            for g in range(FGROUPS):
                for t in range(TT):
                    dve.wait_ge(ab_done, 2 * g + t + 1)
                    nc.vector.tensor_copy(ab[:, g % 2, t, :], ps[:, 2 + t, :]).then_inc(ab_copied, 1)
                if g:
                    f_low(2 * g - 2)
                    f_low(2 * g - 1)
                fold(FOUT, 1, range(g * FOUT_EARLY // FGROUPS, (g + 1) * FOUT_EARLY // FGROUPS))
            f_low(KT - 2)
            f_low(KT - 1)
            for s in range(FOUT.n_w):
                if s == FOUT_SUM + 2:
                    param_cols(11, 10)
                if s < FOUT.n_w - 1:
                    low(FOUT, s + 2)
                if s % 4 == 3:
                    for t in range(TT):
                        gate_block(2, N_FOUR, t, s // 4, ps[:, ROW_BANKS[(s // 4) % 2][t], :])
            next_input(2, N_FOUR, N_X2, PREP_F1, FOUT, 1, 3, 4, 2)
            ffn(1)
            residual(3, N_FFN1, None)

        @block.tensor
        def _(pe):
            def chunk_high(st, j, i=None):
                m = st.w0 + j
                pe.wait_ge(hi_ready, at(m + 1, st.n_w, i))
                return m % 2

            def chunk_low(st, j, i=None):
                pe.wait_ge(raw_done, at(st.raw(j) + PRE + 1, st.n_raw, i))

            def column_tile(st, j, bank, i=None, both=False):
                slot = chunk_high(st, j, i)
                n = 512 if both else 256
                for kt in range(KT):
                    for part in (LAT_HI, LAT_LO):
                        last = nc.tensor.matmul(ps[:, bank, 0:n], w_hi[:, slot, kt * P:(kt + 1) * P],
                                                hT[:, kt, part:part + (2 if both else 1), :],
                                                start=(kt == 0 and part == LAT_HI), stop=False)
                last.then_inc(hi_used, 1)
                chunk_low(st, j, i)
                for kt in range(KT):
                    last = nc.tensor.matmul(ps[:, bank, 0:n], w_lo[:, slot, kt * P:(kt + 1) * P],
                                            hT[:, kt, LAT_HI:LAT_HI + (2 if both else 1), :],
                                            start=False, stop=(kt == KT - 1))
                last.then_inc(chunk_used, 1)

            def first_tiles(st, first):
                for kt in range(KT):
                    if kt % 2 == 0:
                        pe.wait_ge(pair_lo, first + kt // 2 + 1)
                    for j in range(2):
                        slot = chunk_high(st, j) if kt == 0 else (st.w0 + j) % 2
                        for part in (LAT_HI, LAT_LO):
                            last = nc.tensor.matmul(ps[:, j, 0:256], w_hi[:, slot, kt * P:(kt + 1) * P],
                                                    hT[:, kt, part, :],
                                                    start=(kt == 0 and part == LAT_HI), stop=False)
                        if kt == KT - 1:
                            last.then_inc(hi_used, 1)
                for j in range(2):
                    chunk_low(st, j)
                    for kt in range(KT):
                        last = nc.tensor.matmul(ps[:, j, 0:256], w_lo[:, (st.w0 + j) % 2, kt * P:(kt + 1) * P],
                                                hT[:, kt, LAT_HI, :], start=False, stop=(kt == KT - 1))
                    last.then_inc(chunk_used, 1)

            def row_chunk(st, j, tiles, first, final, i=None):
                slot = chunk_high(st, j, i)
                for k in range(4):
                    cols = slice(k * 512, (k + 1) * 512)
                    for bank, hi, lo in tiles:
                        for q, a in enumerate((hi, lo)):
                            last = nc.tensor.matmul(ps[:, bank, :], a(k), w_hi[:, slot, cols],
                                                    start=(first and k == 0 and q == 0), stop=False)
                last.then_inc(hi_used, 1)
                chunk_low(st, j, i)
                for bank, hi, lo in tiles:
                    for k in range(4):
                        last = nc.tensor.matmul(ps[:, bank, :], hi(k), w_lo[:, slot, k * 512:(k + 1) * 512],
                                                start=False, stop=(final and k == 3))
                last.then_inc(chunk_used, 1)

            def latent_rows(b, kt0, hi=LAT_HI, lo=LAT_LO):
                return [(ROW_BANKS[b % 2][t],
                         lambda k, t=t: hT[:, kt0 + k, hi, t * P:(t + 1) * P],
                         lambda k, t=t: hT[:, kt0 + k, lo, t * P:(t + 1) * P]) for t in range(TT)]

            def prep(n, src, first_xn):
                for t in range(TT):
                    for pr in range(8):
                        if pr % 4 == 0:
                            pe.wait_ge(xn_made, first_xn + 2 * t + pr // 4)
                        for k in range(2):
                            kt = 2 * pr + k
                            last = nc.tensor.transpose(ps[:, pr, k * 256 + t * P:k * 256 + (t + 1) * P],
                                                       src[:, t, kt * P:(kt + 1) * P], ident)
                        if t == TT - 1:
                            last.then_inc(pair_T, 1)

            def sum_rows(fma_raw, i=None, per_turn=0):
                pe.wait_ge(raw_done, at(fma_raw + PRE + 1, per_turn, i))
                for b in range(4):
                    last = nc.tensor.matmul(ps[32 * b:32 * b + 32, SUM_BANK, :], ones[:, :],
                                            acc[:, b * 512:(b + 1) * 512], start=True, stop=True)
                last.then_inc(acc_free, 1)

            def rows_to_cols(count, i=None):
                pe.wait_ge(row_copied, at(count, 1, i))
                for r in range(4):
                    last = nc.tensor.transpose(ps[:, COL_BANK, r * P:(r + 1) * P],
                                               row_sb[:, r * P:(r + 1) * P], ident)
                last.then_inc(cols_made, 1)

            def gate(n):
                pe.wait_ge(gate_col, n + 1)
                nc.tensor.transpose(ps[0:16, SUM_BANK, 0:P], gate_cols[:, :], ident).then_inc(gate_T, 1)

            pe.wait_ge(in_small, 16 * 8)
            pe.wait_ge(zeros_set, 1)
            for n, (rows, width) in enumerate(((32, 32), (128, 128), (96, 96), (96, 96))):
                nc.tensor.transpose(ps[:, 2 + n, 0:width], small_rows[0:rows, n, :], ident[0:rows, 0:rows])\
                    .then_inc(small_T, 1)
            pe.wait_ge(start_w_made, 1)
            pe.wait_ge(small_cols, 3)
            EARLY = {12: (0, xn0, 0), 15: (0, xn0, 4), 18: (1, y, 0), 21: (1, y, 4)}

            def early_transposes(v, x_, pr0):
                pe.wait_ge(xn_made, 4 * v + 4)
                if v or pr0:
                    pe.wait_ge(early_back, 8 * v + pr0)
                for pr in range(pr0, pr0 + 4):
                    for t in range(TT):
                        for k in range(2):
                            kt = 2 * pr + k
                            last = nc.tensor.transpose(ps[:, 2 + pr % 4, k * 256 + t * P:k * 256 + (t + 1) * P],
                                                       x_[:, t, kt * P:(kt + 1) * P], ident)
                    last.then_inc(early_T, 1)

            for n in range(START_CHUNKS):
                par, kt = divmod(n, KT)
                if n in EARLY:
                    early_transposes(*EARLY[n])
                pe.wait_ge(raw_landed[n % RING], 16 * (n // RING + 1))
                for b in range(4):
                    last = nc.tensor.matmul(ps[32 * b:32 * b + 32, par, :], start_w[:, kt, :],
                                            raw[:, n % RING, b * 512:(b + 1) * 512],
                                            start=(kt == 0), stop=(kt == KT - 1))
                last.then_inc(start_used, 1)
            pe.wait_ge(start_row, 2)
            for par in range(2):
                for r in range(4):
                    last = nc.tensor.transpose(ps[:, 6 + par, r * P:(r + 1) * P],
                                               start_rows[:, par, r * P:(r + 1) * P], ident)
                last.then_inc(acc_free if par == 0 else start_T, 1)

            def scores(u, i):
                h, t = divmod(u, 2)
                if u == 0:
                    pe.wait_ge(qk_ready, at(8, 8, i))
                    pe.wait_ge(k_copied, at(4, 4, i))
                    pe.wait_ge(v_act, at(2, 2, i))
                    pe.wait_ge(v_dve, at(2, 2, i))
                if u >= 2:
                    pe.wait_ge(exp_done, at(2 * u - 2, 16, i))
                for cmp in range(2):
                    rows = slice(64 * cmp, 64 * cmp + 64)
                    last = nc.tensor.matmul(ps[:, 2 + 2 * (u % 2) + cmp, :], qT[rows, h, t * P:(t + 1) * P],
                                            kT[rows, h, :], start=True, stop=True)
                last.then_inc(scores_done, 1)

            def transpose_mix(u, i):
                pe.wait_ge(mix_done, at(u + 1, 8, i))
                if u == 0:
                    pe.wait_ge(cols_copied, at(1, 1, i))
                else:
                    pe.wait_ge(aT_ready, at(u, 8, i))
                for k in range(4):
                    last = nc.tensor.transpose(ps[:, COL_BANK, k * P:(k + 1) * P],
                                               probs[:, u % 2, 0, k * P:(k + 1) * P], ident)
                last.then_inc(mix_T, 1)

            def values(u, i):
                h = u // 2
                pe.wait_ge(aT_ready, at(u + 1, 8, i))
                if u:
                    pe.wait_ge(o_copied, at(u, 8, i))
                for k in range(4):
                    last = nc.tensor.matmul(ps[:, SUM_BANK, (u % 4) * P:(u % 4 + 1) * P],
                                            aT[:, u % 2, k * P:(k + 1) * P], v_sb[:, k, h * P:(h + 1) * P],
                                            start=(k == 0), stop=(k == 3))
                last.then_inc(pv_done, 1)

            def o_pair(pr, _=None):
                pe.wait_ge(xn_made, 8 + 2 * (GROUPS - 1 if pr < EARLY_PAIRS else GROUPS))
                if pr >= 2:
                    pe.wait_ge(pair_lo, 8 * PREP_O + pr - 1)
                for t in range(TT):
                    for k in range(2):
                        kt = 2 * pr + k
                        last = nc.tensor.transpose(ps[:, pr % 2, k * 256 + t * P:k * 256 + (t + 1) * P],
                                                   y[:, t, kt * P:(kt + 1) * P], ident)
                last.then_inc(pair_T, 1)

            def attend(ops, i):
                for op in ops:
                    {"S": scores, "T": transpose_mix, "V": values, "O": o_pair}[op[0]](int(op[1:]), i)

            def qkv_step(st, s, g, i=None):
                if s < 8:
                    if 2 <= s < 6:
                        pe.wait_ge(q_copied, at(s - 1, 4, g))
                    elif s >= 6:
                        pe.wait_ge(k_copied, at(s - 5, 4, g))
                    if st is QKV0 and s == 4:
                        pe.wait_ge(pair_lo, 16)
                    column_tile(st, s, s % 2, i, both=s >= 4)
                else:
                    kt0 = 4 * (s - 8)
                    tiles = [(2 + t,
                              lambda k, t=t: hT[:, kt0 + k, LAT_HI + t // 2, (t % 2) * P:(t % 2 + 1) * P],
                              lambda k, t=t: hT[:, kt0 + k, LAT_LO + t // 2, (t % 2) * P:(t % 2 + 1) * P])
                             for t in range(4)]
                    row_chunk(st, s, tiles, s == 8, s == 11, i)
                if s == 11:
                    sum_rows(st.raw0 + st.n_raw - 1, i, st.n_raw)

            first_tiles(QKV0, 0)
            for s in range(2, QKV0.n_w):
                qkv_step(QKV0, s, 0)
            with pe.Fori(0, GROUPS - 1) as i:
                for s in range(QKV.n_w):
                    if s == 1:
                        rows_to_cols(1, i)
                    attend(ATTEND[s], i)
                    qkv_step(QKV, s, i + 1, i)
            attend(["O0", "O1"], GROUPS - 1)
            rows_to_cols(GROUPS)
            attend(ATTEND_LAST, GROUPS - 1)

            for s in range(WO.n_w):
                b = s // 4
                if s == 1:
                    pe.wait_ge(o_copied, 8 * GROUPS)
                    gate(0)
                if s == 2:
                    for pr in range(EARLY_PAIRS, 8):
                        o_pair(pr)
                if s < 4:
                    pe.wait_ge(pair_lo, 16 + 2 * s + 2)
                if b >= 2 and s % 4 == 0:
                    pe.wait_ge(gated, 2 * (b - 1))
                row_chunk(WO, s, latent_rows(b, 4 * (s % 4)), s % 4 == 0, s % 4 == 3)

            def next_prep(n, first_xn):
                prep(n, y, first_xn)

            next_prep(PREP_F0, 17)

            def ffn(layer):
                up, loop, down = FFN_STAGES[layer]
                first = 8 * (PREP_F0, PREP_F1)[layer]

                def up_tile(st, s, hidden, per, i=None):
                    if s % 2 == 0:
                        if hidden:
                            pe.wait_ge(silu_done[layer], at(hidden, per, i))
                    elif hidden:
                        pe.wait_ge(act_done[layer], at(hidden, per, i))
                    column_tile(st, s, s % 2, i)

                def down_chunk(st, s, b, part8, slot, i=None):
                    if b == 0:
                        pe.wait_ge(act_lo_done[layer], at(part8 // 2 + 4, 8, i))
                    if part8 or b >= 2:
                        pe.wait_ge(y_added[layer], at(part8 + 2 * b - 2, 16, i))
                    tiles = [(ROW_BANKS[b % 2][t],
                              lambda k, t=t: act_hi[:, slot + k, t * P:(t + 1) * P],
                              lambda k, t=t: act_lo[:, slot + k, t * P:(t + 1) * P]) for t in range(TT)]
                    row_chunk(st, s, tiles, True, True, i)

                first_tiles(up, first)
                gate(1 + 2 * layer)
                for s in range(2, 8):
                    up_tile(up, s, s // 2, 0)
                with pe.Fori(0, 5) as i:
                    for s in range(24):
                        half, k = divmod(s, 12)
                        if k < 8:
                            up_tile(loop, s, 4 + 4 * half + k // 2, 8, i)
                        else:
                            down_chunk(loop, s, k - 8, 8 * half, 4 * half, i)
                        if layer == 0 and s == LOOP0_SUM:
                            sum_rows(LOOP0.raw(LOOP0_SUM) - 1, i, LOOP0.n_raw)
                        if layer == 0 and s == 23:
                            rows_to_cols(5, i)
                for s in range(4):
                    down_chunk(down, s, s, 8 * (PARTS - 1), 0)

            ffn(0)
            next_prep(PREP_FOUR, 21)

            first_tiles(FIN0, 8 * PREP_FOUR)
            for s in range(2, 4):
                pe.wait_ge(u_copied, s - 1)
                column_tile(FIN0, s, s % 2)
            with pe.Fori(0, 3) as i:
                for s in range(4):
                    pe.wait_ge(u_copied, at(s + 3, 4, i))
                    column_tile(FIN, s, s % 2, i)

            def group_dft(g):
                pe.wait_ge(u_copied, KT)
                pe.wait_ge(in_dft, 16)
                if g:
                    pe.wait_ge(ab_copied, 2 * g)
                for t in range(TT):
                    for k in range(2):
                        last = nc.tensor.matmul(ps[:, 2 + t, :], uT[:, 2 * g + k, t * P:(t + 1) * P],
                                                dft_group[:, k, :], start=(k == 0), stop=(k == 1))
                    last.then_inc(ab_done, 1)

            def token_dft(f):
                g, half = divmod(f, 2)
                pe.wait_ge(ab_copied, 2 * g + 2)
                if f >= 2:
                    pe.wait_ge(f_lo, f - 1)
                for q, table in enumerate((dft_cos, dft_sin)):
                    for k in range(2):
                        col = q * 256 + half * P
                        last = nc.tensor.matmul(ps[:, 4 + f % 2, 0:256], ab[:, g % 2, k, col:col + P],
                                                table[:, k, :], start=(q == 0 and k == 0),
                                                stop=(q == 1 and k == 1))
                last.then_inc(f_done, 1)

            for g in range(FGROUPS):
                group_dft(g)
                if g:
                    token_dft(2 * g - 2)
                    token_dft(2 * g - 1)
            token_dft(KT - 2)
            token_dft(KT - 1)
            pe.wait_ge(f_lo, KT)
            gate(2)
            for s in range(FOUT.n_w):
                b = s // 4
                if b >= 2 and s % 4 == 0:
                    pe.wait_ge(gated, 16 + 2 * (b - 1))
                row_chunk(FOUT, s, latent_rows(b, 4 * (s % 4), CTX_HI, CTX_LO), s % 4 == 0, s % 4 == 3)
                if s == FOUT_SUM:
                    sum_rows(FOUT.raw(FOUT_SUM) - 1)
                if s == FOUT_SUM + 1:
                    rows_to_cols(10)
            next_prep(PREP_F1, 25)
            ffn(1)


def shape_constants():
    inv = (np.float32(THETA) ** (-np.arange(16, dtype=np.float32) / np.float32(16))).astype(np.float32)
    tok = np.arange(SEQ)
    pos = np.stack([tok // GRID_W, tok % GRID_W]).astype(np.float32)
    row = np.arange(P)
    axis, second, freq = (row % 64) // 32, (row % 32) // 16, row % 16
    ang = (pos[axis] * inv[freq][:, None]).astype(np.float32)
    cos, sin = np.cos(ang), np.sin(ang) * np.where(second == 1, 1.0, -1.0)[:, None]
    consts = np.concatenate([np.eye(P), cos, sin], axis=1).astype(np.float32)
    n = np.arange(256)
    a = 2.0 * np.pi * ((n[:, None] * n[None, :]) % 256) / 256.0
    c, s = np.cos(a) / 16.0, np.sin(a) / 16.0
    tiles = lambda m: m.reshape(2, P, -1).transpose(1, 0, 2).reshape(P, -1)
    dft = np.concatenate([tiles(np.concatenate([c, s], axis=1)), tiles(c), tiles(-s)], axis=1)
    return consts, np.ascontiguousarray(dft.astype(np.float32))


_INS = ["x", "c", "ctx", "c_ctx", "mod_w", "mod_b", "norm_g", "ffn_w_gu", "ffn_w_down", "attn_w_qkv",
        "attn_w_o", "attn_lambda", "attn_subln_g", "four_w_in", "four_w_out"]


def kernel(**inputs):
    import concourse.bacc as _bacc
    from concourse.bass_utils import run_bass_kernel_spmd as _run

    nc = _bacc.Bacc("TRN2", target_bir_lowering=False, num_devices=1)
    arrays, args = {}, []
    named = [(name, np.ascontiguousarray(inputs[name])) for name in _INS]
    consts, dft = shape_constants()
    for name, a in named + [("consts", consts), ("dft", dft)]:
        arrays[f"in_{name}"] = a
        args.append(nc.dram_tensor(f"in_{name}", a.shape, mybir.dt.from_np(a.dtype), kind="ExternalInput").ap())
    out = nc.dram_tensor("out_0", (1, SEQ, D), F32, kind="ExternalOutput").ap()
    trunk(nc, *args, out)
    r = _run(nc, [arrays], core_ids=[0])
    return r.results[0]["out_0"]
```

```python
from contextlib import ExitStack

import numpy as np

import concourse.bass as bass
from concourse import mybir

ALU = mybir.AluOpType
ACT = mybir.ActivationFunctionType
AX_X = mybir.AxisListType.X
F32 = mybir.dt.float32
F32R = mybir.dt.float32r
BF16 = mybir.dt.bfloat16

P = 128
D = 2048
SEQ = 256
KT = D // P
TT = SEQ // P
HEADS = 16
HEAD_DIM = 64
GROUPS = 4
HPG = HEADS // GROUPS
FFN = 5632
FGROUPS = 8
PART = 4 * P
PARTS = FFN // PART
EPS = 1e-6
SCALE = HEAD_DIM ** -0.5
LAMBDA_INIT = 0.8 - 0.6
GRID_W = 64
THETA = 10000.0

RING = 4
QUARTERS = 4
START_ORDER = [chunk for q in range(QUARTERS) for chunk in
               [("m", 8 * q + n) for n in range(8)] + [("w", 2 * q + n) for n in range(2)]]
START_RAW = len(START_ORDER)
START_W = 2 * QUARTERS
PRE = RING

C_IDENT, C_COS, C_SIN = 0, P, P + SEQ
C_END = P + 2 * SEQ

ROW_BANKS = ((2, 3), (4, 5))
COL_BANK, SUM_BANK = 6, 7


class Stage:

    def __init__(self, before, n_w, hosts=None, turns=1):
        self.raw0, self.w0, self.m0 = before
        self.n_w, self.turns = n_w, turns
        self.hosts = hosts or [0] * n_w
        assert self.hosts[0] == 0 or not self.raw0
        self.n_m = sum(self.hosts)
        self.n_raw = n_w + self.n_m
        assert self.n_raw % RING == 0 and n_w % 2 == 0
        self.after = (self.raw0 + turns * self.n_raw, self.w0 + turns * n_w, self.m0 + turns * self.n_m)

    def raw(self, j):
        if j >= self.n_w:
            return self.raw0 + self.n_raw + j - self.n_w
        return self.raw0 + j + sum(self.hosts[:j])

    def order(self):
        kt = 0
        for j in range(self.n_w):
            yield "w", j
            for _ in range(self.hosts[j]):
                yield "m", kt
                kt += 1


def spread(n_w, n_m):
    k = n_w - 2
    return [0, 0] + [(j + 1) * n_m // k - j * n_m // k for j in range(k)]


QKV_HOSTS = [0, 0, 0, 1, 1, 0, 1, 1, 2, 3, 3, 4]
QKV0 = Stage((0, START_W, 0), HPG, [4, 4, 4, 4])
QKV = Stage(QKV0.after, 3 * HPG, QKV_HOSTS, GROUPS - 1)
WO = Stage(QKV.after, 16)

ATTEND = [[], ["S0"], ["T0"], ["S1", "V0"], ["S2", "S3", "T1"], ["S4", "S5", "T2", "V1", "T3"],
          ["S6", "S7", "T4", "V2", "T5", "V3"], ["V4", "T6", "V5", "T7"], ["V6", "V7"], [], [], []]
EARLY_PAIRS = 2 * (GROUPS - 1)
ATTEND_LAST = ["S0", "S1"] + [op for u in range(8) for op in
                              ([f"S{u + 2}"] if u < 6 else []) + [f"T{u}"] +
                              ([f"V{u - 1}"] if u else []) + ([f"O{u + 1}"] if 0 < u < 5 else [])]
ATTEND_LAST += ["V7"]
UP0 = Stage(WO.after, 8)
LOOP0 = Stage(UP0.after, 24, spread(20, KT) + [0] * 4, 5)
DOWN0 = Stage(LOOP0.after, 4)
FIN0 = Stage(DOWN0.after, 4)
FIN = Stage(FIN0.after, 4, turns=3)
FOUT_EARLY = 8
FOUT = Stage(FIN.after, 16, [0, FOUT_EARLY, 1, 1, 1, 1, 1, 1, 1, 1] + [0] * 6)
UP1 = Stage(FOUT.after, 8)
LOOP1 = Stage(UP1.after, 24, turns=5)
DOWN1 = Stage(LOOP1.after, 4)
FFN_STAGES = ((UP0, LOOP0, DOWN0), (UP1, LOOP1, DOWN1))

LOOP0_SUM, FOUT_SUM = 21, 10

PREP_LAT, PREP_CTX, PREP_O, PREP_F0, PREP_FOUR, PREP_F1 = range(6)


def at(base, per_turn, i):
    return base if i is None else base + per_turn * i


class Link:

    def __init__(self, eng, sem):
        self.eng, self.sem, self.n, self.more = eng, sem, 0, 0

    def __call__(self, ins):
        ins.then_inc(self.sem, 1)
        self.n += 1
        self.eng.wait_ge(self.sem, self.n + self.more)

    def turn(self, i, per_turn):
        self.start, self.per_turn, self.more = self.n, per_turn, per_turn * i

    def end(self, turns):
        assert self.n - self.start == self.per_turn, (self.n - self.start, self.per_turn)
        self.n, self.more = self.start + turns * self.per_turn, 0


def trunk(nc, x, c, ctx, c_ctx, mod_w, mod_b, norm_g, w_gu, w_down, w_qkv, w_o, lam, subln_g,
          w_in, w_out, consts, dft, out):
    x_d = x.rearrange("b (t p) d -> p (b t) d", p=P)
    ctx_d = ctx.rearrange("b (t p) d -> p (b t) d", p=P)
    out_d = out.rearrange("b (t p) d -> p (b t) d", p=P)
    mod_d = mod_w.rearrange("l d n -> (l d) n")
    gu_d = w_gu.rearrange("l d n -> (l d) n")
    down_d = w_down.rearrange("l d n -> (l d) n")
    qkv_d = w_qkv.rearrange("l d n -> (l d) n")
    wo_d = w_o.rearrange("l d n -> (l d) n")
    in_d = w_in.rearrange("l d n -> (l d) n")
    out_w_d = w_out.rearrange("l d n -> (l d) n")
    gate_scratch = nc.dram_tensor("gate_scratch", (4, D), F32, kind="Internal").ap()

    es = ExitStack()
    with es:
        def sb(name, shape, dt=F32):
            return es.enter_context(nc.sbuf_tensor(name, shape, dt))

        def sem(name):
            return es.enter_context(nc.semaphore(name))

        raw = sb("raw", [P, RING, 2048])
        w_hi = sb("w_hi", [P, 2, 2048], F32R)
        w_lo = sb("w_lo", [P, 2, 2048], F32R)
        LAT_HI, CTX_HI, LAT_LO, CTX_LO = range(4)
        hT = sb("hT", [P, KT, 4, SEQ], F32R)
        act_hi = hT[:, 0:8, CTX_HI, :]
        act_lo = hT[:, 0:8, CTX_LO, :]
        y = sb("y", [P, TT, D])
        acc = sb("acc", [P, 2048])
        htmp = acc[:, :].rearrange("p (b k t) -> p b k t", b=4, k=2)
        region = sb("region", [P, 8192])
        qT = region[:, 0:1024].rearrange("p (h t) -> p h t", h=HPG)
        kT = region[:, 1024:3072].rearrange("p (h t) -> p h t", h=HPG)
        v_sb = region[:, 3072:5120].rearrange("p (t e) -> p t e", t=4)
        probs = region[:, 5120:7168].rearrange("p (b c k) -> p b c k", b=2, c=2)
        aT = region[:, 7168:8192].rearrange("p (b k) -> p b k", b=2)
        xn0 = region[:, 0:4096].rearrange("p (t d) -> p t d", t=TT)
        small_rows = region[:, 4096:4608].rearrange("p (n k) -> p n k", n=4)
        lam_rows = region[:, 4608:4864].rearrange("p (n k) -> p n k", n=4)
        start_rows = region[:, 5120:6144].rearrange("p (n k) -> p n k", n=2)
        start_w = region[:, 6144:6656].rearrange("p (k c) -> p k c", k=KT)
        lam_prod = region[:, 6656:6784].rearrange("p (n k) -> p n k", n=2)
        xs = region[:, 0:4096].rearrange("p (t d) -> p t d", t=TT)
        gate_row = region[:, 4096:6144]
        silu_g = region[:, 6144:6656].rearrange("p (b t) -> p b t", b=2)
        act_f = region[:, 6656:7168].rearrange("p (b t) -> p b t", b=2)
        dft_sb = y[:, 0, :]
        dft_group = [sb(f"dft_group_{n}", [P, 2, 512], F32R) for n in ("hi", "lo")]
        dft_token = [hT[:, 8:12, n, :] for n in (LAT_HI, LAT_LO)]
        ab_hi, ab_lo = (hT[:, 0:8, n, :].rearrange("p (b t q) f -> p b t q f", b=2, t=2)
                        for n in (LAT_HI, LAT_LO))

        cst = sb("cst", [P, C_END])
        ident = cst[:, C_IDENT:C_IDENT + P]
        rope_cos = cst[:, C_COS:C_COS + SEQ]
        rope_sin = cst[:, C_SIN:C_SIN + SEQ]
        rope_c = sb("rope_c", [P, SEQ])
        rope_s = sb("rope_s", [P, SEQ])
        row_sb = sb("row_sb", [P, 512])
        gate16 = sb("gate16", [16, P])
        c_cols = sb("c_cols", [P, 2 * KT])
        g_cols = sb("g_cols", [P, 8 * KT])
        b_cols = sb("b_cols", [P, 12 * KT])
        p_cols = sb("p_cols", [P, 12 * KT])
        silu_c = sb("silu_c", [P, 2 * KT])
        start_cols = sb("start_cols", [P, 2, 2, KT])
        ab_start = sb("ab_start", [P, 2, 2, KT])
        ab_cols, ab_ctx = ab_start[:, 0, :, :], ab_start[:, 1, :, :]
        q_next = sb("q_next", [P, HPG, SEQ])
        gate_cols = sb("gate_cols", [P, KT])
        ones = sb("ones", [P, 32])
        subln = sb("subln", [P, 1])
        lam_s = sb("lam_s", [P, 4])
        stat = sb("stat", [P, 10, 16])
        s_max, s_neg, s_sum, s_rec, s_sq, s_ms, s_rstd, s_half, s_hsq, s_tot = (
            stat[:, n, :] for n in range(10))
        junk = sb("junk", [P, 512], BF16)

        ps = es.enter_context(nc.psum_tensor("ps", [P, 8, 512], F32))

        raw_landed = [sem(f"raw_landed{s}") for s in range(RING)]
        start_used = sem("start_used")
        raw_done = sem("raw_done")
        hi_ready = sem("hi_ready")
        hi_used = sem("hi_used")
        chunk_used = sem("chunk_used")
        first_tile = sem("first_tile")
        acc_free = sem("acc_free")
        row_copied = sem("row_copied")
        cols_made = sem("cols_made")
        cols_copied = sem("cols_copied")
        in_x = sem("in_x")
        in_ctx = sem("in_ctx")
        in_small = sem("in_small")
        in_xs = sem("in_xs")
        in_dft = sem("in_dft")
        half_set = sem("half_set")
        zeros_set = sem("zeros_set")
        dve_step = sem("dve_step")
        rope_step = sem("rope_step")
        small_T = sem("small_T")
        small_cols = sem("small_cols")
        silu_c_made = sem("silu_c_made")
        start_w_made = sem("start_w_made")
        start_hi = sem("start_hi")
        start_row = sem("start_row")
        start_T = sem("start_T")
        start_read = sem("start_read")
        start_split = sem("start_split")
        lam_summed = sem("lam_summed")
        lam_exp = sem("lam_exp")
        squared = sem("squared")
        ms_made = sem("ms_made")
        rstd_made = sem("rstd_made")
        xn_made = sem("xn_made")
        ab_made = sem("ab_made")
        early_T = sem("early_T")
        early_back = sem("early_back")
        pair_T = sem("pair_T")
        pair_dve = sem("pair_dve")
        pair_act = sem("pair_act")
        pair_hi = sem("pair_hi")
        pair_lo = sem("pair_lo")
        q_copied = sem("q_copied")
        k_copied = sem("k_copied")
        qk_ready = sem("qk_ready")
        v_act = sem("v_act")
        v_dve = sem("v_dve")
        scores_done = sem("scores_done")
        neg_made = sem("neg_made")
        exp_done = sem("exp_done")
        mix_done = sem("mix_done")
        mix_T = sem("mix_T")
        aT_ready = sem("aT_ready")
        pv_done = sem("pv_done")
        o_copied = sem("o_copied")
        head_ms = sem("head_ms")
        head_rstd = sem("head_rstd")
        gated = sem("gated")
        gate_T = sem("gate_T")
        gate_col = sem("gate_col")
        gate_16 = sem("gate_16")
        gate_dma = sem("gate_dma")
        res_done = sem("res_done")
        y_zero = [sem(f"y_zero{l}") for l in range(2)]
        y_added = [sem(f"y_added{l}") for l in range(2)]
        silu_done = [sem(f"silu_done{l}") for l in range(2)]
        act_done = [sem(f"act_done{l}") for l in range(2)]
        act_hi_done = [sem(f"act_hi_done{l}") for l in range(2)]
        act_lo_done = [sem(f"act_lo_done{l}") for l in range(2)]
        u_hi = sem("u_hi")
        u_lo = sem("u_lo")
        dft_hi = sem("dft_hi")
        dft_lo = sem("dft_lo")
        ab_done = sem("ab_done")
        ab_high = sem("ab_high")
        ab_low = sem("ab_low")
        f_done = sem("f_done")
        f_hi = sem("f_hi")
        f_lo = sem("f_lo")
        out_done = sem("out_done")

        block = es.enter_context(nc.Block())

        N_LAT, N_CTX, N_ATT, N_X0, N_FFN0, N_X1, N_FOUR, N_X2, N_FFN1 = range(9)

        @block.sync
        def _(sp):
            def start_free(n):
                if n >= RING:
                    kind, before = START_ORDER[n - RING]
                    sp.wait_ge(start_used if kind == "m" else start_split, before + 1)

            def load(src, n0, per_turn, i):
                sp.wait_ge(raw_done, at(n0 + 1, per_turn, i))
                if n0 < RING:
                    start_free(START_RAW + n0)
                s = n0 % RING
                k = src.shape[1] if len(src.shape) == 3 else 1
                dst = raw[:, s, :] if k == 1 else raw[:, s, :].rearrange("p (k c) -> p k c", k=k)
                sp.dma_start(dst, src).then_inc(raw_landed[s], 16)

            def cols(w, col):
                return w[0:D, bass.ds(col, P)].rearrange("(k p) c -> p k c", p=P)

            def rows(w, row, col):
                return w[bass.ds(row, 4 * P), bass.ds(col, 512)].rearrange("(k p) c -> p k c", p=P)

            def stage(st, source, param, i=None):
                n0 = st.raw0
                for kind, j in st.order():
                    if kind == "w":
                        src = source(j)
                    else:
                        layer = 0 if param[0] == 0 else 1
                        src = mod_d[layer * D + j * P:layer * D + (j + 1) * P, bass.ds(param[1] * D, D)]
                    load(src, n0, st.n_raw, i)
                    n0 += 1

            for n, (kind, idx) in enumerate(START_ORDER):
                start_free(n)
                if kind == "m":
                    q, par, r = idx // 8, idx // 4 % 2, idx % 4
                    src = rows(mod_d, r * 512, par * D + q * 512)
                else:
                    src = rows(qkv_d, idx // 2 * 512, idx % 2 * D)
                sp.dma_start(raw[:, n % RING, :].rearrange("p (k c) -> p k c", k=4), src)\
                    .then_inc(raw_landed[n % RING], 16)

            def qkv(g, j):
                kind, t = divmod(j, HPG)
                if kind < 2:
                    return cols(qkv_d, g * 512 + (kind * D + t * P))
                return rows(qkv_d, t * 512, g * 512 + 2 * D)

            stage(QKV0, lambda j: qkv(0, 2 * HPG + j), (0, 2))
            with sp.Fori(0, GROUPS - 1) as i:
                stage(QKV, lambda j: qkv(i + 1, j), (0, i + 3), i)

            stage(WO, lambda j: rows(wo_d, (j % 4) * 512, (j // 4) * 512), None)

            for layer in range(2):
                gu = gu_d[layer * D:(layer + 1) * D, :]
                dn = down_d[layer * FFN:(layer + 1) * FFN, :]
                up, loop, down = FFN_STAGES[layer]

                def up_src(part, j):
                    return cols(gu, part * PART + ((j // 2) * P + (j % 2) * FFN))

                def down_src(part, j):
                    return rows(dn, part * PART, j * 512)

                stage(up, lambda j: up_src(0, j), None)
                with sp.Fori(0, 5) as i:
                    def body(j):
                        half, k = divmod(j, 12)
                        if k < 8:
                            return up_src(2 * i + (1 + half), k)
                        return down_src(2 * i + half, k - 8)
                    stage(loop, body, (1, i), i)
                stage(down, lambda j: down_src(PARTS - 1, j), None)
                if layer == 0:
                    stage(FIN0, lambda j: cols(in_d, j * P), None)
                    with sp.Fori(0, 3) as i:
                        stage(FIN, lambda j: cols(in_d, i * 512 + (512 + j * P)), None, i)
                    stage(FOUT, lambda j: rows(out_w_d, (j % 4) * 512, (j // 4) * 512), (1, 5))

            for t in range(TT):
                for b in range(4):
                    sp.wait_ge(res_done, 24 + 4 * t + b + 1)
                    sp.dma_start(out_d[:, t, b * 512:(b + 1) * 512], xs[:, t, b * 512:(b + 1) * 512])\
                        .then_inc(out_done, 16)
            sp.wait_ge(out_done, 16 * TT * 4)
            sp.wait_ge(gate_dma, 16 * 8)

        @block.gpsimd
        def _(pool):
            nc.gpsimd.memset(ones[:, :], 1.0).then_inc(zeros_set, 1)
            nc.gpsimd.memset(start_w[:, :, :], 0.0).then_inc(zeros_set, 1)
            nc.gpsimd.memset(s_half, -0.5).then_inc(half_set, 1)
            pool.wait_ge(half_set, 1)

            def power(n):
                for t in range(TT):
                    o = 2 * (n % 2) + t
                    pool.wait_ge(ms_made, 2 * n + t + 1)
                    nc.gpsimd.tensor_tensor(s_rstd[:, o:o + 1], s_ms[:, o:o + 1], s_half[:, 0:1], ALU.pow)\
                        .then_inc(rstd_made, 1)

            def gate(n):
                pool.wait_ge(gate_16, n + 1)
                pool.dma_start(gate_scratch[n, :].rearrange("(k c) -> k c", c=P), gate16[:, :])\
                    .then_inc(gate_dma, 16)
                pool.wait_ge(gate_dma, 32 * n + 16)
                pool.dma_start(gate_row, gate_scratch[n, :].partition_broadcast(P)).then_inc(gate_dma, 16)

            power(N_LAT)
            power(N_CTX)

            def head_power(i):
                pool.wait_ge(head_ms, at(1, 1, i))
                nc.gpsimd.tensor_tensor(s_rstd[:, 8:16], s_ms[:, 8:16], s_half[:, 0:8], ALU.pow)\
                    .then_inc(head_rstd, 1)

            with pool.Fori(0, GROUPS - 1) as i:
                head_power(i)
            head_power(GROUPS - 1)
            pool.wait_ge(pv_done, 8 * GROUPS)
            pool.dma_start(xs, x_d).then_inc(in_xs, 16)
            gate(0)
            power(N_ATT)
            power(N_X0)
            for layer in range(2):
                pool.wait_ge(pair_T, 8 * ((PREP_F0, PREP_F1)[layer] - 2) + 8)
                for n in range(4):
                    nc.gpsimd.memset(y[:, n // 2, (n % 2) * 1024:(n % 2 + 1) * 1024], 0.0)\
                        .then_inc(y_zero[layer], 1)
                gate(1 + 2 * layer)
                power((N_FFN0, N_FFN1)[layer])
                if layer == 0:
                    power(N_X1)
                    pool.wait_ge(pair_T, 8 * (PREP_FOUR - 2) + 8)
                    pool.dma_start(dft_sb, dft).then_inc(in_dft, 16)
                    gate(2)
                    power(N_FOUR)
                    power(N_X2)

        @block.scalar
        def _(act):

            def high(st, j, i=None):
                n, m = st.raw(j), st.w0 + j
                act.wait_ge(raw_landed[n % RING],
                            at(16 * ((START_RAW + n) // RING + 1), 16 * st.n_raw // RING, i))
                if m >= 2:
                    if st is QKV0 and j < 2:
                        act.wait_ge(start_split, m - 1)
                    else:
                        act.wait_ge(raw_done, at(st.raw(j - 2) + PRE + 1, st.n_raw, i))
                    act.wait_ge(hi_used, at(m - 1, st.n_w, i))
                nc.scalar.activation(w_hi[:, m % 2, :], raw[:, n % RING, :], ACT.Copy).then_inc(hi_ready, 1)

            def used(st, j, i=None):
                act.wait_ge(chunk_used, at(st.w0 + j + 1, st.n_w, i))

            def sums_ready(st, s, t, r):
                if s == st.n_w - 1 and t == 0:
                    act.wait_ge(first_tile, r + 1)
                else:
                    used(st, s)

            def prep(n, hi):
                def odd(pr):
                    act.wait_ge(pair_T, 8 * (n - 2) + pr + 1)
                    act.wait_ge(ab_made, n + 2)
                    act.wait_ge(pair_lo, 8 * n + max(pr - 3, 0))
                    for k in range(2):
                        kt = 2 * pr + k
                        nc.scalar.activation(htmp[:, pr % 4, k, :], ps[:, pr, k * 256:(k + 1) * 256],
                                             ACT.Identity, bias=ab_cols[:, 1, kt:kt + 1],
                                             scale=ab_cols[:, 0, kt:kt + 1]).then_inc(pair_act, 1)

                def high_pair(pr):
                    if pr % 2:
                        act.wait_ge(pair_act, 8 * (n - 3) + pr + 1)
                    else:
                        act.wait_ge(pair_dve, 8 * (n - 3) + pr + 2)
                    nc.scalar.activation(hT[:, 2 * pr:2 * pr + 2, hi, :], htmp[:, pr % 4, :, :], ACT.Copy)\
                        .then_inc(pair_hi, 1)

                for pr in range(0, 8, 2):
                    odd(pr + 1)
                    high_pair(pr)
                    high_pair(pr + 1)

            def square(n, t, b, src):
                col = 8 * (n % 2) + 4 * t + b
                if b or t or n:
                    self_count = squares_done[0]
                    act.wait_ge(squared, self_count)
                squares_done[0] += 1
                nc.scalar.activation(junk[:, :], src, ACT.Square, accum_out=s_sq[:, col:col + 1])\
                    .then_inc(squared, 1)

            squares_done = [0]

            def blocks(x_):
                return [(t, b, x_[:, t, b * 512:(b + 1) * 512]) for t in range(TT) for b in range(4)]

            def row_copy(p, i=None):
                act.wait_ge(acc_free, at(p + 2, 1, i))
                nc.scalar.activation(row_sb[:, :], ps[:, SUM_BANK, :], ACT.Copy).then_inc(row_copied, 1)

            def gate(n):
                act.wait_ge(gate_T, n + 1)
                if n:
                    act.wait_ge(gate_dma, 32 * n)
                nc.scalar.activation(gate16[:, :], ps[0:16, SUM_BANK, 0:P], ACT.Copy).then_inc(gate_16, 1)

            act.dma_start(small_rows[0:16, 0, :], c.rearrange("b (k c) -> (b k) c", c=P)).then_inc(in_small, 16)
            act.dma_start(small_rows[16:32, 0, :], c_ctx.rearrange("(k c) -> k c", c=P)).then_inc(in_small, 16)
            act.dma_start(small_rows[:, 1, :], norm_g.rearrange("l n (k c) -> (l n k) c", c=P))\
                .then_inc(in_small, 16)
            for layer in range(2):
                act.dma_start(small_rows[0:96, 2 + layer, :], mod_b[layer, :].rearrange("(k c) -> k c", c=P))\
                    .then_inc(in_small, 16)
            act.dma_start(cst[:, :], consts).then_inc(in_small, 16)
            act.dma_start(subln[:, :], subln_g.rearrange("l e -> e l")).then_inc(in_small, 16)
            act.dma_start(lam_rows[:, :, :], lam.rearrange("l n d -> (l n) d").partition_broadcast(P))\
                .then_inc(in_small, 16)
            act.dma_start(xn0, x_d).then_inc(in_x, 16)
            act.dma_start(y[:, :, :], ctx_d).then_inc(in_ctx, 16)

            act.wait_ge(small_cols, 3)
            nc.scalar.activation(silu_c[:, :], c_cols[:, :], ACT.Silu).then_inc(silu_c_made, 1)
            act.wait_ge(in_x, 16)
            for t, b, src in blocks(xn0):
                square(N_LAT, t, b, src)
            act.wait_ge(in_ctx, 16)
            for t, b, src in blocks(y):
                square(N_CTX, t, b, src)
            act.wait_ge(lam_summed, 1)
            nc.scalar.activation(lam_s[:, 2:4], lam_s[:, 0:2], ACT.Exp).then_inc(lam_exp, 1)

            def start_high(n, v, pr):
                src = (xn0, y)[v]
                act.wait_ge(ab_made, n // 4 + 1)
                act.wait_ge(early_back, 8 * v + pr + 1)
                for k in range(2):
                    kt = 2 * pr + k
                    nc.scalar.activation(hT[:, kt, LAT_HI + v, :], src[:, k, pr * 256:(pr + 1) * 256],
                                         ACT.Identity, bias=ab_start[:, v, 1, kt:kt + 1],
                                         scale=ab_start[:, v, 0, kt:kt + 1]).then_inc(start_hi, 1)

            def start_weight_high(m):
                n = START_ORDER.index(("w", m))
                act.wait_ge(raw_landed[n % RING], 16 * (n // RING + 1))
                if m >= 2:
                    act.wait_ge(start_split, m - 1)
                    act.wait_ge(hi_used, m - 1)
                nc.scalar.activation(w_hi[:, m % 2, :], raw[:, n % RING, :], ACT.Copy).then_inc(hi_ready, 1)

            for q in range(QUARTERS):
                for par in range(2):
                    act.wait_ge(start_used, 8 * q + 4 * par + 4)
                    if q:
                        act.wait_ge(start_T, 2 * q + par - 1)
                    nc.scalar.activation(start_rows[:, par, :], ps[:, 6 + par, :], ACT.Copy).then_inc(start_row, 1)
                for v in range(2):
                    for n in range(2):
                        start_high(4 * q + 2 * v + n, v, 2 * q + n)
                    start_weight_high(2 * q + v)
            high(QKV0, 0)
            act.wait_ge(chunk_used, START_W - 1)
            for t in range(HPG):
                nc.scalar.activation(q_next[:, t, :], ps[:, t // 2, t % 2 * 256:(t % 2 + 1) * 256], ACT.Copy)\
                    .then_inc(q_copied, 1)
            high(QKV0, 1)
            act.wait_ge(chunk_used, START_W)
            for t in range(HPG):
                nc.scalar.activation(kT[:, t, :], ps[:, 2 + t, :], ACT.Copy).then_inc(k_copied, 1)

            def attend(ops, i):
                for op in [o for o in ops if o[0] != "S"] + [o for o in ops if o[0] == "S"]:
                    u = int(op[1:])
                    if op[0] == "T":
                        act.wait_ge(mix_T, at(u + 1, 8, i))
                        if u >= 2:
                            act.wait_ge(pv_done, at(u - 1, 8, i))
                        nc.scalar.activation(aT[:, u % 2, :], ps[:, COL_BANK, :], ACT.Copy).then_inc(aT_ready, 1)
                    elif op[0] == "V":
                        h, t = divmod(u, 2)
                        act.wait_ge(pv_done, at(u + 1, 8, i))
                        nc.scalar.activation(y[:, t, bass.ds(i * 512 + h * P, P)],
                                             ps[:, SUM_BANK, (u % 4) * P:(u % 4 + 1) * P], ACT.Copy)\
                            .then_inc(o_copied, 1)
                    else:
                        act.wait_ge(neg_made, at(u + 1, 8, i))
                        if u >= 2:
                            act.wait_ge(mix_T, at(u - 1, 8, i))
                        for h in range(2):
                            bank = 2 + 2 * (u % 2) + h
                            nc.scalar.activation(probs[:, u % 2, h, :], ps[:, bank, :], ACT.Exp,
                                                 bias=s_neg[:, 2 * u + h:2 * u + h + 1], scale=SCALE,
                                                 accum_out=s_sum[:, 2 * u + h:2 * u + h + 1])\
                                .then_inc(exp_done, 1)

            def qkv_step(st, s, g, i=None):
                high(st, s + 2, i)
                used(st, s, i)
                if s < 4:
                    nc.scalar.activation(q_next[:, s, :], ps[:, s % 2, 0:256], ACT.Copy).then_inc(q_copied, 1)
                elif s < 8:
                    nc.scalar.activation(kT[:, s - 4, :], ps[:, s % 2, :], ACT.Copy).then_inc(k_copied, 1)
                if s == 11:
                    values_out(g)

            def values_out(g):
                for t in range(2):
                    nc.scalar.activation(v_sb[:, t, :], ps[:, 2 + t, :], ACT.Copy).then_inc(v_act, 1)
                row_copy(0, g)

            for s in range(QKV0.n_w):
                high(QKV0, s + 2)
            used(QKV0, QKV0.n_w - 1)
            values_out(0)
            with act.Fori(0, GROUPS - 1) as i:
                for s in range(QKV.n_w):
                    attend(ATTEND[s], i)
                    qkv_step(QKV, s, i + 1, i)

            def o_high(pr):
                act.wait_ge(pair_T, pr + 1)
                nc.scalar.activation(hT[:, 2 * pr:2 * pr + 2, LAT_HI, :],
                                     ps[:, pr % 2, :].rearrange("p (k t) -> p k t", k=2),
                                     ACT.Copy, scale=subln[:, 0:1]).then_inc(pair_hi, 1)

            order = ["S0"] + [op for u in range(8) for op in
                              ([f"S{u + 1}"] if u < 7 else []) + ([f"O{u}"] if u < EARLY_PAIRS else []) +
                              [f"T{u}"] + ([f"V{u - 1}"] if u else [])]
            for op in order + ["V7"]:
                if op[0] == "O":
                    o_high(int(op[1:]))
                else:
                    attend([op], GROUPS - 1)

            for s in range(WO.n_w):
                if s < WO.n_w - 1:
                    high(WO, s + 2)
                if s == 1:
                    for pr in range(EARLY_PAIRS, 8):
                        o_high(pr)
                if s % 4 == 3:
                    for t in range(2):
                        sums_ready(WO, s, t, 0)
                        square(N_ATT, t, s // 4, ps[:, ROW_BANKS[(s // 4) % 2][t], :])
                if s == 0:
                    gate(0)

            def ffn(layer):
                up, loop, down = FFN_STAGES[layer]

                def up_step(st, s, hidden, per, slot, i=None):
                    if s % 2 == 0:
                        used(st, s, i)
                        nc.scalar.activation(silu_g[:, hidden % 2, :], ps[:, 0, 0:256], ACT.Silu)\
                            .then_inc(silu_done[layer], 1)
                    else:
                        act.wait_ge(act_done[layer], at(hidden + 1, per, i))
                        nc.scalar.activation(act_hi[:, slot, :], act_f[:, hidden % 2, :], ACT.Copy)\
                            .then_inc(act_hi_done[layer], 1)

                for s in range(8):
                    high(up, s + 2)
                    up_step(up, s, s // 2, 0, s // 2)
                    if s == 0:
                        gate(1 + 2 * layer)
                with act.Fori(0, 5) as i:
                    for s in range(24):
                        high(loop, s + 2, i)
                        half, k = divmod(s, 12)
                        if k < 8:
                            up_step(loop, s, 4 + 4 * half + k // 2, 8, 4 * (1 - half) + k // 2, i)
                        if layer == 0 and s == LOOP0_SUM:
                            row_copy(4, i)
                for s in range(4):
                    if s < (3 if layer == 0 else 2):
                        high(down, s + 2)
                    for t in range(TT):
                        act.wait_ge(y_added[layer], 8 * (PARTS - 1) + 2 * s + t + 1)
                        square((N_FFN0, N_FFN1)[layer], t, s, y[:, t, s * 512:(s + 1) * 512])

            def squares_x(n, r, st):
                for t, b, src in blocks(xs):
                    act.wait_ge(res_done, 8 * r + 4 * t + b + 1)
                    square(n, t, b, src)
                high(st, st.n_w + 1)

            squares_x(N_X0, 0, WO)
            prep(PREP_F0, LAT_HI)
            ffn(0)
            squares_x(N_X1, 1, DOWN0)
            prep(PREP_FOUR, LAT_HI)

            def fin_step(st, s, tile, i=None):
                high(st, s + 2, i)
                used(st, s, i)
                nc.scalar.activation(hT[:, bass.ds(tile, 1), CTX_HI, :], ps[:, s % 2, 0:256].unsqueeze(1),
                                     ACT.Copy).then_inc(u_hi, 1)

            for s in range(4):
                fin_step(FIN0, s, s)
            act.wait_ge(in_dft, 16)
            nc.scalar.activation(dft_group[0][:, :, :], dft_sb[:, 0:1024].rearrange("p (k f) -> p k f", k=2),
                                 ACT.Copy).then_inc(dft_hi, 1)
            with act.Fori(0, 3) as i:
                for s in range(4):
                    fin_step(FIN, s, i * 4 + (4 + s), i)
            def f_high(f):
                act.wait_ge(f_done, f + 1)
                nc.scalar.activation(hT[:, f, CTX_HI, :], ps[:, 4 + f % 2, 0:256], ACT.Copy).then_inc(f_hi, 1)

            nc.scalar.activation(dft_token[0], dft_sb[:, 1024:2048].rearrange("p (k f) -> p k f", k=4),
                                 ACT.Copy).then_inc(dft_hi, 1)
            for g in range(FGROUPS):
                for t in range(TT):
                    act.wait_ge(ab_done, 2 * g + t + 1)
                    if g >= 2:
                        act.wait_ge(f_done, 2 * g - 2)
                    nc.scalar.activation(ab_hi[:, g % 2, t, :, :],
                                         ps[:, 2 * (g % 2) + t, :].rearrange("p (q f) -> p q f", q=2), ACT.Copy)\
                        .then_inc(ab_high, 1)
                if g:
                    f_high(2 * g - 2)
                    f_high(2 * g - 1)
            f_high(KT - 2)
            f_high(KT - 1)
            gate(2)
            for s in range(FOUT.n_w):
                if s < FOUT.n_w - 1:
                    high(FOUT, s + 2)
                if s % 4 == 3:
                    for t in range(2):
                        sums_ready(FOUT, s, t, 2)
                        square(N_FOUR, t, s // 4, ps[:, ROW_BANKS[(s // 4) % 2][t], :])
                if s == FOUT_SUM:
                    row_copy(9)
            squares_x(N_X2, 2, FOUT)
            prep(PREP_F1, LAT_HI)
            ffn(1)

        @block.vector
        def _(dve):
            link = Link(dve, dve_step)

            def low(st, j, i=None):
                n, m = st.raw(j), st.w0 + j
                dve.wait_ge(hi_ready, at(m + 1, st.n_w, i))
                if m >= 2:
                    dve.wait_ge(chunk_used, at(m - 1, st.n_w, i))
                nc.vector.tensor_tensor(w_lo[:, m % 2, :], raw[:, n % RING, :],
                                        w_hi[:, m % 2, :].bitcast(F32), ALU.subtract).then_inc(raw_done, 1)
                if j < st.n_w and not (st is FOUT and j == 1):
                    fold(st, j, range(st.hosts[j]), i)

            def fold(st, j, which, i=None):
                for q in which:
                    n = st.raw(j) + 1 + q
                    kt = sum(st.hosts[:j]) + q
                    dve.wait_ge(raw_landed[n % RING],
                                at(16 * ((START_RAW + n) // RING + 1), 16 * st.n_raw // RING, i))
                    if kt == 0:
                        if st is QKV0:
                            dve.wait_ge(pair_lo, 16)
                        dve.wait_ge(acc_free, at(st.m0 // KT + 1, 1, i))
                        nc.vector.tensor_scalar(acc[:, :], raw[:, n % RING, :], silu_c[:, 0:1], None,
                                                ALU.mult).then_inc(raw_done, 1)
                    else:
                        dve.wait_ge(raw_done, at(n + PRE, st.n_raw, i))
                        nc.vector.scalar_tensor_tensor(out=acc[:, :], in0=raw[:, n % RING, :],
                                                       scalar=silu_c[:, kt:kt + 1], in1=acc[:, :],
                                                       op0=ALU.mult, op1=ALU.add).then_inc(raw_done, 1)

            def used(st, j, i=None):
                dve.wait_ge(chunk_used, at(st.w0 + j + 1, st.n_w, i))

            def prep(n, lo, hi):
                def even(pr):
                    dve.wait_ge(pair_T, 8 * (n - 2) + pr + 1)
                    if pr >= 4:
                        dve.wait_ge(pair_lo, 8 * n + pr - 3)
                    for k in range(2):
                        kt = 2 * pr + k
                        nc.vector.tensor_scalar(htmp[:, pr % 4, k, :], ps[:, pr, k * 256:(k + 1) * 256],
                                                ab_cols[:, 0, kt:kt + 1], ab_cols[:, 1, kt:kt + 1],
                                                ALU.mult, ALU.add).then_inc(pair_dve, 1)

                def low_pair(pr):
                    dve.wait_ge(pair_hi, 8 * (n - 2) + pr + 1)
                    nc.vector.tensor_tensor(hT[:, 2 * pr:2 * pr + 2, lo, :], htmp[:, pr % 4, :, :],
                                            hT[:, 2 * pr:2 * pr + 2, hi, :].bitcast(F32), ALU.subtract)\
                        .then_inc(pair_lo, 1)

                even(0)
                for pr in range(0, 8, 2):
                    if pr + 2 < 8:
                        even(pr + 2)
                    low_pair(pr)
                    low_pair(pr + 1)

            def mean_square(n, t, ready):
                dve.wait_ge(squared, 8 * n + ready)
                o = 2 * (n % 2) + t
                link(nc.vector.tensor_reduce(s_tot[:, o:o + 1], s_sq[:, 4 * o:4 * o + 4], AX_X, ALU.add))
                nc.vector.tensor_scalar(s_ms[:, o:o + 1], s_tot[:, o:o + 1], 1.0 / D, EPS, ALU.mult, ALU.add)\
                    .then_inc(ms_made, 1)

            def rstd(n, t):
                dve.wait_ge(rstd_made, 2 * n + t + 1)
                o = 2 * (n % 2) + t
                return s_rstd[:, o:o + 1]

            def normalise(n, t, dst, src):
                scale = rstd(n, t)
                for half in range(2):
                    cols = slice(half * D // 2, (half + 1) * D // 2)
                    nc.vector.tensor_scalar(dst[:, t, cols], src[:, t, cols], scale, None, ALU.mult)\
                        .then_inc(xn_made, 1)

            def cols_of(layer, par):
                return slice((6 * layer + par) * KT, (6 * layer + par + 1) * KT)

            def modulation(layer, shift, scale, norm):
                link(nc.vector.scalar_tensor_tensor(
                    out=ab_cols[:, 0, :], in0=p_cols[:, cols_of(layer, scale)], scalar=1.0,
                    in1=b_cols[:, cols_of(layer, scale)], op0=ALU.add, op1=ALU.add))
                g = g_cols[:, (4 * layer + norm) * KT:(4 * layer + norm + 1) * KT]
                link(nc.vector.tensor_tensor(ab_cols[:, 0, :], ab_cols[:, 0, :], g, ALU.mult))
                nc.vector.tensor_tensor(ab_cols[:, 1, :], p_cols[:, cols_of(layer, shift)],
                                        b_cols[:, cols_of(layer, shift)], ALU.add).then_inc(ab_made, 1)

            def gate(n, layer, par, norm):
                if n:
                    dve.wait_ge(gate_T, n)
                link(nc.vector.tensor_tensor(gate_cols[:, :], p_cols[:, cols_of(layer, par)],
                                             b_cols[:, cols_of(layer, par)], ALU.add))
                g = g_cols[:, (4 * layer + norm) * KT:(4 * layer + norm + 1) * KT]
                nc.vector.tensor_tensor(gate_cols[:, :], gate_cols[:, :], g, ALU.mult).then_inc(gate_col, 1)

            def gate_block(r, norm, t, b, src):
                dve.wait_ge(squared, 8 * norm + 2 * b + t + 1)
                dve.wait_ge(gate_dma, 32 * r + 32)
                nc.vector.tensor_tensor(y[:, t, b * 512:(b + 1) * 512], src,
                                        gate_row[:, b * 512:(b + 1) * 512], ALU.mult).then_inc(gated, 1)

            def residual(r, norm, next_norm, last_block):
                if r == 0:
                    dve.wait_ge(in_xs, 16)
                last_block(0)
                mean_square(norm, 0, 7)
                for t in range(TT):
                    scale = rstd(norm, t)
                    dve.wait_ge(gated, 8 * r + 7 + t)
                    for b in range(4):
                        blk = xs[:, t, b * 512:(b + 1) * 512]
                        nc.vector.scalar_tensor_tensor(out=blk, in0=y[:, t, b * 512:(b + 1) * 512],
                                                       scalar=scale, in1=blk, op0=ALU.mult, op1=ALU.add)\
                            .then_inc(res_done, 1)
                        if t == 0 and b == 1:
                            last_block(1)
                        if t == 0 and b == 2:
                            mean_square(norm, 1, 8)
                        if next_norm is not None and t == 1 and b == 1:
                            mean_square(next_norm, 0, 4)
                if next_norm is not None:
                    normalise(next_norm, 0, y, xs)
                    mean_square(next_norm, 1, 8)
                    normalise(next_norm, 1, y, xs)

            def param_cols(idx, count, i=None):
                dve.wait_ge(cols_made, at(count, 1, i))
                dst = p_cols[:, bass.ds(idx * KT, KT)] if i is not None else p_cols[:, idx * KT:(idx + 1) * KT]
                nc.vector.tensor_copy(dst.rearrange("p (b r) -> p r b", b=4),
                                      ps[:, COL_BANK, :].rearrange("p (r b z) -> p r b z", r=4, b=4)[:, :, :, 0])\
                    .then_inc(cols_copied, 1)

            for n in range(PRE):
                nc.vector.memset(gate_cols[:, n:n + 1], 0.0).then_inc(raw_done, 1)
            dve.wait_ge(small_T, 4)
            nc.vector.tensor_copy(c_cols[:, :], ps[:, 2, 0:32]).then_inc(small_cols, 1)
            nc.vector.tensor_copy(g_cols[:, :], ps[:, 3, 0:128]).then_inc(small_cols, 1)
            nc.vector.tensor_copy(b_cols[:, :].rearrange("p (l k) -> p l k", l=2),
                                  ps[:, 4:6, 0:96]).then_inc(small_cols, 1)
            dve.wait_ge(silu_c_made, 1)
            dve.wait_ge(zeros_set, 2)
            nc.vector.tensor_copy(start_w[:, :, 0:2], silu_c[:, :].rearrange("p (v k) -> p k v", v=2))\
                .then_inc(start_w_made, 1)
            link(nc.vector.tensor_tensor(lam_prod[:, :, :], lam_rows[:, 0::2, :], lam_rows[:, 1::2, :], ALU.mult))
            nc.vector.tensor_reduce(lam_s[:, 0:2], lam_prod[:, :, :], AX_X, ALU.add).then_inc(lam_summed, 1)
            link(nc.vector.tensor_scalar(subln[:, :], subln[:, :], 1.0 - LAMBDA_INIT, None, ALU.mult))

            def back(first, last):
                for n in range(first, last):
                    x_, pr = (xn0, y)[n // 8], n % 8
                    dve.wait_ge(early_T, n + 1)
                    nc.vector.tensor_copy(x_[:, :, pr * 256:(pr + 1) * 256],
                                          ps[:, n % 6, :].rearrange("p (k t) -> p k t", k=2))\
                        .then_inc(early_back, 1)

            for n, x_ in ((N_LAT, xn0), (N_CTX, y)):
                mean_square(n, 0, 4)
                mean_square(n, 1, 8)
                for t in range(TT):
                    normalise(n, t, x_, x_)
                if n == N_LAT:
                    back(0, 4)
            back(4, 16)
            dve.wait_ge(lam_exp, 1)
            link(nc.vector.tensor_scalar(lam_s[:, 0:1], lam_s[:, 3:4], -LAMBDA_INIT, None, ALU.add))
            link(nc.vector.tensor_tensor(lam_s[:, 0:1], lam_s[:, 0:1], lam_s[:, 2:3], ALU.subtract))
            neg_lam = lam_s[:, 0:1]
            def start_modulation(q):
                tiles = slice(4 * q, 4 * q + 4)
                for par in range(2):
                    if (q, par) == (QUARTERS - 1, 1):
                        dve.wait_ge(acc_free, 1)
                    else:
                        dve.wait_ge(start_T, 2 * q + par + 1)
                    nc.vector.tensor_reduce(start_cols[:, par, :, tiles].rearrange("p v r -> p r v"),
                                            ps[:, 6 + par, :].rearrange("p (r k z) -> p r z k", r=4, k=4)
                                            [:, :, 0:2, :], AX_X, ALU.add).then_inc(start_read, 1)
                dve.wait_ge(start_read, 2 * q + 2)

                def both(cols):
                    return cols.unsqueeze(1).to_broadcast([P, 2, 4])

                scale, shift = (b_cols[:, cols_of(0, par)][:, tiles] for par in (1, 0))
                link(nc.vector.scalar_tensor_tensor(out=ab_start[:, :, 0, tiles], in0=start_cols[:, 1, :, tiles],
                                                    scalar=1.0, in1=both(scale), op0=ALU.add, op1=ALU.add))
                link(nc.vector.tensor_tensor(ab_start[:, :, 0, tiles], ab_start[:, :, 0, tiles],
                                             both(g_cols[:, tiles]), ALU.mult))
                nc.vector.tensor_tensor(ab_start[:, :, 1, tiles], start_cols[:, 0, :, tiles], both(shift), ALU.add)\
                    .then_inc(ab_made, 1)
                dve.wait_ge(ab_made, q + 1)

            def start_low(n, v, pr):
                src = (xn0, y)[v]
                if n >= 4:
                    dve.wait_ge(pair_lo, n - 3)
                for k in range(2):
                    kt = 2 * pr + k
                    made = nc.vector.tensor_scalar(htmp[:, n % 4, k, :], src[:, k, pr * 256:(pr + 1) * 256],
                                                   ab_start[:, v, 0, kt:kt + 1], ab_start[:, v, 1, kt:kt + 1],
                                                   ALU.mult, ALU.add)
                link(made)
                dve.wait_ge(start_hi, 2 * n + 2)
                nc.vector.tensor_tensor(hT[:, 2 * pr:2 * pr + 2, LAT_LO + v, :], htmp[:, n % 4, :, :],
                                        hT[:, 2 * pr:2 * pr + 2, LAT_HI + v, :].bitcast(F32), ALU.subtract)\
                    .then_inc(pair_lo, 1)

            def start_weight_low(m):
                n = START_ORDER.index(("w", m))
                dve.wait_ge(hi_ready, m + 1)
                if m >= 2:
                    dve.wait_ge(chunk_used, m - 1)
                nc.vector.tensor_tensor(w_lo[:, m % 2, :], raw[:, n % RING, :], w_hi[:, m % 2, :].bitcast(F32),
                                        ALU.subtract).then_inc(start_split, 1)

            for q in range(QUARTERS):
                start_modulation(q)
                for v in range(2):
                    for n in range(2):
                        start_low(4 * q + 2 * v + n, v, 2 * q + n)
                    start_weight_low(2 * q + v)

            SWAP = [(r + 16) % 32 for r in range(32)]

            def rope(dst, src, tile, g):
                if tile:
                    dve.wait_ge(qk_ready, at(tile, 8, g))
                nc.vector.tensor_tensor(rope_c[:, :], src, rope_cos, ALU.mult).then_inc(rope_step, 1)
                link(nc.vector.stream_shuffle(rope_s[:, :], src, SWAP))
                nc.vector.tensor_tensor(rope_s[:, :], rope_s[:, :], rope_sin, ALU.mult).then_inc(rope_step, 1)
                dve.wait_ge(rope_step, at(2 * tile + 2, 16, g))
                nc.vector.tensor_tensor(dst, rope_c[:, :], rope_s[:, :], ALU.add).then_inc(qk_ready, 1)

            def maxima(u, i):
                dve.wait_ge(scores_done, at(u + 1, 8, i))
                bank = 2 + 2 * (u % 2)
                link(nc.vector.tensor_reduce(s_max[:, 2 * u:2 * u + 2], ps[:, bank:bank + 2, :], AX_X, ALU.max))
                nc.vector.tensor_scalar(s_neg[:, 2 * u:2 * u + 2], s_max[:, 2 * u:2 * u + 2], -SCALE, None,
                                        ALU.mult).then_inc(neg_made, 1)

            def mix(u, i):
                dve.wait_ge(exp_done, at(2 * u + 2, 16, i))
                link(nc.vector.reciprocal(s_rec[:, 2 * u:2 * u + 2], s_sum[:, 2 * u:2 * u + 2]))
                e0, e1 = probs[:, u % 2, 0, :], probs[:, u % 2, 1, :]
                link(nc.vector.tensor_scalar(e1, e1, s_rec[:, 2 * u + 1:2 * u + 2], neg_lam, ALU.mult, ALU.mult))
                nc.vector.scalar_tensor_tensor(out=e0, in0=e0, scalar=s_rec[:, 2 * u:2 * u + 1], in1=e1,
                                               op0=ALU.mult, op1=ALU.add).then_inc(mix_done, 1)

            def head_squares(i):
                dve.wait_ge(o_copied, at(8, 8, i))
                sq = probs[:, 0, :, :]
                o = y[:, :, bass.ds(i * 512, 512)]
                link(nc.vector.tensor_tensor(sq, o, o, ALU.mult))
                link(nc.vector.tensor_reduce(s_hsq[:, 0:8], sq.rearrange("p t (h e) -> p t h e", h=4), AX_X, ALU.add))
                nc.vector.tensor_scalar(s_ms[:, 8:16], s_hsq[:, 0:8], 1.0 / P, EPS, ALU.mult, ALU.add)\
                    .then_inc(head_ms, 1)

            def head_norm(i):
                dve.wait_ge(head_rstd, at(1, 1, i))
                for t in range(TT):
                    o = y[:, t, bass.ds(i * 512, 512)].rearrange("p (h e) -> p h e", h=4)
                    r = s_rstd[:, 8 + 4 * t:12 + 4 * t].unsqueeze(2).to_broadcast([P, 4, P])
                    nc.vector.tensor_tensor(o, o, r, ALU.mult).then_inc(xn_made, 1)

            def attend(ops, i):
                units = [int(op[1:]) for op in ops if op[0] == "S"]
                for u in units:
                    maxima(u, i)
                for u in units:
                    mix(u, i)

            def qkv_step(st, s, g, i=None):
                if 5 <= s < 9:
                    dve.wait_ge(k_copied, at(s - 4, 4, g))
                    rope(kT[:, s - 5, 0:256], kT[:, s - 5, 0:256], s - 5, g)
                if s >= 8:
                    dve.wait_ge(q_copied, at(s - 7, 4, g))
                    rope(qT[:, s - 8, :], q_next[:, s - 8, :], s - 4, g)
                if s == 11:
                    used(st, 11, i)
                    values_out()
                low(st, s + 2, i)

            def values_out():
                for t in range(2, 4):
                    nc.vector.tensor_copy(v_sb[:, t, :], ps[:, 2 + t, :]).then_inc(v_dve, 1)

            low(QKV0, 0)
            low(QKV0, 1)
            for s in range(QKV0.n_w):
                for tile in range(2 * s, 2 * s + 2):
                    if tile < HPG:
                        dve.wait_ge(k_copied, tile + 1)
                        rope(kT[:, tile, 0:256], kT[:, tile, 0:256], tile, 0)
                    else:
                        dve.wait_ge(q_copied, tile - HPG + 1)
                        rope(qT[:, tile - HPG, :], q_next[:, tile - HPG, :], tile, 0)
                if s == QKV0.n_w - 1:
                    used(QKV0, s)
                    values_out()
                low(QKV0, s + 2)
            with dve.Fori(0, GROUPS - 1) as i:
                link.turn(i, 8 * 1 + 8 * 3 + 2)
                for s in range(QKV.n_w):
                    if s == 1:
                        param_cols(i + 2, 1, i)
                    attend(ATTEND[s], i)
                    if s == 9:
                        head_squares(i)
                    if s == 11:
                        head_norm(i)
                    qkv_step(QKV, s, i + 1, i)
            link.end(GROUPS - 1)
            param_cols(5, 4)
            last = GROUPS - 1
            maxima(0, last)
            maxima(1, last)

            def o_low(pr):
                dve.wait_ge(pair_hi, pr + 1)
                nc.vector.scalar_tensor_tensor(out=hT[:, 2 * pr:2 * pr + 2, LAT_LO, :],
                                               in0=ps[:, pr % 2, :].rearrange("p (k t) -> p k t", k=2),
                                               scalar=subln[:, 0:1],
                                               in1=hT[:, 2 * pr:2 * pr + 2, LAT_HI, :].bitcast(F32),
                                               op0=ALU.mult, op1=ALU.subtract).then_inc(pair_lo, 1)

            for u in range(8):
                mix(u, last)
                if u + 2 < 8:
                    maxima(u + 2, last)
                if u < EARLY_PAIRS:
                    o_low(u)
            gate(0, 0, 2, 1)
            head_squares(last)

            modulation(0, 3, 4, 2)

            for s in range(WO.n_w):
                if s < WO.n_w - 1:
                    low(WO, s + 2)
                if s == 0:
                    head_norm(last)
                if s == 1:
                    for pr in range(EARLY_PAIRS, 8):
                        o_low(pr)
                if s % 4 == 3 and s < WO.n_w - 1:
                    for t in range(TT):
                        gate_block(0, N_ATT, t, s // 4, ps[:, ROW_BANKS[(s // 4) % 2][t], :])

            def next_input(r, norm, next_norm, prep_n, st, last_block):
                residual(r, norm, next_norm, last_block)
                dve.wait_ge(ab_made, prep_n + 2)
                if st is DOWN0:
                    low(st, st.n_w)
                prep(prep_n, LAT_LO, LAT_HI)
                low(st, st.n_w + 1)

            next_input(0, N_ATT, N_X0, PREP_F0, WO,
                       lambda t: gate_block(0, N_ATT, t, 3, ps[:, ROW_BANKS[1][t], :]))

            def ffn(layer):
                up, loop, down = FFN_STAGES[layer]
                gate(1 + 2 * layer, layer, 5, 3)

                def act_mul(st, s, hidden, per, i=None):
                    used(st, s, i)
                    dve.wait_ge(silu_done[layer], at(hidden + 1, per, i))
                    if hidden >= 2:
                        dve.wait_ge(act_lo_done[layer], at(hidden - 1, per, i))
                    nc.vector.tensor_tensor(act_f[:, hidden % 2, :], ps[:, 1, 0:256], silu_g[:, hidden % 2, :],
                                            ALU.mult).then_inc(act_done[layer], 1)

                def act_low(hidden, per, slot, i=None):
                    dve.wait_ge(act_hi_done[layer], at(hidden + 1, per, i))
                    nc.vector.tensor_tensor(act_lo[:, slot, :], act_f[:, hidden % 2, :],
                                            act_hi[:, slot, :].bitcast(F32), ALU.subtract)\
                        .then_inc(act_lo_done[layer], 1)

                def add(st, s, b, part8, i=None, tiles=range(TT)):
                    for t in tiles:
                        if st is down and s == 3 and t == 0:
                            dve.wait_ge(first_tile, 2 * layer + 2)
                        else:
                            used(st, s, i)
                        done = part8 + 2 * b + t
                        if i is not None or done:
                            if part8 or i is None:
                                dve.wait_ge(y_added[layer], at(done, 16, i))
                        blk = y[:, t, b * 512:(b + 1) * 512]
                        nc.vector.tensor_tensor(blk, blk, ps[:, ROW_BANKS[b % 2][t], :], ALU.add)\
                            .then_inc(y_added[layer], 1)

                for s in range(8):
                    if s % 2:
                        act_mul(up, s, s // 2, 0)
                    low(up, s + 2)
                    if s % 2:
                        act_low(s // 2, 0, s // 2)
                dve.wait_ge(y_zero[layer], 4)
                with dve.Fori(0, 5) as i:
                    for s in range(24):
                        half, k = divmod(s, 12)
                        hidden = 4 + 4 * half + k // 2
                        if k < 8 and k % 2:
                            act_mul(loop, s, hidden, 8, i)
                        if k >= 8:
                            add(loop, s, k - 8, 8 * half, i)
                        low(loop, s + 2, i)
                        if k < 8 and k % 2:
                            act_low(hidden, 8, 4 * (1 - half) + k // 2, i)
                    if layer == 0:
                        param_cols(i + 6, 5, i)
                def gate_y(s, tiles=range(TT)):
                    for t in tiles:
                        gate_block(1 + 2 * layer, (N_FFN0, N_FFN1)[layer], t, s,
                                   y[:, t, s * 512:(s + 1) * 512])

                if layer == 0:
                    modulation(1, 0, 1, 0)
                for s in range(3):
                    add(down, s, s, 8 * (PARTS - 1))
                    if s < 2:
                        low(down, s + 2)
                    if s:
                        gate_y(s - 1)
                gate_y(2)

                def last_block(t):
                    add(down, 3, 3, 8 * (PARTS - 1), tiles=(t,))
                    gate_y(3, (t,))
                return last_block

            last_block = ffn(0)
            next_input(1, N_FFN0, N_X1, PREP_FOUR, DOWN0, last_block)

            def fin_step(st, s, tile, i=None):
                dve.wait_ge(u_hi, at(s + 1 if st is FIN0 else s + 5, 4, i))
                nc.vector.tensor_tensor(hT[:, bass.ds(tile, 1), CTX_LO, :], ps[:, s % 2, 0:256].unsqueeze(1),
                                        hT[:, bass.ds(tile, 1), CTX_HI, :].bitcast(F32), ALU.subtract)\
                    .then_inc(u_lo, 1)
                low(st, s + 2, i)

            for s in range(4):
                fin_step(FIN0, s, s)
            dve.wait_ge(dft_hi, 1)
            nc.vector.tensor_tensor(dft_group[1][:, :, :], dft_sb[:, 0:1024].rearrange("p (k f) -> p k f", k=2),
                                    dft_group[0][:, :, :].bitcast(F32), ALU.subtract).then_inc(dft_lo, 1)
            with dve.Fori(0, 3) as i:
                for s in range(4):
                    fin_step(FIN, s, i * 4 + (4 + s), i)
            gate(2, 1, 2, 1)

            def f_low(f):
                dve.wait_ge(f_hi, f + 1)
                nc.vector.tensor_tensor(hT[:, f, CTX_LO, :], ps[:, 4 + f % 2, 0:256],
                                        hT[:, f, CTX_HI, :].bitcast(F32), ALU.subtract).then_inc(f_lo, 1)

            dve.wait_ge(dft_hi, 2)
            nc.vector.tensor_tensor(dft_token[1], dft_sb[:, 1024:2048].rearrange("p (k f) -> p k f", k=4),
                                    dft_token[0].bitcast(F32), ALU.subtract).then_inc(dft_lo, 1)
            for g in range(FGROUPS):
                for t in range(TT):
                    dve.wait_ge(ab_high, 2 * g + t + 1)
                    nc.vector.tensor_tensor(ab_lo[:, g % 2, t, :, :],
                                            ps[:, 2 * (g % 2) + t, :].rearrange("p (q f) -> p q f", q=2),
                                            ab_hi[:, g % 2, t, :, :].bitcast(F32), ALU.subtract)\
                        .then_inc(ab_low, 1)
                if g:
                    f_low(2 * g - 2)
                    f_low(2 * g - 1)
                fold(FOUT, 1, range(g * FOUT_EARLY // FGROUPS, (g + 1) * FOUT_EARLY // FGROUPS))
            f_low(KT - 2)
            f_low(KT - 1)
            modulation(1, 3, 4, 2)
            for s in range(FOUT.n_w):
                if s == FOUT_SUM + 2:
                    param_cols(11, 10)
                if s < FOUT.n_w - 1:
                    low(FOUT, s + 2)
                if s % 4 == 3 and s < FOUT.n_w - 1:
                    for t in range(TT):
                        gate_block(2, N_FOUR, t, s // 4, ps[:, ROW_BANKS[(s // 4) % 2][t], :])
            next_input(2, N_FOUR, N_X2, PREP_F1, FOUT,
                       lambda t: gate_block(2, N_FOUR, t, 3, ps[:, ROW_BANKS[1][t], :]))
            last_block = ffn(1)
            residual(3, N_FFN1, None, last_block)

        @block.tensor
        def _(pe):
            def chunk_high(st, j, i=None):
                m = st.w0 + j
                pe.wait_ge(hi_ready, at(m + 1, st.n_w, i))
                return m % 2

            def chunk_low(st, j, i=None):
                pe.wait_ge(raw_done, at(st.raw(j) + PRE + 1, st.n_raw, i))

            def column_tile(st, j, bank, i=None, both=False):
                slot = chunk_high(st, j, i)
                n = 512 if both else 256
                for kt in range(KT):
                    for part in (LAT_HI, LAT_LO):
                        last = nc.tensor.matmul(ps[:, bank, 0:n], w_hi[:, slot, kt * P:(kt + 1) * P],
                                                hT[:, kt, part:part + (2 if both else 1), :],
                                                start=(kt == 0 and part == LAT_HI), stop=False)
                last.then_inc(hi_used, 1)
                chunk_low(st, j, i)
                for kt in range(KT):
                    last = nc.tensor.matmul(ps[:, bank, 0:n], w_lo[:, slot, kt * P:(kt + 1) * P],
                                            hT[:, kt, LAT_HI:LAT_HI + (2 if both else 1), :],
                                            start=False, stop=(kt == KT - 1))
                last.then_inc(chunk_used, 1)

            def first_tiles(st, first):
                for kt in range(KT):
                    if kt % 2 == 0:
                        pe.wait_ge(pair_lo, first + kt // 2 + 1)
                    for j in range(2):
                        slot = chunk_high(st, j) if kt == 0 else (st.w0 + j) % 2
                        for part in (LAT_HI, LAT_LO):
                            last = nc.tensor.matmul(ps[:, j, 0:256], w_hi[:, slot, kt * P:(kt + 1) * P],
                                                    hT[:, kt, part, :],
                                                    start=(kt == 0 and part == LAT_HI), stop=False)
                        if kt == KT - 1:
                            last.then_inc(hi_used, 1)
                for j in range(2):
                    chunk_low(st, j)
                    for kt in range(KT):
                        last = nc.tensor.matmul(ps[:, j, 0:256], w_lo[:, (st.w0 + j) % 2, kt * P:(kt + 1) * P],
                                                hT[:, kt, LAT_HI, :], start=False, stop=(kt == KT - 1))
                    last.then_inc(chunk_used, 1)

            def row_chunk(st, j, tiles, first, final, i=None):
                slot = chunk_high(st, j, i)
                for k in range(4):
                    cols = slice(k * 512, (k + 1) * 512)
                    for bank, hi, lo in tiles:
                        for q, a in enumerate((hi, lo)):
                            last = nc.tensor.matmul(ps[:, bank, :], a(k), w_hi[:, slot, cols],
                                                    start=(first and k == 0 and q == 0), stop=False)
                last.then_inc(hi_used, 1)
                chunk_low(st, j, i)
                for bank, hi, lo in tiles:
                    for k in range(4):
                        last = nc.tensor.matmul(ps[:, bank, :], hi(k), w_lo[:, slot, k * 512:(k + 1) * 512],
                                                start=False, stop=(final and k == 3))
                last.then_inc(chunk_used, 1)

            def last_row_chunk(st, tiles, first=False):
                j = st.n_w - 1
                slot = chunk_high(st, j)
                for t, (bank, hi, lo) in enumerate(tiles):
                    for k in range(4):
                        for q, a in enumerate((hi, lo)):
                            last = nc.tensor.matmul(ps[:, bank, :], a(k), w_hi[:, slot, k * 512:(k + 1) * 512],
                                                    start=(first and k == 0 and q == 0), stop=False)
                    if t == 1:
                        last.then_inc(hi_used, 1)
                    else:
                        chunk_low(st, j)
                    for k in range(4):
                        last = nc.tensor.matmul(ps[:, bank, :], hi(k), w_lo[:, slot, k * 512:(k + 1) * 512],
                                                start=False, stop=(k == 3))
                    last.then_inc(chunk_used if t == 1 else first_tile, 1)

            def latent_rows(b, kt0, hi=LAT_HI, lo=LAT_LO):
                return [(ROW_BANKS[b % 2][t],
                         lambda k, t=t: hT[:, kt0 + k, hi, t * P:(t + 1) * P],
                         lambda k, t=t: hT[:, kt0 + k, lo, t * P:(t + 1) * P]) for t in range(TT)]

            def prep(n, src, first_xn):
                for t in range(TT):
                    for pr in range(8):
                        if pr % 4 == 0:
                            pe.wait_ge(xn_made, first_xn + 2 * t + pr // 4)
                        for k in range(2):
                            kt = 2 * pr + k
                            last = nc.tensor.transpose(ps[:, pr, k * 256 + t * P:k * 256 + (t + 1) * P],
                                                       src[:, t, kt * P:(kt + 1) * P], ident)
                        if t == TT - 1:
                            last.then_inc(pair_T, 1)

            def sum_rows(fma_raw, i=None, per_turn=0):
                pe.wait_ge(raw_done, at(fma_raw + PRE + 1, per_turn, i))
                for b in range(4):
                    last = nc.tensor.matmul(ps[32 * b:32 * b + 32, SUM_BANK, :], ones[:, :],
                                            acc[:, b * 512:(b + 1) * 512], start=True, stop=True)
                last.then_inc(acc_free, 1)

            def rows_to_cols(count, i=None):
                pe.wait_ge(row_copied, at(count, 1, i))
                for r in range(4):
                    last = nc.tensor.transpose(ps[:, COL_BANK, r * P:(r + 1) * P],
                                               row_sb[:, r * P:(r + 1) * P], ident)
                last.then_inc(cols_made, 1)

            def gate(n):
                pe.wait_ge(gate_col, n + 1)
                nc.tensor.transpose(ps[0:16, SUM_BANK, 0:P], gate_cols[:, :], ident).then_inc(gate_T, 1)

            pe.wait_ge(in_small, 16 * 8)
            pe.wait_ge(zeros_set, 1)
            for n, (rows, width) in enumerate(((32, 32), (128, 128), (96, 96), (96, 96))):
                nc.tensor.transpose(ps[:, 2 + n, 0:width], small_rows[0:rows, n, :], ident[0:rows, 0:rows])\
                    .then_inc(small_T, 1)
            pe.wait_ge(start_w_made, 1)
            pe.wait_ge(small_cols, 3)
            EARLY = {4: [(0, xn0, 0)], 5: [(0, xn0, 4)], 7: [(1, y, 0), (1, y, 4)]}

            def early_transposes(v, x_, pr0):
                pe.wait_ge(xn_made, 4 * v + 4)
                for pr in range(pr0, pr0 + 4):
                    if 8 * v + pr >= 6:
                        pe.wait_ge(early_back, 8 * v + pr - 5)
                    for t in range(TT):
                        for k in range(2):
                            kt = 2 * pr + k
                            last = nc.tensor.transpose(ps[:, (8 * v + pr) % 6, k * 256 + t * P:k * 256 + (t + 1) * P],
                                                       x_[:, t, kt * P:(kt + 1) * P], ident)
                    last.then_inc(early_T, 1)

            def start_transposes(q, par):
                pe.wait_ge(start_row, 2 * q + par + 1)
                for r in range(4):
                    last = nc.tensor.transpose(ps[:, 6 + par, r * P:(r + 1) * P],
                                               start_rows[:, par, r * P:(r + 1) * P], ident)
                last.then_inc(acc_free if (q, par) == (QUARTERS - 1, 1) else start_T, 1)

            def start_tile(kind, t):
                return ps[:, t // 2, t % 2 * 256:(t % 2 + 1) * 256] if kind == 0 else ps[:, 2 + t, :]

            def start_high_pass(q, kind, tiles):
                m = 2 * q + kind
                pe.wait_ge(hi_ready, m + 1)
                pe.wait_ge(pair_lo, 4 * q + 2 * kind + 2)
                if (q, kind) == (0, 0):
                    pe.wait_ge(early_back, 16)
                for t in tiles:
                    for k in range(4):
                        for part in (LAT_HI, LAT_LO):
                            last = nc.tensor.matmul(start_tile(kind, t),
                                                    w_hi[:, m % 2, k * 512 + t * P:k * 512 + (t + 1) * P],
                                                    hT[:, 4 * q + k, part:part + 1 + kind, :],
                                                    start=(q == 0 and k == 0 and part == LAT_HI and
                                                           (kind == 1 or t % 2 == 0)), stop=False)
                if t == HPG - 1:
                    last.then_inc(hi_used, 1)

            def start_low_pass(q, kind):
                m = 2 * q + kind
                pe.wait_ge(start_split, m + 1)
                for t in range(HPG):
                    for k in range(4):
                        last = nc.tensor.matmul(start_tile(kind, t),
                                                w_lo[:, m % 2, k * 512 + t * P:k * 512 + (t + 1) * P],
                                                hT[:, 4 * q + k, LAT_HI:LAT_HI + 1 + kind, :],
                                                start=False, stop=(q == QUARTERS - 1 and k == 3 and
                                                                   (kind == 1 or t % 2 == 1)))
                last.then_inc(chunk_used, 1)

            for n in range(8 * QUARTERS):
                q, par, r = n // 8, n // 4 % 2, n % 4
                if q and n % 8 == 1:
                    start_high_pass(q - 1, 0, range(4))
                elif q and n % 8 == 2:
                    start_low_pass(q - 1, 0)
                elif q and n % 8 == 3:
                    start_high_pass(q - 1, 1, range(2))
                elif q and n % 8 == 5:
                    start_high_pass(q - 1, 1, range(2, 4))
                if n % 8 == 5:
                    start_transposes(q, 0)
                for batch in EARLY.get(n, []):
                    early_transposes(*batch)
                at_raw = START_ORDER.index(("m", n))
                pe.wait_ge(raw_landed[at_raw % RING], 16 * (at_raw // RING + 1))
                if q and r == 0:
                    pe.wait_ge(start_read, 2 * q + par - 1)
                for k in range(4):
                    last = nc.tensor.matmul(ps[32 * k:32 * k + 32, 6 + par, :], start_w[:, 4 * r + k, :],
                                            raw[:, at_raw % RING, k * 512:(k + 1) * 512],
                                            start=(r == 0), stop=(r == 3))
                last.then_inc(start_used, 1)
                if n % 8 == 7:
                    start_transposes(q, 1)
                    if q:
                        start_low_pass(q - 1, 1)
            start_high_pass(QUARTERS - 1, 0, range(4))
            start_low_pass(QUARTERS - 1, 0)
            start_high_pass(QUARTERS - 1, 1, range(4))
            start_low_pass(QUARTERS - 1, 1)

            def scores(u, i):
                h, t = divmod(u, 2)
                if u == 0:
                    pe.wait_ge(qk_ready, at(8, 8, i))
                    pe.wait_ge(k_copied, at(4, 4, i))
                    pe.wait_ge(v_act, at(2, 2, i))
                    pe.wait_ge(v_dve, at(2, 2, i))
                if u >= 2:
                    pe.wait_ge(exp_done, at(2 * u - 2, 16, i))
                for cmp in range(2):
                    rows = slice(64 * cmp, 64 * cmp + 64)
                    last = nc.tensor.matmul(ps[:, 2 + 2 * (u % 2) + cmp, :], qT[rows, h, t * P:(t + 1) * P],
                                            kT[rows, h, :], start=True, stop=True)
                last.then_inc(scores_done, 1)

            def transpose_mix(u, i):
                pe.wait_ge(mix_done, at(u + 1, 8, i))
                if u == 0:
                    pe.wait_ge(cols_copied, at(1, 1, i))
                else:
                    pe.wait_ge(aT_ready, at(u, 8, i))
                for k in range(4):
                    last = nc.tensor.transpose(ps[:, COL_BANK, k * P:(k + 1) * P],
                                               probs[:, u % 2, 0, k * P:(k + 1) * P], ident)
                last.then_inc(mix_T, 1)

            def values(u, i):
                h = u // 2
                pe.wait_ge(aT_ready, at(u + 1, 8, i))
                if u:
                    pe.wait_ge(o_copied, at(u, 8, i))
                for k in range(4):
                    last = nc.tensor.matmul(ps[:, SUM_BANK, (u % 4) * P:(u % 4 + 1) * P],
                                            aT[:, u % 2, k * P:(k + 1) * P], v_sb[:, k, h * P:(h + 1) * P],
                                            start=(k == 0), stop=(k == 3))
                last.then_inc(pv_done, 1)

            def o_pair(pr, _=None):
                pe.wait_ge(xn_made, 8 + 2 * (GROUPS - 1 if pr < EARLY_PAIRS else GROUPS))
                if pr >= 2:
                    pe.wait_ge(pair_lo, 8 * PREP_O + pr - 1)
                for t in range(TT):
                    for k in range(2):
                        kt = 2 * pr + k
                        last = nc.tensor.transpose(ps[:, pr % 2, k * 256 + t * P:k * 256 + (t + 1) * P],
                                                   y[:, t, kt * P:(kt + 1) * P], ident)
                last.then_inc(pair_T, 1)

            def attend(ops, i):
                for op in ops:
                    {"S": scores, "T": transpose_mix, "V": values, "O": o_pair}[op[0]](int(op[1:]), i)

            def values_chunk(st, s, c, i=None):
                tiles = [(2 + t,
                          lambda k, t=t: hT[:, 4 * c + k, LAT_HI + t // 2, (t % 2) * P:(t % 2 + 1) * P],
                          lambda k, t=t: hT[:, 4 * c + k, LAT_LO + t // 2, (t % 2) * P:(t % 2 + 1) * P])
                         for t in range(4)]
                row_chunk(st, s, tiles, c == 0, c == 3, i)

            def qkv_step(st, s, g, i=None):
                if s < 8:
                    if 2 <= s < 6:
                        pe.wait_ge(q_copied, at(s - 1, 4, g))
                    elif s >= 6:
                        pe.wait_ge(k_copied, at(s - 5, 4, g))
                    column_tile(st, s, s % 2, i, both=s >= 4)
                else:
                    values_chunk(st, s, s - 8, i)
                if s == 11:
                    sum_rows(st.raw0 + st.n_raw - 1, i, st.n_raw)

            pe.wait_ge(k_copied, HPG)
            for s in range(QKV0.n_w):
                values_chunk(QKV0, s, s)
            sum_rows(QKV0.raw0 + QKV0.n_raw - 1)
            with pe.Fori(0, GROUPS - 1) as i:
                for s in range(QKV.n_w):
                    if s == 1:
                        rows_to_cols(1, i)
                    attend(ATTEND[s], i)
                    qkv_step(QKV, s, i + 1, i)
            attend(["O0", "O1"], GROUPS - 1)
            rows_to_cols(GROUPS)
            attend(ATTEND_LAST, GROUPS - 1)

            for s in range(WO.n_w):
                b = s // 4
                if s == 1:
                    pe.wait_ge(o_copied, 8 * GROUPS)
                    gate(0)
                if s == 2:
                    for pr in range(EARLY_PAIRS, 8):
                        o_pair(pr)
                if s < 4:
                    pe.wait_ge(pair_lo, 16 + 2 * s + 2)
                if b >= 2 and s % 4 == 0:
                    pe.wait_ge(gated, 2 * (b - 1))
                if s == WO.n_w - 1:
                    last_row_chunk(WO, latent_rows(b, 12))
                else:
                    row_chunk(WO, s, latent_rows(b, 4 * (s % 4)), s % 4 == 0, s % 4 == 3)

            def next_prep(n, first_xn):
                prep(n, y, first_xn)

            next_prep(PREP_F0, 17)

            def ffn(layer):
                up, loop, down = FFN_STAGES[layer]
                first = 8 * (PREP_F0, PREP_F1)[layer]

                def up_tile(st, s, hidden, per, i=None):
                    if s % 2 == 0:
                        if hidden:
                            pe.wait_ge(silu_done[layer], at(hidden, per, i))
                    elif hidden:
                        pe.wait_ge(act_done[layer], at(hidden, per, i))
                    column_tile(st, s, s % 2, i)

                def down_chunk(st, s, b, part8, slot, i=None):
                    if b == 0:
                        pe.wait_ge(act_lo_done[layer], at(part8 // 2 + 4, 8, i))
                    if part8 or b >= 2:
                        pe.wait_ge(y_added[layer], at(part8 + 2 * b - 2, 16, i))
                    tiles = [(ROW_BANKS[b % 2][t],
                              lambda k, t=t: act_hi[:, slot + k, t * P:(t + 1) * P],
                              lambda k, t=t: act_lo[:, slot + k, t * P:(t + 1) * P]) for t in range(TT)]
                    if st is down and s == 3:
                        last_row_chunk(st, tiles, first=True)
                    else:
                        row_chunk(st, s, tiles, True, True, i)

                first_tiles(up, first)
                gate(1 + 2 * layer)
                for s in range(2, 8):
                    up_tile(up, s, s // 2, 0)
                with pe.Fori(0, 5) as i:
                    for s in range(24):
                        half, k = divmod(s, 12)
                        if k < 8:
                            up_tile(loop, s, 4 + 4 * half + k // 2, 8, i)
                        else:
                            down_chunk(loop, s, k - 8, 8 * half, 4 * half, i)
                        if layer == 0 and s == LOOP0_SUM:
                            sum_rows(LOOP0.raw(LOOP0_SUM) - 1, i, LOOP0.n_raw)
                        if layer == 0 and s == 23:
                            rows_to_cols(5, i)
                for s in range(4):
                    down_chunk(down, s, s, 8 * (PARTS - 1), 0)

            ffn(0)
            next_prep(PREP_FOUR, 21)

            first_tiles(FIN0, 8 * PREP_FOUR)
            for s in range(2, 4):
                pe.wait_ge(u_lo, s - 1)
                column_tile(FIN0, s, s % 2)
            with pe.Fori(0, 3) as i:
                for s in range(4):
                    pe.wait_ge(u_lo, at(s + 3, 4, i))
                    column_tile(FIN, s, s % 2, i)

            def group_dft(g):
                if g == 0:
                    pe.wait_ge(u_lo, KT)
                    pe.wait_ge(dft_lo, 1)
                if g >= 2:
                    pe.wait_ge(ab_low, 2 * g - 2)
                for t in range(TT):
                    for k in range(2):
                        for u_part, table in ((CTX_HI, 0), (CTX_LO, 0), (CTX_HI, 1)):
                            last = nc.tensor.matmul(ps[:, 2 * (g % 2) + t, :],
                                                    hT[:, 2 * g + k, u_part, t * P:(t + 1) * P],
                                                    dft_group[table][:, k, :],
                                                    start=(k == 0 and u_part == CTX_HI and table == 0),
                                                    stop=(k == 1 and table == 1))
                    last.then_inc(ab_done, 1)

            def token_dft(f):
                g, half = divmod(f, 2)
                pe.wait_ge(ab_low, 2 * g + 2)
                if f >= 2:
                    pe.wait_ge(f_lo, f - 1)
                if f == 0:
                    pe.wait_ge(dft_lo, 2)
                for q in range(2):
                    for k in range(2):
                        for n, (part, table) in enumerate(((ab_hi, 0), (ab_lo, 0), (ab_hi, 1))):
                            last = nc.tensor.matmul(ps[:, 4 + f % 2, 0:256],
                                                    part[:, g % 2, k, q, half * P:(half + 1) * P],
                                                    dft_token[table][:, 2 * q + k, :],
                                                    start=(q == 0 and k == 0 and n == 0),
                                                    stop=(q == 1 and k == 1 and n == 2))
                last.then_inc(f_done, 1)

            for g in range(FGROUPS):
                group_dft(g)
                if g:
                    token_dft(2 * g - 2)
                    token_dft(2 * g - 1)
            token_dft(KT - 2)
            token_dft(KT - 1)
            for s in range(FOUT.n_w):
                b = s // 4
                if s < 4:
                    pe.wait_ge(f_lo, 4 * s + 4)
                if s == 1:
                    gate(2)
                if b >= 2 and s % 4 == 0:
                    pe.wait_ge(gated, 16 + 2 * (b - 1))
                if s == FOUT.n_w - 1:
                    last_row_chunk(FOUT, latent_rows(b, 12, CTX_HI, CTX_LO))
                else:
                    row_chunk(FOUT, s, latent_rows(b, 4 * (s % 4), CTX_HI, CTX_LO), s % 4 == 0, s % 4 == 3)
                if s == FOUT_SUM:
                    sum_rows(FOUT.raw(FOUT_SUM) - 1)
                if s == FOUT_SUM + 1:
                    rows_to_cols(10)
            next_prep(PREP_F1, 25)
            ffn(1)


def shape_constants():
    inv = (np.float32(THETA) ** (-np.arange(16, dtype=np.float32) / np.float32(16))).astype(np.float32)
    tok = np.arange(SEQ)
    pos = np.stack([tok // GRID_W, tok % GRID_W]).astype(np.float32)
    row = np.arange(P)
    axis, second, freq = (row % 64) // 32, (row % 32) // 16, row % 16
    ang = (pos[axis] * inv[freq][:, None]).astype(np.float32)
    cos, sin = np.cos(ang), np.sin(ang) * np.where(second == 1, 1.0, -1.0)[:, None]
    consts = np.concatenate([np.eye(P), cos, sin], axis=1).astype(np.float32)
    n = np.arange(256)
    a = 2.0 * np.pi * ((n[:, None] * n[None, :]) % 256) / 256.0
    c, s = np.cos(a) / 16.0, np.sin(a) / 16.0
    tiles = lambda m: m.reshape(2, P, -1).transpose(1, 0, 2).reshape(P, -1)
    dft = np.concatenate([tiles(np.concatenate([c, s], axis=1)), tiles(c), tiles(-s)], axis=1)
    return consts, np.ascontiguousarray(dft.astype(np.float32))


_INS = ["x", "c", "ctx", "c_ctx", "mod_w", "mod_b", "norm_g", "ffn_w_gu", "ffn_w_down", "attn_w_qkv",
        "attn_w_o", "attn_lambda", "attn_subln_g", "four_w_in", "four_w_out"]


def kernel(**inputs):
    import concourse.bacc as _bacc
    from concourse.bass_utils import run_bass_kernel_spmd as _run

    nc = _bacc.Bacc("TRN2", target_bir_lowering=False, num_devices=1)
    arrays, args = {}, []
    named = [(name, np.ascontiguousarray(inputs[name])) for name in _INS]
    consts, dft = shape_constants()
    for name, a in named + [("consts", consts), ("dft", dft)]:
        arrays[f"in_{name}"] = a
        args.append(nc.dram_tensor(f"in_{name}", a.shape, mybir.dt.from_np(a.dtype), kind="ExternalInput").ap())
    out = nc.dram_tensor("out_0", (1, SEQ, D), F32, kind="ExternalOutput").ap()
    trunk(nc, *args, out)
    r = _run(nc, [arrays], core_ids=[0])
    return r.results[0]["out_0"]
```
